# Optimizing a Trainium2 kernel written in Bass

```python
import math
import jax, jax.numpy as jnp
from jax import lax
import numpy as np
import jax
import jax.numpy as jnp

D_MODEL = 2048
BATCH = 1
SEQ = 256
DEPTH = 1

SSM_WIDTH = D_MODEL // 2
SSM_GROUP = 16
SSM_GROUPS = SSM_WIDTH // SSM_GROUP
SSM_STATE = 64
DT_MIN = 0.001
DT_MAX = 0.1
ATTN_HEADS = 8
HEAD_DIM = 128
ATTN_WIDTH = ATTN_HEADS * HEAD_DIM
MOBA_BLOCK = 256
MOBA_TOPK = 3
Q_BLOCK = 128
REL_BUCKETS = 32
REL_MAX_DIST = 128
D_FF = 4 * D_MODEL
N_MOD = 6
EPS = 1e-6
NEG_INF = -1e30
IN_WIDTH = SSM_WIDTH + 3 * ATTN_WIDTH + 2 * D_MODEL


def rms_norm(x, g):
    x32 = x.astype(jnp.float32)
    y = x32 * lax.rsqrt(jnp.mean(x32 * x32, axis=-1, keepdims=True) + EPS)
    return (y * g.astype(jnp.float32)).astype(x.dtype)

def _ssm_combine(lhs, rhs):
    a_re1, a_im1, b_re1, b_im1 = lhs
    a_re2, a_im2, b_re2, b_im2 = rhs
    a_re = a_re2 * a_re1 - a_im2 * a_im1
    a_im = a_re2 * a_im1 + a_im2 * a_re1
    b_re = a_re2 * b_re1 - a_im2 * b_im1 + b_re2
    b_im = a_re2 * b_im1 + a_im2 * b_re1 + b_im2
    return (a_re, a_im, b_re, b_im)

def s5_branch(u, a_re, a_im, log_dt, b_re, b_im, c_re, c_im, d_skip, w_glu, b_glu):
    bsz, seq_len, _ = u.shape
    f32 = jnp.float32
    u32 = u.astype(f32).reshape(bsz, seq_len, SSM_GROUPS, SSM_GROUP)
    a_re = a_re.astype(f32)
    a_im = a_im.astype(f32)
    dt = jnp.exp(log_dt.astype(f32))[:, None]
    mag = jnp.exp(dt * a_re)
    abar_re = mag * jnp.cos(dt * a_im)
    abar_im = mag * jnp.sin(dt * a_im)
    den = a_re * a_re + a_im * a_im
    p_re = abar_re - 1.0
    f_re = (p_re * a_re + abar_im * a_im) / den
    f_im = (abar_im * a_re - p_re * a_im) / den
    b_re = b_re.astype(f32)
    b_im = b_im.astype(f32)
    bbar_re = f_re[..., None] * b_re - f_im[..., None] * b_im
    bbar_im = f_re[..., None] * b_im + f_im[..., None] * b_re
    bu_re = jnp.einsum('blgp,gnp->blgn', u32, bbar_re)
    bu_im = jnp.einsum('blgp,gnp->blgn', u32, bbar_im)
    a_seq_re = jnp.broadcast_to(abar_re, bu_re.shape)
    a_seq_im = jnp.broadcast_to(abar_im, bu_im.shape)
    _, _, s_re, s_im = lax.associative_scan(
        _ssm_combine, (a_seq_re, a_seq_im, bu_re, bu_im), axis=1)
    y = (jnp.einsum('blgn,gpn->blgp', s_re, c_re.astype(f32))
         - jnp.einsum('blgn,gpn->blgp', s_im, c_im.astype(f32)))
    y = y.reshape(bsz, seq_len, SSM_WIDTH) + d_skip.astype(f32) * u32.reshape(bsz, seq_len, SSM_WIDTH)
    y = jax.nn.gelu(y).astype(u.dtype)
    return y * jax.nn.sigmoid(y @ w_glu + b_glu)

def t5_bucket(rel):
    n = jnp.maximum(rel, 0)
    max_exact = REL_BUCKETS // 2
    nf = jnp.maximum(n, 1).astype(jnp.float32)
    large = max_exact + (jnp.log(nf / max_exact) / math.log(REL_MAX_DIST / max_exact)
                         * (REL_BUCKETS - max_exact)).astype(jnp.int32)
    large = jnp.minimum(large, REL_BUCKETS - 1)
    return jnp.where(n < max_exact, n, large)

def moba_attention(q, k, v, rel_bias):
    bsz, seq_len = q.shape[0], q.shape[1]
    n_blk = -(-seq_len // MOBA_BLOCK)
    pad = n_blk * MOBA_BLOCK - seq_len
    n_sel = min(MOBA_TOPK, n_blk - 1)
    q = q.transpose(0, 2, 1, 3)
    k = jnp.pad(k.transpose(0, 2, 1, 3), ((0, 0), (0, 0), (0, pad), (0, 0)))
    v = jnp.pad(v.transpose(0, 2, 1, 3), ((0, 0), (0, 0), (0, pad), (0, 0)))
    kb = k.reshape(bsz, ATTN_HEADS, n_blk, MOBA_BLOCK, HEAD_DIM)
    vb = v.reshape(bsz, ATTN_HEADS, n_blk, MOBA_BLOCK, HEAD_DIM)
    kmean = jnp.mean(kb.astype(jnp.float32), axis=3).astype(k.dtype)
    bias_table = rel_bias.T
    head_ix = jnp.arange(ATTN_HEADS)
    n_qblk = seq_len // Q_BLOCK
    scale = HEAD_DIM ** -0.5
    blk_off = jnp.arange(MOBA_BLOCK)

    def one_block(i):
        b = i // n_qblk
        q0 = (i % n_qblk) * Q_BLOCK
        own = q0 // MOBA_BLOCK
        qc = lax.dynamic_slice_in_dim(lax.dynamic_index_in_dim(q, b, 0, keepdims=False),
                                      q0, Q_BLOCK, axis=1)
        kb_b = lax.dynamic_index_in_dim(kb, b, 0, keepdims=False)
        vb_b = lax.dynamic_index_in_dim(vb, b, 0, keepdims=False)
        q_pos = q0 + jnp.arange(Q_BLOCK)
        k_own = lax.dynamic_index_in_dim(kb_b, own, 1, keepdims=False)
        v_own = lax.dynamic_index_in_dim(vb_b, own, 1, keepdims=False)
        rel_own = q_pos[:, None] - (own * MOBA_BLOCK + blk_off)[None, :]
        s_own = (jnp.einsum('hqd,hsd->hqs', qc, k_own).astype(jnp.float32) * scale
                 + bias_table[:, t5_bucket(rel_own)].astype(jnp.float32))
        s_own = jnp.where(rel_own[None] >= 0, s_own, NEG_INF)
        if n_sel == 0:
            p = jax.nn.softmax(s_own, axis=-1).astype(v.dtype)
            return jnp.einsum('hqs,hsd->hqd', p, v_own)
        gate = jnp.einsum('hqd,hnd->hqn', qc, kmean[b]).astype(jnp.float32)
        gate = jnp.where(jnp.arange(n_blk) < own, gate, NEG_INF)
        _, sel = lax.top_k(gate, n_sel)
        valid = jnp.arange(n_sel) < own
        kg = kb_b[head_ix[:, None, None], sel]
        vg = vb_b[head_ix[:, None, None], sel]
        rel_sel = q_pos[None, :, None, None] - (sel[..., None] * MOBA_BLOCK + blk_off)
        s_sel = (jnp.einsum('hqd,hqksd->hqks', qc, kg).astype(jnp.float32) * scale
                 + bias_table[head_ix[:, None, None, None], t5_bucket(rel_sel)].astype(jnp.float32))
        s_sel = jnp.where(valid[None, None, :, None], s_sel, NEG_INF)
        s = jnp.concatenate([s_sel.reshape(ATTN_HEADS, Q_BLOCK, n_sel * MOBA_BLOCK), s_own], axis=-1)
        p = jax.nn.softmax(s, axis=-1).astype(v.dtype)
        p_sel = p[..., :n_sel * MOBA_BLOCK].reshape(ATTN_HEADS, Q_BLOCK, n_sel, MOBA_BLOCK)
        return (jnp.einsum('hqks,hqksd->hqd', p_sel, vg)
                + jnp.einsum('hqs,hsd->hqd', p[..., n_sel * MOBA_BLOCK:], v_own))

    o = lax.map(one_block, jnp.arange(bsz * n_qblk))
    o = o.reshape(bsz, n_qblk, ATTN_HEADS, Q_BLOCK, HEAD_DIM).transpose(0, 1, 3, 2, 4)
    return o.reshape(bsz, seq_len, ATTN_WIDTH)

def first_inputs(seed: int = 0) -> dict:
    key = jax.random.key(seed)
    ks = jax.random.split(key, 24)
    f32 = jnp.float32
    nrm = lambda k, shape, s: jax.random.normal(k, shape, f32) * s
    n_idx = jnp.arange(SSM_STATE, dtype=f32)
    a_re = -0.5 + nrm(ks[4], (DEPTH, SSM_GROUPS, SSM_STATE), 0.01)
    a_im = math.pi * n_idx + nrm(ks[5], (DEPTH, SSM_GROUPS, SSM_STATE), 0.01)
    log_dt = jax.random.uniform(ks[6], (DEPTH, SSM_GROUPS), f32,
                                math.log(DT_MIN), math.log(DT_MAX))
    return {
        "x": nrm(ks[0], (BATCH, SEQ, D_MODEL), 1.0),
        "c": nrm(ks[1], (BATCH, D_MODEL), 1.0),
        "rel_bias": nrm(ks[2], (REL_BUCKETS, ATTN_HEADS), 0.5),
        "w_ada": nrm(ks[3], (DEPTH, D_MODEL, N_MOD * D_MODEL), 0.5 * D_MODEL ** -0.5),
        "b_ada": nrm(ks[7], (DEPTH, N_MOD * D_MODEL), 0.02),
        "norm_mix_g": 1.0 + nrm(ks[8], (DEPTH, D_MODEL), 0.02),
        "w_in": nrm(ks[9], (DEPTH, D_MODEL, IN_WIDTH), D_MODEL ** -0.5),
        "ssm_a_re": a_re,
        "ssm_a_im": a_im,
        "ssm_log_dt": log_dt,
        "ssm_b_re": nrm(ks[10], (DEPTH, SSM_GROUPS, SSM_STATE, SSM_GROUP), (2 * SSM_GROUP) ** -0.5),
        "ssm_b_im": nrm(ks[11], (DEPTH, SSM_GROUPS, SSM_STATE, SSM_GROUP), (2 * SSM_GROUP) ** -0.5),
        "ssm_c_re": nrm(ks[12], (DEPTH, SSM_GROUPS, SSM_GROUP, SSM_STATE), (2 * SSM_STATE) ** -0.5),
        "ssm_c_im": nrm(ks[13], (DEPTH, SSM_GROUPS, SSM_GROUP, SSM_STATE), (2 * SSM_STATE) ** -0.5),
        "ssm_d": nrm(ks[14], (DEPTH, SSM_WIDTH), 1.0),
        "w_glu": nrm(ks[15], (DEPTH, SSM_WIDTH, SSM_WIDTH), SSM_WIDTH ** -0.5),
        "b_glu": nrm(ks[16], (DEPTH, SSM_WIDTH), 0.02),
        "w_proj_ssm": nrm(ks[17], (DEPTH, SSM_WIDTH, D_MODEL), SSM_WIDTH ** -0.5),
        "w_proj_attn": nrm(ks[18], (DEPTH, ATTN_WIDTH, D_MODEL), ATTN_WIDTH ** -0.5),
        "w_out": nrm(ks[19], (DEPTH, D_MODEL, D_MODEL), D_MODEL ** -0.5),
        "norm_mlp_g": 1.0 + nrm(ks[20], (DEPTH, D_MODEL), 0.02),
        "w_ff1": nrm(ks[21], (DEPTH, D_MODEL, D_FF), D_MODEL ** -0.5),
        "w_ff2": nrm(ks[22], (DEPTH, D_FF, D_MODEL), D_FF ** -0.5),
        "norm_final_g": 1.0 + nrm(ks[23], (D_MODEL,), 0.02),
    }

def first_block(x, c, rel_bias, w_ada, b_ada, norm_mix_g, w_in, ssm_a_re, ssm_a_im, ssm_log_dt,
              ssm_b_re, ssm_b_im, ssm_c_re, ssm_c_im, ssm_d, w_glu, b_glu, w_proj_ssm,
              w_proj_attn, w_out, norm_mlp_g, w_ff1, w_ff2, norm_final_g):
    bsz, seq_len, _ = x.shape
    split_at = [SSM_WIDTH, SSM_WIDTH + ATTN_WIDTH, SSM_WIDTH + 2 * ATTN_WIDTH,
                SSM_WIDTH + 3 * ATTN_WIDTH, SSM_WIDTH + 3 * ATTN_WIDTH + D_MODEL]
    c_act = jax.nn.silu(c)
    for l in range(DEPTH):
        mod = c_act @ w_ada[l] + b_ada[l]
        sh1, sc1, g1, sh2, sc2, g2 = [m[:, None, :] for m in jnp.split(mod, N_MOD, axis=-1)]
        h = rms_norm(x, norm_mix_g[l]) * (1.0 + sc1) + sh1
        proj = h @ w_in[l]
        u, q, k, v, ga, gb = jnp.split(proj, split_at, axis=-1)
        y_ssm = s5_branch(u, ssm_a_re[l], ssm_a_im[l], ssm_log_dt[l], ssm_b_re[l], ssm_b_im[l],
                          ssm_c_re[l], ssm_c_im[l], ssm_d[l], w_glu[l], b_glu[l])
        shp = (bsz, seq_len, ATTN_HEADS, HEAD_DIM)
        y_att = moba_attention(q.reshape(shp), k.reshape(shp), v.reshape(shp), rel_bias)
        merged = (jax.nn.sigmoid(ga) * (y_ssm @ w_proj_ssm[l])
                  + jax.nn.sigmoid(gb) * (y_att @ w_proj_attn[l]))
        x = x + g1 * (merged @ w_out[l])
        h2 = rms_norm(x, norm_mlp_g[l]) * (1.0 + sc2) + sh2
        x = x + g2 * (jnp.square(jax.nn.relu(h2 @ w_ff1[l])) @ w_ff2[l])
    return rms_norm(x, norm_final_g)


NSA_WIDTH = D_MODEL // 2
NSA_HEADS = NSA_WIDTH // HEAD_DIM
NSA_KV_HEADS = max(1, NSA_HEADS // 4)
NSA_GROUP = NSA_HEADS // NSA_KV_HEADS
CMP_LEN = 32
CMP_STRIDE = 16
SLC_LEN = 64
N_SELECT = 16
FORCED_SCORE = 1e4
WINDOW = 512
WIN_BLOCK = 128
SLC_Q_CHUNK = 32
RNN_WIDTH = D_MODEL - NSA_WIDTH
RNN_BLOCKS = RNN_WIDTH // HEAD_DIM
RNN_BLOCK_DIM = RNN_WIDTH // RNN_BLOCKS
CONV_WIDTH = 4
LRU_C = 8.0
PEER_HEADS = 8
PEER_KEYS = 128
PEER_EXPERTS = PEER_KEYS * PEER_KEYS
PEER_TOPK = 16
PEER_DQ = 256
PEER_TOK_CHUNK = 128
ROPE_THETA = 10000.0

Q_COLS = NSA_HEADS * HEAD_DIM
KV_COLS = NSA_KV_HEADS * HEAD_DIM
GATE_COLS = 3 * NSA_HEADS
N_IN = Q_COLS + 6 * KV_COLS + GATE_COLS + 2 * RNN_WIDTH


def rms_norm_2(x, g):
    x32 = x.astype(jnp.float32)
    y = x32 * lax.rsqrt(jnp.mean(x32 * x32, axis=-1, keepdims=True) + EPS)
    return (y * g.astype(jnp.float32)).astype(x.dtype)

def rope(x, pos):
    half = x.shape[-1] // 2
    freqs = ROPE_THETA ** (-jnp.arange(half, dtype=jnp.float32) / half)
    ang = pos.astype(jnp.float32)[:, None] * freqs[None, :]
    cos = jnp.cos(ang)[:, None, :]
    sin = jnp.sin(ang)[:, None, :]
    x32 = x.astype(jnp.float32)
    x1, x2 = x32[..., :half], x32[..., half:]
    return jnp.concatenate([x1 * cos - x2 * sin, x2 * cos + x1 * sin], axis=-1).astype(x.dtype)

def masked_softmax(s, mask):
    s = jnp.where(mask, s.astype(jnp.float32), -jnp.inf)
    m = jnp.max(s, axis=-1, keepdims=True)
    m = jnp.where(jnp.isfinite(m), m, 0.0)
    p = jnp.exp(s - m)
    d = jnp.sum(p, axis=-1, keepdims=True)
    return p / jnp.where(d > 0, d, 1.0)

def compress_blocks(k, pe, w):
    B, S, G, dh = k.shape
    n_cmp = (S - CMP_LEN) // CMP_STRIDE + 1
    idx = (jnp.arange(n_cmp) * CMP_STRIDE)[:, None] + jnp.arange(CMP_LEN)[None, :]
    blk = k[:, idx] + pe[None, None, :, None, :]
    blk = jnp.transpose(blk, (0, 3, 1, 2, 4)).reshape(B, G, n_cmp, CMP_LEN * dh)
    return blk @ w

def nsa_attention(q, kc, vc, ks, vs, kw, vw, gates):
    B, G, S, R, dh = q.shape
    scale = dh ** -0.5
    t = jnp.arange(S)
    n_cmp = kc.shape[2]
    cmp_start = jnp.arange(n_cmp) * CMP_STRIDE
    mask_c = (cmp_start + CMP_LEN - 1)[None, :] <= t[:, None]
    p_c = masked_softmax(jnp.einsum('bgsrd,bgcd->bgsrc', q, kc) * scale, mask_c[None, None, :, None, :])
    o_cmp = jnp.einsum('bgsrc,bgcd->bgsrd', p_c.astype(vc.dtype), vc)
    n_slc = S // SLC_LEN
    slc_start = jnp.arange(n_slc) * SLC_LEN
    overlap = jnp.maximum(
        jnp.minimum(cmp_start[:, None] + CMP_LEN, slc_start[None, :] + SLC_LEN)
        - jnp.maximum(cmp_start[:, None], slc_start[None, :]), 0).astype(jnp.float32) / CMP_LEN
    imp = jnp.einsum('bgsrc,cj->bgsj', p_c, overlap)
    cur = t // SLC_LEN
    jb = jnp.arange(n_slc)
    forced = (jb[None, :] == 0) | (jb[None, :] == cur[:, None]) | (jb[None, :] == cur[:, None] - 1)
    valid = slc_start[None, :] <= t[:, None]
    imp = jnp.where(forced, FORCED_SCORE, jnp.where(valid, imp, -FORCED_SCORE))
    n_sel = min(N_SELECT, n_slc)
    _, sel = lax.top_k(imp, n_sel)
    kb = ks.reshape(B, G, n_slc, SLC_LEN, dh)
    vb = vs.reshape(B, G, n_slc, SLC_LEN, dh)
    nq = S // SLC_Q_CHUNK
    q_chunks = jnp.moveaxis(q.reshape(B, G, nq, SLC_Q_CHUNK, R, dh), 2, 0)
    sel_chunks = jnp.moveaxis(sel.reshape(B, G, nq, SLC_Q_CHUNK, n_sel), 2, 0)
    t_chunks = t.reshape(nq, SLC_Q_CHUNK)
    bi = jnp.arange(B)[:, None, None, None]
    gi = jnp.arange(G)[None, :, None, None]
    n_key = n_sel * SLC_LEN

    def slc_chunk(args):
        q_i, sel_i, t_i = args
        kg = kb[bi, gi, sel_i].reshape(B, G, SLC_Q_CHUNK, n_key, dh)
        vg = vb[bi, gi, sel_i].reshape(B, G, SLC_Q_CHUNK, n_key, dh)
        kpos = (sel_i[..., None] * SLC_LEN + jnp.arange(SLC_LEN)).reshape(B, G, SLC_Q_CHUNK, n_key)
        mask = (kpos <= t_i[None, None, :, None])[:, :, :, None, :]
        p = masked_softmax(jnp.einsum('bgqrd,bgqkd->bgqrk', q_i, kg) * scale, mask)
        return jnp.einsum('bgqrk,bgqkd->bgqrd', p.astype(vg.dtype), vg)

    o_slc = lax.map(slc_chunk, (q_chunks, sel_chunks, t_chunks))
    o_slc = jnp.moveaxis(o_slc, 0, 2).reshape(B, G, S, R, dh)
    nb = S // WIN_BLOCK
    npre = WINDOW // WIN_BLOCK
    pad = ((0, 0), (0, 0), (WINDOW, 0), (0, 0))
    kp = jnp.pad(kw, pad).reshape(B, G, nb + npre, WIN_BLOCK, dh)
    vp = jnp.pad(vw, pad).reshape(B, G, nb + npre, WIN_BLOCK, dh)
    kband = jnp.concatenate([kp[:, :, i:i + nb] for i in range(npre + 1)], axis=3)
    vband = jnp.concatenate([vp[:, :, i:i + nb] for i in range(npre + 1)], axis=3)
    qw = q.reshape(B, G, nb, WIN_BLOCK, R, dh)
    qi = jnp.arange(WIN_BLOCK)
    kj = jnp.arange((npre + 1) * WIN_BLOCK)
    rel = kj[None, :] - WINDOW - qi[:, None]
    kabs = (jnp.arange(nb) * WIN_BLOCK)[:, None] + kj[None, :] - WINDOW
    mask_w = ((rel <= 0) & (rel > -WINDOW))[None, :, :] & (kabs >= 0)[:, None, :]
    p_w = masked_softmax(jnp.einsum('bgnqrd,bgnkd->bgnqrk', qw, kband) * scale,
                         mask_w[None, None, :, :, None, :])
    o_win = jnp.einsum('bgnqrk,bgnkd->bgnqrd', p_w.astype(vband.dtype), vband).reshape(B, G, S, R, dh)
    return gates[..., 0:1] * o_cmp + gates[..., 1:2] * o_slc + gates[..., 2:3] * o_win

def rglru_branch(xr, xg, conv_w, conv_b, wa, ba, wi, bi, lam):
    B, S, W = xr.shape
    xp = jnp.pad(xr, ((0, 0), (CONV_WIDTH - 1, 0), (0, 0)))
    u = conv_b + sum(xp[:, i:i + S] * conv_w[i] for i in range(CONV_WIDTH))
    ub = u.reshape(B, S, RNN_BLOCKS, RNN_BLOCK_DIM)
    r = jax.nn.sigmoid((jnp.einsum('bsnd,nde->bsne', ub, wa).reshape(B, S, W) + ba).astype(jnp.float32))
    ig = jax.nn.sigmoid((jnp.einsum('bsnd,nde->bsne', ub, wi).reshape(B, S, W) + bi).astype(jnp.float32))
    log_a = -LRU_C * r * jax.nn.softplus(-lam.astype(jnp.float32))
    a = jnp.exp(log_a)
    b = jnp.sqrt(-jnp.expm1(2.0 * log_a)) * ig * u.astype(jnp.float32)

    def combine(left, right):
        a1, b1 = left
        a2, b2 = right
        return a1 * a2, a2 * b1 + b2

    _, hs = lax.associative_scan(combine, (a, b), axis=1)
    return (jax.nn.gelu(xg.astype(jnp.float32), approximate=False) * hs).astype(xr.dtype)

def hybrid_mixer(h, w_in, w_out, q_norm_g, k_norm_g, cmp_pe_k, cmp_pe_v, cmp_w_k, cmp_w_v, gate_b,
                 conv_w, conv_b, lru_wa, lru_ba, lru_wi, lru_bi, lru_lam, out_g_attn, out_g_rnn):
    B, S, _ = h.shape
    G, R, dh = NSA_KV_HEADS, NSA_GROUP, HEAD_DIM
    z = h @ w_in
    cuts = [int(v) for v in np.cumsum([Q_COLS] + [KV_COLS] * 6 + [GATE_COLS, RNN_WIDTH])]
    q, kc, vc, ks, vs, kw, vw, gl, xr, xg = jnp.split(z, cuts, axis=-1)
    pos = jnp.arange(S)
    q = rope(rms_norm_2(q.reshape(B, S, NSA_HEADS, dh), q_norm_g), pos)
    kc = rms_norm_2(compress_blocks(rope(kc.reshape(B, S, G, dh), pos), cmp_pe_k, cmp_w_k), k_norm_g[0])
    vc = compress_blocks(vc.reshape(B, S, G, dh), cmp_pe_v, cmp_w_v)
    ks = rope(rms_norm_2(ks.reshape(B, S, G, dh), k_norm_g[1]), pos)
    kw = rope(rms_norm_2(kw.reshape(B, S, G, dh), k_norm_g[2]), pos)
    qg = q.reshape(B, S, G, R, dh).transpose(0, 2, 1, 3, 4)
    gates = jax.nn.sigmoid(gl + gate_b).reshape(B, S, G, R, 3).transpose(0, 2, 1, 3, 4)
    o_attn = nsa_attention(qg, kc, vc,
                           jnp.swapaxes(ks, 1, 2), jnp.swapaxes(vs.reshape(B, S, G, dh), 1, 2),
                           jnp.swapaxes(kw, 1, 2), jnp.swapaxes(vw.reshape(B, S, G, dh), 1, 2), gates)
    o_attn = o_attn.transpose(0, 2, 1, 3, 4).reshape(B, S, NSA_WIDTH)
    o_rnn = rglru_branch(xr, xg, conv_w, conv_b, lru_wa, lru_ba, lru_wi, lru_bi, lru_lam)
    y = jnp.concatenate([rms_norm_2(o_attn, out_g_attn), rms_norm_2(o_rnn, out_g_rnn)], axis=-1)
    return y @ w_out

def peer_ffn(h, wq, keys, down, up):
    B, S, D = h.shape
    T = B * S
    hf = h.reshape(T, D)
    q = (hf @ wq).reshape(T, PEER_HEADS, 2, PEER_DQ // 2)
    s = jnp.einsum('thpd,hpkd->thpk', q, keys).astype(jnp.float32)
    v1, i1 = lax.top_k(s[:, :, 0], PEER_TOPK)
    v2, i2 = lax.top_k(s[:, :, 1], PEER_TOPK)
    cand = (v1[..., :, None] + v2[..., None, :]).reshape(T, PEER_HEADS, PEER_TOPK * PEER_TOPK)
    cidx = (i1[..., :, None] * PEER_KEYS + i2[..., None, :]).reshape(T, PEER_HEADS, PEER_TOPK * PEER_TOPK)
    vals, pick = lax.top_k(cand, PEER_TOPK)
    eidx = jnp.take_along_axis(cidx, pick, axis=-1)
    g = jax.nn.softmax(vals, axis=-1)
    nc = T // PEER_TOK_CHUNK

    def chunk(args):
        x_c, e_c, g_c = args
        act = jax.nn.gelu(jnp.einsum('td,thkd->thk', x_c, down[e_c]).astype(jnp.float32),
                          approximate=False) * g_c
        return jnp.einsum('thk,thkd->td', act.astype(up.dtype), up[e_c])

    out = lax.map(chunk, (hf.reshape(nc, PEER_TOK_CHUNK, D),
                          eidx.reshape(nc, PEER_TOK_CHUNK, PEER_HEADS, PEER_TOPK),
                          g.reshape(nc, PEER_TOK_CHUNK, PEER_HEADS, PEER_TOPK)))
    return out.reshape(B, S, D).astype(h.dtype)

def second_inputs(seed: int = 0) -> dict:
    key = jax.random.key(seed)
    ks = jax.random.split(key, 32)
    f32 = jnp.float32
    L = DEPTH

    def nrm(k, shape, s):
        return jax.random.normal(k, shape, f32) * s

    u = jax.random.uniform(ks[26], (L, RNN_WIDTH), f32, 0.9, 0.999)
    return {
        'x': nrm(ks[0], (BATCH, SEQ, D_MODEL), 1.0),
        'c': nrm(ks[1], (BATCH, D_MODEL), 1.0),
        'ada_w': nrm(ks[2], (L, D_MODEL, 6 * D_MODEL), 0.5 * D_MODEL ** -0.5),
        'ada_b': nrm(ks[3], (L, 6 * D_MODEL), 0.02),
        'norm_mix_g': 1.0 + nrm(ks[4], (L, D_MODEL), 0.02),
        'norm_ffn_g': 1.0 + nrm(ks[5], (L, D_MODEL), 0.02),
        'w_in': nrm(ks[6], (L, D_MODEL, N_IN), D_MODEL ** -0.5),
        'w_out': nrm(ks[7], (L, NSA_WIDTH + RNN_WIDTH, D_MODEL), (NSA_WIDTH + RNN_WIDTH) ** -0.5),
        'q_norm_g': 1.0 + nrm(ks[8], (L, HEAD_DIM), 0.02),
        'k_norm_g': 1.0 + nrm(ks[9], (L, 3, HEAD_DIM), 0.02),
        'cmp_pe_k': nrm(ks[10], (L, CMP_LEN, HEAD_DIM), 0.02),
        'cmp_pe_v': nrm(ks[11], (L, CMP_LEN, HEAD_DIM), 0.02),
        'cmp_w_k': nrm(ks[12], (L, CMP_LEN * HEAD_DIM, HEAD_DIM), (CMP_LEN * HEAD_DIM) ** -0.5),
        'cmp_w_v': nrm(ks[13], (L, CMP_LEN * HEAD_DIM, HEAD_DIM), (CMP_LEN * HEAD_DIM) ** -0.5),
        'gate_b': nrm(ks[14], (L, GATE_COLS), 0.1),
        'conv_w': nrm(ks[15], (L, CONV_WIDTH, RNN_WIDTH), CONV_WIDTH ** -0.5),
        'conv_b': nrm(ks[16], (L, RNN_WIDTH), 0.02),
        'lru_wa': nrm(ks[17], (L, RNN_BLOCKS, RNN_BLOCK_DIM, RNN_BLOCK_DIM), RNN_BLOCK_DIM ** -0.5),
        'lru_ba': nrm(ks[18], (L, RNN_WIDTH), 0.1),
        'lru_wi': nrm(ks[19], (L, RNN_BLOCKS, RNN_BLOCK_DIM, RNN_BLOCK_DIM), RNN_BLOCK_DIM ** -0.5),
        'lru_bi': nrm(ks[20], (L, RNN_WIDTH), 0.1),
        'lru_lam': jnp.log(u) - jnp.log1p(-u),
        'out_g_attn': 1.0 + nrm(ks[21], (L, NSA_WIDTH), 0.02),
        'out_g_rnn': 1.0 + nrm(ks[22], (L, RNN_WIDTH), 0.02),
        'peer_wq': nrm(ks[23], (L, D_MODEL, PEER_HEADS * PEER_DQ), D_MODEL ** -0.5),
        'peer_keys': nrm(ks[24], (L, PEER_HEADS, 2, PEER_KEYS, PEER_DQ // 2), (PEER_DQ // 2) ** -0.5),
        'peer_down': nrm(ks[25], (L, PEER_EXPERTS, D_MODEL), D_MODEL ** -0.5),
        'peer_up': nrm(ks[27], (L, PEER_EXPERTS, D_MODEL), PEER_HEADS ** -0.5),
    }

def second_block(x, c, ada_w, ada_b, norm_mix_g, norm_ffn_g, w_in, w_out, q_norm_g, k_norm_g,
              cmp_pe_k, cmp_pe_v, cmp_w_k, cmp_w_v, gate_b, conv_w, conv_b, lru_wa, lru_ba,
              lru_wi, lru_bi, lru_lam, out_g_attn, out_g_rnn, peer_wq, peer_keys, peer_down, peer_up):
    for l in range(DEPTH):
        mod = jax.nn.silu(c) @ ada_w[l] + ada_b[l]
        sh1, sc1, gt1, sh2, sc2, gt2 = jnp.split(mod, 6, axis=-1)
        h = rms_norm_2(x, norm_mix_g[l]) * (1 + sc1[:, None]) + sh1[:, None]
        x = x + gt1[:, None] * hybrid_mixer(
            h, w_in[l], w_out[l], q_norm_g[l], k_norm_g[l], cmp_pe_k[l], cmp_pe_v[l], cmp_w_k[l],
            cmp_w_v[l], gate_b[l], conv_w[l], conv_b[l], lru_wa[l], lru_ba[l], lru_wi[l], lru_bi[l],
            lru_lam[l], out_g_attn[l], out_g_rnn[l])
        h = rms_norm_2(x, norm_ffn_g[l]) * (1 + sc2[:, None]) + sh2[:, None]
        x = x + gt2[:, None] * peer_ffn(h, peer_wq[l], peer_keys[l], peer_down[l], peer_up[l])
    return x


def setup_inputs(seed=0):
    out = dict(first_inputs(seed))
    for name, value in second_inputs(seed + 1).items():
        if name != "x":
            out[name + "_2"] = value
    return out


def reference(
    x, c, rel_bias, w_ada, b_ada, norm_mix_g, w_in, ssm_a_re, ssm_a_im, ssm_log_dt, ssm_b_re,
    ssm_b_im, ssm_c_re, ssm_c_im, ssm_d, w_glu, b_glu, w_proj_ssm, w_proj_attn, w_out,
    norm_mlp_g, w_ff1, w_ff2, norm_final_g, c_2, ada_w_2, ada_b_2, norm_mix_g_2, norm_ffn_g_2,
    w_in_2, w_out_2, q_norm_g_2, k_norm_g_2, cmp_pe_k_2, cmp_pe_v_2, cmp_w_k_2, cmp_w_v_2,
    gate_b_2, conv_w_2, conv_b_2, lru_wa_2, lru_ba_2, lru_wi_2, lru_bi_2, lru_lam_2,
    out_g_attn_2, out_g_rnn_2, peer_wq_2, peer_keys_2, peer_down_2, peer_up_2,
):
    x = first_block(
        x, c, rel_bias, w_ada, b_ada, norm_mix_g, w_in, ssm_a_re, ssm_a_im, ssm_log_dt,
        ssm_b_re, ssm_b_im, ssm_c_re, ssm_c_im, ssm_d, w_glu, b_glu, w_proj_ssm, w_proj_attn,
        w_out, norm_mlp_g, w_ff1, w_ff2, norm_final_g,
    )
    return second_block(
        x, c_2, ada_w_2, ada_b_2, norm_mix_g_2, norm_ffn_g_2, w_in_2, w_out_2, q_norm_g_2,
        k_norm_g_2, cmp_pe_k_2, cmp_pe_v_2, cmp_w_k_2, cmp_w_v_2, gate_b_2, conv_w_2, conv_b_2,
        lru_wa_2, lru_ba_2, lru_wi_2, lru_bi_2, lru_lam_2, out_g_attn_2, out_g_rnn_2, peer_wq_2,
        peer_keys_2, peer_down_2, peer_up_2,
    )


_drawn_inputs = setup_inputs


def setup_inputs(seed=0):
    import zlib

    import numpy as np

    out = dict(_drawn_inputs(seed))
    spreads = {}
    factors = {'rel_bias': 3.039,
     'norm_mix_g': 8.0,
     'ssm_a_re': 64.0,
     'ssm_a_im': 64.0,
     'ssm_log_dt': 64.0,
     'ssm_b_re': 64.0,
     'ssm_b_im': 64.0,
     'ssm_c_re': 64.0,
     'ssm_c_im': 64.0,
     'b_glu': 8.0,
     'norm_mlp_g': 5.101,
     'norm_mix_g_2': 6.627,
     'norm_ffn_g_2': 28.847,
     'q_norm_g_2': 8.0,
     'k_norm_g_2': 8.0,
     'cmp_pe_k_2': 185.983,
     'cmp_pe_v_2': 90.723,
     'gate_b_2': 6.156,
     'conv_b_2': 5.11,
     'lru_ba_2': 8.0,
     'lru_bi_2': 5.716,
     'out_g_attn_2': 58.659,
     'out_g_rnn_2': 67.644}
    for name, (base, spread) in spreads.items():
        noise = np.random.default_rng([zlib.crc32(name.encode()), seed]).standard_normal(out[name].shape)
        drawn = base * np.exp(spread * noise) if base else spread * noise
        out[name] = jnp.asarray(drawn.astype(out[name].dtype))
    for name, factor in factors.items():
        out[name] = (out[name] * factor).astype(out[name].dtype)
    return out
```

```python
from contextlib import ExitStack

import numpy as np
import concourse.bass as bass
from concourse import mybir

F32 = mybir.dt.float32
F32R = mybir.dt.float32r
I32 = mybir.dt.int32
U32 = mybir.dt.uint32
ALU = mybir.AluOpType
ACT = mybir.ActivationFunctionType
AX = mybir.AxisListType

P = 128
T = 256
D = 2048
DC = D // P
EPS = 1e-6
NEG = -1e30

COL = {}


def _columns():
    at = 0
    for name, n in (
        ("c", DC), ("c_2", DC), ("b_ada", 6 * DC), ("ada_b_2", 6 * DC),
        ("norm_mix_g", DC), ("norm_mlp_g", DC), ("norm_final_g", DC), ("norm_mix_g_2", DC), ("norm_ffn_g_2", DC),
        ("ssm_a_re", 32), ("ssm_a_im", 32), ("ssm_log_dt", 32), ("ssm_d", 8), ("b_glu", 8),
        ("q_norm_g_2", 1), ("k_norm_g_2", 3), ("gate_b_2", 1), ("conv_w_2", 32), ("conv_b_2", 8),
        ("lru_ba_2", 8), ("lru_bi_2", 8), ("lru_lam_2", 8), ("out_g_2", DC),
        ("cmp_pe_k_2", 32), ("cmp_pe_v_2", 32),
    ):
        COL[name] = (at, n)
        at += n
    return at


COLS = _columns()

PW = 1024
RAW, HI, LO = 4, 4, 2
PAN = {}


def _panels():
    at = 0
    for name, n in (
        ("u", 16), ("qkv", 48), ("glu", 8), ("merge", 96), ("out", 32), ("ff", 256),
        ("in2", 74), ("lru", 2), ("cmp", 8), ("out2", 32), ("wq", 32), ("keys", 2),
    ):
        PAN[name] = at
        at += n
    return at


PANELS = _panels()


class Chain:

    def __init__(self, engine, semaphore):
        self.engine, self.semaphore, self.n = engine, semaphore, 0

    def __call__(self, instruction, wait=True):
        instruction.then_inc(self.semaphore, 1)
        self.n += 1
        if wait:
            self.engine.wait_ge(self.semaphore, self.n)

    def wait(self):
        self.engine.wait_ge(self.semaphore, self.n)


GRP = {}


def _groups():
    at = 0
    for name, n in (
        ("u", 8), ("qkv", 24), ("glu", 8), ("merge", 16), ("out", 16), ("ff", 128),
        ("in2", 37), ("out2", 16), ("wq", 16),
    ):
        GRP[name] = at
        at += n


_groups()
ADA_GROUPS, HALVES = 6, 4
SC = float(P) ** -0.5
TWO_PI = (6.28125, 0.0019350051879882812, 3.0199159819e-07)
PAIRS = (0, 2, 4, 6, 10, 12, 8)
N2 = 32
PICKS = 128
LN2 = (0.693359375, -2.12194440e-4)

CON = {}
CON_N = (("ident", P), ("swap", P), ("rope_cos", T), ("rope_sin", T), ("causal", 3 * P), ("cmp_add", 2 * 16),
         ("cmp_mul", 2 * 16), ("bucket", 384), ("iota16", 16))


def _consts():
    at = 0
    for name, n in CON_N:
        CON[name] = (at, n)
        at += n
    return at


CONSTS = _consts()


SEMS = ("""small xload bload land0 land1 land2 land3 aland0 aland1 aland2 aland3 hi lo panel freed init sigc ada adaps
        adacol sq ss mean rs nt nh op chain_v chain_p chain_a par ang sin bf bt btc cs cx vmm wdone prod ymm yadd yg
        ghi glo gmul msig mterm hid ffc line_ps line line_out bias vt vtc sc sm nm ex pn tp ptc pv ov done uop zsq zss zmean zrs zy zsw zrot blkd lsig lsq lgel gsig rnn kcc ksq kss kmean krs kcd vcc vctp vctc
        vtt2 vtc2 gtt gtc csc cmx cex cpn cpt ptct ysq yss ymean yrs yy yhi yop hft hfc scp scc eix g1 g2 gg
        stage used dcp gat0 gat1 gat2 gat3 tout xout store""").replace("\n", " ")


def constants():
    out = np.zeros((P, CONSTS), np.float32)

    def put(name, value):
        at, n = CON[name]
        out[:value.shape[0], at:at + n] = value

    put("ident", np.eye(P, dtype=np.float32))
    half = P // 2
    swap = np.zeros((P, P), np.float32)
    for i in range(half):
        swap[half + i, i] = -1.0
        swap[i, half + i] = 1.0
    put("swap", swap)
    freqs = (np.float32(10000.0) ** (-np.arange(half, dtype=np.float32) / np.float32(half))).astype(np.float32)
    ang = (np.arange(T, dtype=np.float32)[:, None] * freqs[None]).astype(np.float32)
    put("rope_cos", np.concatenate([np.cos(ang), np.cos(ang)], 1).T.astype(np.float32))
    put("rope_sin", np.concatenate([np.sin(ang), np.sin(ang)], 1).T.astype(np.float32))
    p = np.arange(P)
    m = np.arange(3 * P)
    put("causal", np.where(m[None] - P > p[:, None] + 0, NEG, 0.0).astype(np.float32)[:, :3 * P])
    add, mul = np.zeros((P, 2, 16), np.float32), np.zeros((P, 2, 16), np.float32)
    for qc in range(2):
        for n in range(16):
            ok = (n < 15) & (16 * n + 31 <= qc * P + p)
            add[:, qc, n] = np.where(ok, 0.0, NEG)
            mul[:, qc, n] = ok
    put("cmp_add", add.reshape(P, 32))
    put("cmp_mul", mul.reshape(P, 32))
    rel = 255 - np.arange(384)
    n = np.maximum(rel, 0)
    nf = np.maximum(n, 1).astype(np.float32)
    large = 16 + (np.log(nf / np.float32(16)) / np.float32(np.log(8.0)) * np.float32(16)).astype(np.int32)
    bucket = np.where(n < 16, n, np.minimum(large, 31))
    hot = np.zeros((P, 384), np.float32)
    for b in range(32):
        hot[b] = (bucket == b) & (rel >= 0)
    hot[32] = rel < 0
    put("bucket", hot)
    put("iota16", np.broadcast_to(np.arange(16, dtype=np.float32), (P, 16)))
    return out



def build(nc, a):
    ctx = ExitStack()
    with ctx:
        def sb(name, shape, dt=F32):
            return ctx.enter_context(nc.sbuf_tensor(name, shape, dt))

        x_res = sb("x_res", [P, DC, T])
        cols = sb("cols", [P, COLS])
        con = sb("con", [P, CONSTS])
        ones = sb("ones", [P, P])
        mod = sb("mod", [P, 12 * DC])
        gain = sb("gain", [P, DC])
        rstd = sb("rstd", [P, 2, T])
        minus_half = sb("minus_half", [P, T])
        csil = sb("csil", [P, 2, DC])
        sg = sb("sg", [P, 4, T])
        mix = sb("mix", [P, 2, T])
        stat = sb("stat", [P, 5, 32])
        sp4 = sb("sp4", [P, 8])
        gate_t = sb("gate_t", [P, 2, 24])
        kcn = sb("kcn", [P, 32])
        kcn2 = sb("kcn2", [P, 32])
        kcr = sb("kcr", [P, 2, 32])
        vcx = sb("vcx", [P, 32])
        cs = sb("cs", [P, 3, 16])
        dot4 = sb("dot4", [P, 4])
        zero1 = sb("zero1", [P, 1], I32)
        st_a = [sb(f"st_a{i}", [P, 1], I32) for i in range(4)]
        st_b = [sb(f"st_b{i}", [P, 1], I32) for i in range(4)]
        raws = sb("raws", [P, RAW, PW])
        raw = [raws[:, i, :] for i in range(RAW)]
        w_hi = [sb(f"w_hi{i}", [P, 8, P], F32R) for i in range(HI)]
        w_lo = [sb(f"w_lo{i}", [P, 8, P], F32R) for i in range(LO)]
        a_raws = sb("a_raws", [P, HALVES, PW])
        a_raw = [a_raws[:, i, :] for i in range(HALVES)]
        a_acc = sb("a_acc", [P, HALVES, PW])
        opa_hi = sb("opa_hi", [P, DC, T], F32R)
        opa_lo = sb("opa_lo", [P, DC, T], F32R)
        acts = sb("acts", [P, 32, T])
        tmp = acts[:, 16:32, :]
        with ExitStack() as early:
            def es(name, shape, dt=F32):
                return early.enter_context(nc.sbuf_tensor(name, shape, dt))
            ssm_w = es("ssm_w", [P, 2, 4, 2, T])
            ssm_cs = es("ssm_cs", [P, 2, 2, 2, T])
            ssm_r2 = es("ssm_r2", [P, 2, T])
            ssm_t2 = es("ssm_t2", [P, 2, T])
            ssm_par = es("ssm_par", [P, 32, 32])
        idx_t = sb("idx_t", [P, 256], I32)
        opb_hi = sb("opb_hi", [P, DC, T], F32R)
        opb_lo = sb("opb_lo", [P, DC, T], F32R)

        def flat(ap):
            return ap.rearrange("p a t -> p (a t)")

        e_tab = flat(acts[:, 8:16, :]).rearrange("p (f g n) -> p f g n", f=4, g=32)
        b_t = flat(acts[:, 16:24, :]).rearrange("p (r j s) -> p r j s", r=2, j=8)
        c_x = flat(acts[:, 24:32, :]).rearrange("p (r g m) -> p r g m", r=2, g=32)
        ssm_flat = ssm_w[:, :, :, :, :].rearrange("p a b c t -> p (a b c t)")
        b_x = ssm_flat[:, 0:2048].rearrange("p (r g m) -> p r g m", r=2, g=32)
        b_f = ssm_flat[:, 2048:4096].rearrange("p (r g m) -> p r g m", r=2, g=32)
        b_tmp = ssm_cs[:, :, :, :, :].rearrange("p a b c t -> p (a b c t)")[:, 0:2048].rearrange(
            "p (r g m) -> p r g m", r=2, g=32)
        v_tok = flat(acts[:, 0:8, :]).rearrange("p (k h d) -> p k h d", k=2, h=8)
        p_buf = acts[:, 24:26, :]
        pt_buf = acts[:, 26:28, :]
        bias = [sg[:, h, :] if h < 4 else acts[:, 24 + h, :] for h in range(8)]
        acc16 = a_acc[:, :, :].rearrange("p h (c t) -> p (h c) t", t=T)
        raw16 = a_raws[:, :, :].rearrange("p h (c t) -> p (h c) t", t=T)
        u_buf, r_buf = raw16[:, 0:8, :], raw16[:, 8:16, :]
        i_buf, q_buf = acts[:, 20:28, :], acc16[:, 5:13, :]
        blk = [flat(acc16[:, 5 + 4 * i:9 + 4 * i, :])[:, 0:960] for i in range(2)]
        blk_hi = [flat(opb_hi[:, 4 * i:4 * i + 4, :])[:, 0:960] for i in range(2)]
        blk_lo = [flat(opb_lo[:, 4 * i:4 * i + 4, :])[:, 0:960] for i in range(2)]
        v_tok2 = flat(acts[:, 20:24, :]).rearrange("p (k v d) -> p k v d", k=2, v=4)
        pct = flat(acc16[:, 5:13, :]).rearrange("p (u q) -> p u q", u=16)
        pc = acc16[:, 13, :].rearrange("p (u n) -> p u n", u=16)
        vct = acc16[:, 14, :].rearrange("p (g d) -> p g d", g=2)
        hf = [flat(acts[:, 8 * c:8 * c + 8, :]) for c in range(2)]
        score = flat(acts[:, 16:32, :]).rearrange("p (u k) -> p u k", u=32)
        p_acc = [flat(acts[:, 16 + 8 * c:24 + 8 * c, :]) for c in range(2)]
        top_v = flat(raw16[:, 0:2, :]).rearrange("p (u k) -> p u k", u=32)
        top_i = flat(raw16[:, 2:4, :]).rearrange("p (u k) -> p u k", u=32)
        top_u = top_i.bitcast(U32)
        top_f = flat(raw16[:, 4:6, :]).rearrange("p (u k) -> p u k", u=32)
        val = raw16[:, 6, :].rearrange("p (u k) -> p u k", u=16)
        pick = raw16[:, 7, :].rearrange("p (u k) -> p u k", u=16)
        dec = [raw16[:, 8 + i, :].rearrange("p (u k) -> p u k", u=16) for i in range(8)]
        cand = flat(acc16).rearrange("p (u k) -> p u k", u=16)
        gslot = [flat(raws[:, 2 * i:2 * i + 2, :]) for i in range(2)] + [
            flat(a_acc[:, 2 * i:2 * i + 2, :]) for i in range(2)]
        dots_t, gsm_t = raw16[:, 0, :], raw16[:, 15, :]
        line = flat(rstd[0:8, :, :])[:, 0:384]
        rel_b = mix[0:33, 1, 0:8]

        ps = ctx.enter_context(nc.psum_tensor("ps", [P, 8, 512], F32))

        S = {n: ctx.enter_context(nc.semaphore("s_" + n)) for n in SEMS.split()}
        land = [S[f"land{i}"] for i in range(4)]
        aland = [S[f"aland{i}"] for i in range(4)]

        def col(name, j=0, n=1):
            at = COL[name][0] + j
            return cols[:, at:at + n]

        def cst(name):
            at, n = CON[name]
            return con[:, at:at + n]

        ident = cst("ident")
        par = lambda i: ssm_par[:, i, :]
        DT, MAG, CO, SI, FR, FI, PCO, PSI = 0, 1, 2, 3, 4, 5, 6, 14
        X1, X2, X3, X4, X5 = 22, 23, 24, 25, 26
        UNITS = 16
        mean2, rs2 = [mix[:, :, :], sg[:, 0:2, :]], [rstd[:, :, :], sg[:, 2:4, :]]

        def modcol(v, n=DC, j=0):
            return mod[:, v * DC + j:v * DC + j + n]

        block = ctx.enter_context(nc.Block())

        @block.sync
        def _(sp):
            sp.dma_start(cols[:, :], a["cols"]).then_inc(S["small"], 16)
            sp.dma_start(con[:, :], a["consts"]).then_inc(S["small"], 16)

            def load_w(p, slot, first=False):
                if not first:
                    sp.wait_ge(S["lo"], p - 3)
                sp.dma_start(raw[slot], a["w"][bass.ds(p, 1)].rearrange("o p n -> (o p) n")).then_inc(
                    land[slot], 16)

            def load_a(q, slot, first=False):
                if not first:
                    sp.wait_ge(S["ada"], q - 3)
                sp.dma_start(a_raw[slot], a["ada"][bass.ds(q, 1)].rearrange("o p n -> (o p) n")).then_inc(
                    aland[slot], 16)

            for h in range(HALVES):
                load_a(h, h, first=True)
            sp.dma_start(x_res[:, :, :], a["xT"]).then_inc(S["xload"], 16)
            sp.dma_start(b_x, a["b_x"]).then_inc(S["bload"], 16)
            with sp.Fori(1, 16) as k:
                for h in range(HALVES):
                    load_a(k * HALVES + h, h)
            for p in range(4):
                load_w(p, p, first=True)
            sp.wait_ge(S["op"], 4)
            sp.dma_start(c_x, a["c_x"]).then_inc(S["cx"], 16)

            def stream(p0, n, aq=None):
                for j in range(n):
                    load_w(p0 + j, j % 4)
                    if aq is not None and j < 8:
                        load_a(aq + j, j % 4)

            for j in range(8):
                load_w(4 + j, j % 4)
                load_a(64 + j, j % 4)
            stream(12, 8, 72)
            with sp.Fori(0, 6) as i:
                stream(PAN["qkv"] + 4 + i * 8, 8, i * 8 + 80)
            stream(PAN["glu"] + 4, 8)
            sp.wait_ge(S["op"], 4 + 8)
            sp.dma_start(mix[0:32, 1, 0:8], a["relb"]).then_inc(S["bload"], 16)
            sp.wait_ge(S["line"], 1)
            sp.dma_start(a["line"].rearrange("h (p m) -> h p m", p=P),
                         line.unsqueeze(1).broadcast_to([8, P, 3 * P])).then_inc(S["line_out"], 16)
            sp.wait_ge(S["line_out"], 16)
            sp.wait_ge(S["vt"], 4)
            for h in range(8):
                src = bass.AP(a["line"].tensor, h * P * 3 * P + P - 1, [[3 * P - 1, P], [1, T]])
                sp.dma_start(bias[h], src).then_inc(S["bias"], 16)
            with sp.Fori(0, 8) as i:
                stream(PAN["merge"] + 4 + i * 12, 12, i * 8 + 128)
            with sp.Fori(0, 4) as i:
                stream(PAN["out"] + 4 + i * 8, 8)
            with sp.Fori(0, 24) as i:
                stream(PAN["ff"] + 4 + i * 8, 8, i * 8 + 192)
            with sp.Fori(24, 32) as i:
                stream(PAN["ff"] + 4 + i * 8, 8)
            with sp.Fori(0, (PANELS - PAN["in2"] - 4) // 8) as i:
                stream(PAN["in2"] + 4 + i * 8, 8)
            for p in range(PANELS - 2, PANELS):
                load_w(p, p % 4)
            for c in range(2):
                sp.wait_ge(S["xout"], 4 * (c + 1))
                ts = slice(c * P, c * P + P)
                sp.dma_start(a["out"][:, :, ts], x_res[:, :, ts]).then_inc(S["store"], 16)
            sp.wait_ge(S["store"], 32)
            for s in range(4):
                sp.wait_ge(land[s], 16 * ((PANELS - s + 3) // 4))
                sp.wait_ge(aland[s], 16 * 96)

        @block.tensor
        def _(pe):
            def mm(out, lhs, rhs, start, stop):
                return nc.tensor.matmul(out, lhs, rhs, start=start, stop=stop)

            def panel(p, j, out, rhs, c0, first, last):
                hi, lo = w_hi[j % 4], w_lo[j % 2]
                pe.wait_ge(S["lo"], p + 1)
                for b in range(8):
                    mm(out, hi[:, b, :], rhs[0][:, c0 + b, :], first and b == 0, False)
                    mm(out, hi[:, b, :], rhs[1][:, c0 + b, :], False, False)
                    m = mm(out, lo[:, b, :], rhs[0][:, c0 + b, :], False, last and b == 7)
                m.then_inc(S["panel"], 1)

            opa, opb = (opa_hi, opa_lo), (opb_hi, opb_lo)

            def linear(p0, g0, rhs, groups=4, wait=True):
                for j in range(groups):
                    if wait:
                        pe.wait_ge(S["freed"], g0 + j - 3)
                    out = ps[:, j % 4, 0:T]
                    panel(p0 + 2 * j, 2 * j, out, rhs, 0, True, False)
                    panel(p0 + 2 * j + 1, 2 * j + 1, out, rhs, 8, False, True)

            def ada_sums(g):
                pe.wait_ge(S["ada"], 64 * (g + 1))
                if g:
                    pe.wait_ge(S["adacol"], g)
                for h in range(HALVES):
                    for b in range(8):
                        m = mm(ps[:, 7, 8 * h + b:8 * h + b + 1], a_acc[:, h, b * P:(b + 1) * P], ones[:, 0:1],
                               True, True)
                m.then_inc(S["adaps"], 1)

            def norm(n):
                for j in range(4):
                    pe.wait_ge(S["sq"], 4 * n + j + 1)
                    for k in range(4 * j, 4 * j + 4):
                        m = mm(ps[:, 6, 0:T], ones[:, :], tmp[:, k, :], k == 0, k == DC - 1)
                m.then_inc(S["ss"], 1)

            def scores(n, at, qc, q, k):
                if n >= 2:
                    pe.wait_ge(S["sm"], at - 1)
                mm(ps[:, 4 + n % 2, 0:P * (qc + 1)], q, k, True, True).then_inc(S["sc"], 1)

            def turn_rows(n, at, qc):
                pe.wait_ge(S["pn"], at + 1)
                if n >= 2:
                    pe.wait_ge(S["ptc"], at - 1)
                for kc in range(qc + 1):
                    m = nc.tensor.transpose(ps[:, 6 + n % 2, kc * P:(kc + 1) * P],
                                            p_buf[:, n % 2, kc * P:(kc + 1) * P], ident)
                m.then_inc(S["tp"], 1)

            pe.wait_ge(S["small"], 32)
            pe.wait_ge(S["init"], 2)
            norm(0)
            ada_sums(0)
            pe.wait_ge(S["op"], 4)
            linear(0, 0, opa, wait=False)
            linear(8, 4, opa)
            pe.wait_ge(S["bf"], 1)
            for j in range(8):
                if j >= 4:
                    pe.wait_ge(S["btc"], j - 3)
                for r in range(2):
                    src = b_f[:, r, 4 * j:4 * j + 4, :].rearrange("p g m -> p (g m)")
                    m = nc.tensor.transpose(ps[:, 4 + j % 4, r * P:(r + 1) * P], src, ident)
                m.then_inc(S["bt"], 1)
            pe.wait_ge(S["freed"], 8)
            pe.wait_ge(S["btc"], 8)
            pe.wait_ge(S["cx"], 16)

            def drive(s):
                if s >= 2:
                    pe.wait_ge(S["wdone"], s - 1)
                j = s // 2
                for i in (2 * (s % 2), 2 * (s % 2) + 1):
                    rows = slice(32 * i, 32 * i + 32)
                    for r in range(2):
                        m = mm(ps[:, 4 + i, r * T:(r + 1) * T], b_t[rows, r, j, :], acts[rows, j, :], True, True)
                m.then_inc(S["vmm"], 1)

            def read_out(s):
                pe.wait_ge(S["prod"], s + 1)
                j = s // 2
                if s % 2 == 0 and j >= 2:
                    pe.wait_ge(S["yadd"], j - 1)
                w = ssm_w[:, s % 2]
                for g in range(2):
                    i = 2 * (s % 2) + g
                    out = ps[32 * i:32 * i + 32, j % 2, 0:T]
                    tile = 4 * j + i
                    for n, (r, part) in enumerate(((0, 0), (0, 1), (1, 2), (1, 3))):
                        m = mm(out, c_x[:, r, tile, :], w[:, part, g, :], n == 0, n == 3)
                m.then_inc(S["ymm"], 1)

            drive(0)
            for s in range(16):
                if s + 1 < 16:
                    drive(s + 1)
                read_out(s)
            with pe.Fori(0, 6) as i:
                linear(PAN["qkv"] + i * 8, GRP["qkv"] + i * 4, opa)
            ada_sums(1)
            for n in range(8):
                if n == 0:
                    pe.wait_ge(S["glo"], 1)
                pe.wait_ge(S["freed"], GRP["glu"] + n - 3)
                panel(PAN["glu"] + n, n, ps[:, n % 4, 0:T], opb, 8, True, True)
            pe.wait_ge(S["bload"], 32)
            pe.wait_ge(S["init"], 3)
            mm(ps[0:8, 6, 0:384], rel_b, con[0:33, CON["bucket"][0]:CON["bucket"][0] + 384], True, True).then_inc(
                S["line_ps"], 1)
            pe.wait_ge(S["freed"], GRP["merge"])
            for b in range(4):
                for kc in range(2):
                    for hh in range(2):
                        at = (2 * kc + hh) * P
                        m = nc.tensor.transpose(ps[:, b, at:at + P], acts[:, 24 + 2 * b + hh, kc * P:(kc + 1) * P],
                                                ident)
                m.then_inc(S["vt"], 1)
            for n in range(UNITS + 2):
                if n < UNITS:
                    h, qc = n // 2, n % 2
                    scores(n, n, qc, acts[:, 8 + h, qc * P:(qc + 1) * P], acts[:, 16 + h, 0:P * (qc + 1)])
                if n == 0:
                    pe.wait_ge(S["vtc"], 4)
                if 1 <= n <= UNITS:
                    turn_rows(n - 1, n - 1, (n - 1) % 2)
                if n >= 2:
                    u = n - 2
                    pe.wait_ge(S["ptc"], u + 1)
                    if u >= 2:
                        pe.wait_ge(S["ov"], u - 1)
                    for kc in range(u % 2 + 1):
                        m = mm(ps[:, u % 2, 0:P], v_tok[:, kc, u // 2, :], pt_buf[:, u % 2, kc * P:(kc + 1) * P],
                               kc == 0, kc == u % 2)
                    m.then_inc(S["pv"], 1)
            pe.wait_ge(S["ov"], UNITS)
            with pe.Fori(0, 8) as i:
                for par_ in range(2):
                    p0 = PAN["merge"] + i * 12 + 6 * par_
                    b0 = 4 * par_
                    pe.wait_ge(S["freed"], GRP["merge"] + 2 * i + par_ - 1)
                    for g in range(2):
                        panel(p0 + 2 * g, 6 * par_ + 2 * g, ps[:, b0 + g, 0:T], opa, 0, True, False)
                        panel(p0 + 2 * g + 1, 6 * par_ + 2 * g + 1, ps[:, b0 + g, 0:T], opa, 8, False, True)
                    for g in range(2):
                        panel(p0 + 4 + g, 6 * par_ + 4 + g, ps[:, b0 + 2 + g, 0:T], opb, 8 * g, True, True)
            pe.wait_ge(S["freed"], GRP["out"])
            ada_sums(2)
            pe.wait_ge(S["op"], 8 + 8)
            with pe.Fori(0, 4) as i:
                linear(PAN["out"] + i * 8, GRP["out"] + i * 4, opa)
            norm(1)
            pe.wait_ge(S["op"], 8 + 12)
            for q in range(4):
                with pe.Fori(0, 4) as i:
                    linear(PAN["ff"] + 64 * q + i * 8, GRP["ff"] + 32 * q + i * 4, opa)
                pe.wait_ge(S["hid"], 16 * (q + 1))
                with pe.Fori(0, 4) as i:
                    linear(PAN["ff"] + 64 * q + 32 + i * 8, GRP["ff"] + 32 * q + 16 + i * 4, opb)
                if q < 3:
                    ada_sums(3 + q)
            norm(2)
            norm(3)
            pe.wait_ge(S["op"], 24)
            with pe.Fori(0, 9) as i:
                linear(PAN["in2"] + i * 8, GRP["in2"] + i * 4, opa)
            linear(PAN["in2"] + 72, GRP["in2"] + 36, opa, groups=1)
            for i in range(8):
                if i < 6:
                    pe.wait_ge(S["zsq"], i + 1)
                    if i >= 2:
                        pe.wait_ge(S["zmean"], i - 1)
                    sq2 = flat(r_buf[:, 2 * (i % 2):2 * (i % 2) + 2, :])
                    mm(ps[:, 4 + i % 2, :], ones[:, :], sq2, True, True).then_inc(S["zss"], 1)
                if i >= 1:
                    k = i - 1
                    pe.wait_ge(S["zy"], k + 1)
                    if k >= 2:
                        pe.wait_ge(S["zrot"], k - 1)
                    mm(ps[:, 6 + k % 2, :], cst("swap"), flat(acts[:, PAIRS[k]:PAIRS[k] + 2, :]), True,
                       True).then_inc(S["zsw"], 1)
            pe.wait_ge(S["uop"], 1)
            pe.wait_ge(S["freed"], GRP["out2"])
            for r in range(2):
                p = PAN["lru"] + r
                pe.wait_ge(S["lo"], p + 1)
                if r == 1:
                    pe.wait_ge(S["zrot"], 7)
                for b in range(8):
                    out = ps[:, 4 * r + b // 2, (b % 2) * T:(b % 2 + 1) * T]
                    mm(out, w_hi[p % 4][:, b, :], opb_hi[:, 8 + b, :], True, False)
                    mm(out, w_hi[p % 4][:, b, :], opb_lo[:, 8 + b, :], False, False)
                    m = mm(out, w_lo[p % 2][:, b, :], opb_hi[:, 8 + b, :], False, True)
                m.then_inc(S["panel"], 1)
            pe.wait_ge(S["blkd"], 1)
            pe.wait_ge(S["lsig"], 8)
            for x in range(2):
                for j in range(4):
                    p = PAN["cmp"] + 4 * x + j
                    pe.wait_ge(S["lo"], p + 1)
                    for b in range(8):
                        at = 30 * (8 * j + b)
                        hi, lo = blk_hi[x][:, at:at + 30], blk_lo[x][:, at:at + 30]
                        first, last = j + b == 0, j == 3 and b == 7
                        mm(ps[:, x, 0:30], w_hi[p % 4][:, b, :], hi, first, False)
                        mm(ps[:, x, 0:30], w_hi[p % 4][:, b, :], lo, False, False)
                        m = mm(ps[:, x, 0:30], w_lo[p % 2][:, b, :], hi, False, last)
                    m.then_inc(S["panel"], 1)
            pe.wait_ge(S["ksq"], 1)
            mm(ps[:, 2, 0:30], ones[:, :], kcn2[:, 0:30], True, True).then_inc(S["kss"], 1)
            pe.wait_ge(S["vcc"], 1)
            for g in range(2):
                m = nc.tensor.transpose(ps[0:15, 3, g * P:(g + 1) * P], vcx[:, 15 * g:15 * g + 15], ident)
            m.then_inc(S["vctp"], 1)
            pe.wait_ge(S["lsig"], 16)
            for v in range(4):
                for kc in range(2):
                    at = ((v % 2) * 2 + kc) * P
                    m = nc.tensor.transpose(ps[:, 4 + v // 2, at:at + P], acts[:, 16 + v, kc * P:(kc + 1) * P], ident)
                if v % 2:
                    m.then_inc(S["vtt2"], 1)
            pe.wait_ge(S["gsig"], 1)
            for qc in range(2):
                m = nc.tensor.transpose(ps[:, 6, qc * P:(qc + 1) * P], acc16[:, 4, qc * P:(qc + 1) * P], ident)
            m.then_inc(S["gtt"], 1)
            pe.wait_ge(S["kcd"], 1)
            for u in range(16):
                h, qc = u // 2, u % 2
                g = h // 4
                m = mm(ps[:, 7, 16 * u:16 * u + 15], acts[:, h, qc * P:(qc + 1) * P], kcn[:, 15 * g:15 * g + 15],
                       True, True)
            m.then_inc(S["csc"], 1)
            pe.wait_ge(S["cpn"], 1)
            pe.wait_ge(S["vctc"], 1)
            for u in range(16):
                m = nc.tensor.transpose(ps[0:15, u // 4, (u % 4) * P:(u % 4 + 1) * P], pc[:, u, 0:15], ident)
                if u % 4 == 3:
                    m.then_inc(S["cpt"], 1)
            pe.wait_ge(S["ptct"], 4)
            pe.wait_ge(S["vtc2"], 2)
            pe.wait_ge(S["gtc"], 1)
            for n in range(N2 + 2):
                if n < N2:
                    h, qc, kind = n // 4, n // 2 % 2, n % 2
                    scores(n, UNITS + n, qc, acts[:, h, qc * P:(qc + 1) * P],
                           acts[:, 10 + 2 * kind + h // 4, 0:P * (qc + 1)])
                if 1 <= n <= N2:
                    turn_rows(n - 1, UNITS + n - 1, (n - 1) // 2 % 2)
                if n >= 2:
                    k = n - 2
                    h, qc, kind, u = k // 4, k // 2 % 2, k % 2, k // 2
                    pe.wait_ge(S["ptc"], UNITS + k + 1)
                    if kind == 0 and u >= 2:
                        pe.wait_ge(S["ov"], UNITS + u - 1)
                    out = ps[:, u % 2, 0:P]
                    for kc in range(qc + 1):
                        m = mm(out, v_tok2[:, kc, 2 * kind + h // 4, :], pt_buf[:, k % 2, kc * P:(kc + 1) * P],
                               kind == 0 and kc == 0, False)
                    if kind == 1:
                        m = mm(out, vct[0:15, h // 4, :], pct[0:15, u, :], False, True)
                    m.then_inc(S["pv"], 1)
            for x in range(2):
                pe.wait_ge(S["ysq"], x + 1)
                src = i_buf if x == 0 else r_buf
                for k in range(8):
                    m = mm(ps[:, 2, x * T:(x + 1) * T], ones[:, :], src[:, k, :], k == 0, k == 7)
                m.then_inc(S["yss"], 1)
            pe.wait_ge(S["yop"], 2)
            with pe.Fori(0, 4) as i:
                linear(PAN["out2"] + i * 8, GRP["out2"] + i * 4, opb)
            norm(4)
            pe.wait_ge(S["op"], 28)
            with pe.Fori(0, 4) as i:
                linear(PAN["wq"] + i * 8, GRP["wq"] + i * 4, opa)
            pe.wait_ge(S["freed"], GRP["wq"] + 16)
            for c in range(2):
                for b in range(4):
                    for k in range(4):
                        m = nc.tensor.transpose(ps[:, 4 * c + b, k * P:(k + 1) * P],
                                                tmp[:, 4 * b + k, c * P:(c + 1) * P], ident)
                    m.then_inc(S["hft"], 1)
            for x in range(2):
                p = PAN["keys"] + x
                pe.wait_ge(S["lo"], p + 1)
                for c in range(2):
                    for b in range(8):
                        hp = 8 * x + b
                        bank = 4 * c + hp // 4
                        if hp % 4 == 0:
                            pe.wait_ge(S["hfc"], bank + 1)
                        out = ps[:, bank, (hp % 4) * P:(hp % 4 + 1) * P]
                        hi, lo = opb_hi[:, hp, c * P:(c + 1) * P], opb_lo[:, hp, c * P:(c + 1) * P]
                        mm(out, hi, w_hi[p % 4][:, b, :], True, False)
                        mm(out, hi, w_lo[p % 2][:, b, :], False, False)
                        m = mm(out, lo, w_hi[p % 4][:, b, :], False, True)
                m.then_inc(S["panel"], 1)
            pe.wait_ge(S["scc"], 8)
            for c in range(2):
                pe.wait_ge(S["used"], 256 + 128 * (c + 1) + 1)
                for b in range(4):
                    for k in range(4):
                        m = nc.tensor.transpose(ps[:, 4 * c + b, k * P:(k + 1) * P],
                                                p_acc[c][:, (4 * b + k) * P:(4 * b + k + 1) * P], ident)
                    m.then_inc(S["tout"], 1)

        @block.scalar
        def _(act):
            link = Chain(act, S["chain_a"])

            def split(p, n, first=False):
                for q in range(p, p + n):
                    act.wait_ge(land[q % 4], 16 * (q // 4 + 1))
                    if q >= 4:
                        act.wait_ge(S["panel"], q - 3)
                    s = q % 4
                    nc.scalar.activation(w_hi[s][:, :, :].rearrange("p b n -> p (b n)"), raw[s],
                                         ACT.Copy).then_inc(S["hi"], 1)

            def split_loop(base, i, n, per):
                for j in range(n):
                    act.wait_ge(land[j % 4], (base // 4 + j // 4 + 1) * 16 + i * (per * 4))
                    act.wait_ge(S["panel"], base + j - 3 + i * per)
                    nc.scalar.activation(w_hi[j % 4][:, :, :].rearrange("p b n -> p (b n)"), raw[j % 4],
                                         ACT.Copy).then_inc(S["hi"], 1)

            def norm(n, ready, shift):
                act.wait_ge(*ready)
                for j in range(4):
                    s = slice(4 * j, 4 * j + 4)
                    nc.scalar.activation(tmp[:, s, :], x_res[:, s, :], ACT.Square).then_inc(S["sq"], 1)
                for j in range(4):
                    act.wait_ge(S["nt"], 4 * n + j + 1)
                    for k in range(4 * j, 4 * j + 4):
                        out = tmp if shift is not None else x_res
                        link(nc.scalar.activation(out[:, k, :], tmp[:, k, :], ACT.Identity,
                                                  bias=shift[:, k:k + 1] if shift is not None else 0.0,
                                                  scale=gain[:, k:k + 1]), wait=False)
                    link.wait()
                    if shift is not None:
                        s = slice(4 * j, 4 * j + 4)
                        nc.scalar.activation(opa_hi[:, s, :], tmp[:, s, :], ACT.Copy).then_inc(S["nh"], 1)

            def attend(units, base, per):
                for n in range(units + 1):
                    if n < units:
                        nk = P * (n // per % 2 + 1)
                        act.wait_ge(S["nm"], base + n + 1)
                        nc.scalar.activation(p_buf[:, n % 2, 0:nk], p_buf[:, n % 2, 0:nk], ACT.Exp,
                                             bias=stat[:, 1, n:n + 1], scale=SC,
                                             accum_out=stat[:, 2, n:n + 1]).then_inc(S["ex"], 1)
                    if n >= 1:
                        u = n - 1
                        nk = P * (u // per % 2 + 1)
                        act.wait_ge(S["tp"], base + u + 1)
                        if u >= 2:
                            act.wait_ge(S["pv"], base + u - 1)
                        nc.scalar.activation(pt_buf[:, u % 2, 0:nk], ps[:, 6 + u % 2, 0:nk], ACT.Copy).then_inc(
                            S["ptc"], 1)

            act.wait_ge(S["small"], 32)
            for b, name in enumerate(("c", "c_2")):
                nc.scalar.activation(csil[:, b, :], col(name, 0, DC), ACT.Sigmoid).then_inc(S["sigc"], 1)
            act.wait_ge(S["ang"], 1)
            for k in range(2):
                nc.scalar.activation(par(SI if k == 0 else CO), par(X1 if k == 0 else X2), ACT.Sin).then_inc(
                    S["sin"], 1)
            norm(0, (S["xload"], 16), modcol(0))
            for j in range(2):
                split(8 * j, 8)
            for j in range(8):
                act.wait_ge(S["bt"], j + 1)
                nc.scalar.activation(b_t[:, :, j, :], ps[:, 4 + j % 4, 0:2 * P].rearrange("p (r s) -> p r s", r=2),
                                     ACT.Copy).then_inc(S["btc"], 1)
            for j in range(8):
                act.wait_ge(S["yadd"], j + 1)
                nc.scalar.activation(acts[:, j, :], acts[:, j, :], ACT.Gelu_apprx_tanh).then_inc(S["yg"], 1)
            with act.Fori(0, 6) as i:
                split_loop(PAN["qkv"], i, 8, 8)
            act.wait_ge(S["yg"], 8)
            nc.scalar.activation(opb_hi[:, 8:16, :], acts[:, 0:8, :], ACT.Copy).then_inc(S["ghi"], 1)
            split(PAN["glu"], 8)
            for n in range(8):
                act.wait_ge(S["panel"], PAN["glu"] + n + 1)
                if n >= 2:
                    act.wait_ge(S["gmul"], n - 1)
                nc.scalar.activation(sg[:, n % 2, :], ps[:, n % 4, 0:T], ACT.Sigmoid,
                                     bias=col("b_glu", n)).then_inc(S["freed"], 1)
            for b in range(4):
                act.wait_ge(S["vt"], b + 1)
                nc.scalar.activation(v_tok[:, :, 2 * b:2 * b + 2, :],
                                     ps[:, b, :].rearrange("p (k h d) -> p k h d", k=2, h=2),
                                     ACT.Copy).then_inc(S["vtc"], 1)
            attend(UNITS, 0, 1)
            with act.Fori(0, 8) as i:
                base = PAN["merge"]

                def sigmoids(par_):
                    for g in range(2):
                        act.wait_ge(S["panel"], base + 6 * par_ + 2 * g + 2 + i * 12)
                        if g == 0:
                            act.wait_ge(S["freed"], GRP["merge"] + 2 * i + par_ - 1)
                        nc.scalar.activation(sg[:, 2 * par_ + g, :], ps[:, 4 * par_ + g, 0:T],
                                             ACT.Sigmoid).then_inc(S["msig"], 1)

                for j in range(12):
                    act.wait_ge(land[j % 4], (base // 4 + j // 4 + 1) * 16 + i * 48)
                    act.wait_ge(S["panel"], base + j - 3 + i * 12)
                    nc.scalar.activation(w_hi[j % 4][:, :, :].rearrange("p b n -> p (b n)"), raw[j % 4],
                                         ACT.Copy).then_inc(S["hi"], 1)
                    if j == 7:
                        sigmoids(0)
                sigmoids(1)
            for j in range(4):
                s = slice(4 * j, 4 * j + 4)
                act.wait_ge(S["freed"], GRP["out"])
                nc.scalar.activation(opa_hi[:, s, :], tmp[:, s, :], ACT.Copy).then_inc(S["nh"], 1)
            with act.Fori(0, 4) as i:
                split_loop(PAN["out"], i, 8, 8)
            norm(1, (S["freed"], GRP["ff"]), modcol(3))
            with act.Fori(0, 32) as i:
                split_loop(PAN["ff"], i, 8, 8)
            norm(2, (S["freed"], GRP["in2"]), None)
            norm(3, (S["nt"], 12), modcol(6))
            A = nc.scalar.activation
            with act.Fori(0, 9) as i:
                split_loop(PAN["in2"], i, 8, 8)
            split(PAN["in2"] + 72, 4)
            act.wait_ge(S["freed"], GRP["out2"])
            for i in range(6):
                if i >= 2:
                    act.wait_ge(S["zss"], i - 1)
                k = 2 * (i % 2)
                A(r_buf[:, k:k + 2, :], acts[:, PAIRS[i]:PAIRS[i] + 2, :], ACT.Square).then_inc(S["zsq"], 1)
            A(acts[:, 28:32, :], acts[:, 28:32, :], ACT.Gelu).then_inc(S["lgel"], 1)
            A(acc16[:, 0:4, :], acc16[:, 0:4, :], ACT.Gelu).then_inc(S["lgel"], 1)
            A(acc16[:, 4, :], acc16[:, 4, :], ACT.Sigmoid, bias=col("gate_b_2")).then_inc(S["gsig"], 1)
            act.wait_ge(S["zrot"], 7)
            act.wait_ge(S["panel"], PAN["lru"] + 1)
            for k in range(8):
                A(r_buf[:, k, :], ps[:, k // 2, (k % 2) * T:(k % 2 + 1) * T], ACT.Sigmoid,
                  bias=col("lru_ba_2", k)).then_inc(S["lsig"], 1)
            act.wait_ge(S["panel"], PAN["lru"] + 2)
            for k in range(8):
                A(i_buf[:, k, :], ps[:, 4 + k // 2, (k % 2) * T:(k % 2 + 1) * T], ACT.Sigmoid,
                  bias=col("lru_bi_2", k)).then_inc(S["lsig"], 1)
            act.wait_ge(S["lsig"], 8)
            for k in range(8):
                link(A(r_buf[:, k, :], r_buf[:, k, :], ACT.Tanh, scale=sp4[:, k:k + 1]), wait=False)
            link.wait()
            act.wait_ge(S["blkd"], 1)
            A(q_buf, r_buf, ACT.Sqrt).then_inc(S["lsq"], 1)
            split(PAN["cmp"], 8)
            act.wait_ge(S["kcc"], 1)
            A(kcn2[:, 0:30], kcn[:, 0:30], ACT.Square).then_inc(S["ksq"], 1)
            act.wait_ge(S["rnn"], 1)
            for b in range(2):
                act.wait_ge(S["vtt2"], b + 1)
                for v in range(2):
                    ins = A(v_tok2[:, :, 2 * b + v, :], ps[:, 4 + b, 2 * v * P:2 * (v + 1) * P].rearrange(
                        "p (k d) -> p k d", k=2), ACT.Copy)
                ins.then_inc(S["vtc2"], 1)
            act.wait_ge(S["cmx"], 1)
            A(pc[:, :, 0:15], pc[:, :, 0:15], ACT.Exp, scale=SC).then_inc(S["cex"], 1)
            for b in range(4):
                act.wait_ge(S["cpt"], b + 1)
                A(pct[0:15, 4 * b:4 * b + 4, :], ps[0:15, b, :].rearrange("p (u q) -> p u q", u=4),
                  ACT.Copy).then_inc(S["ptct"], 1)
            attend(N2, UNITS, 2)
            act.wait_ge(S["ov"], UNITS + 16)
            A(i_buf, acts[:, 0:8, :], ACT.Square).then_inc(S["ysq"], 1)
            A(r_buf, u_buf, ACT.Square).then_inc(S["ysq"], 1)
            for x in range(2):
                act.wait_ge(S["yy"], x + 1)
                A(opb_hi[:, 8 * x:8 * x + 8, :], acts[:, 0:8, :] if x == 0 else u_buf, ACT.Copy).then_inc(S["yhi"], 1)
            with act.Fori(0, 4) as i:
                split_loop(PAN["out2"], i, 8, 8)
            norm(4, (S["freed"], GRP["wq"]), modcol(9))
            with act.Fori(0, 4) as i:
                split_loop(PAN["wq"], i, 8, 8)
            split(PAN["keys"], 2)
            for b in range(8):
                act.wait_ge(S["hft"], b + 1)
                c = b // 4
                A(hf[c][:, (b % 4) * 512:(b % 4 + 1) * 512], ps[:, b, :], ACT.Copy).then_inc(S["hfc"], 1)
            act.wait_ge(S["panel"], PANELS)
            for b in range(8):
                A(score[:, 4 * b:4 * b + 4, :], ps[:, b, :].rearrange("p (u k) -> p u k", u=4),
                  ACT.Copy).then_inc(S["scc"], 1)
            act.wait_ge(S["g1"], 1)
            A(gsm_t, gsm_t, ACT.Exp).then_inc(S["gg"], 1)
            for c in range(2):
                act.wait_ge(S["dcp"], PICKS * (c + 1))
                A(dots_t[:, c * P:(c + 1) * P], dots_t[:, c * P:(c + 1) * P], ACT.Gelu).then_inc(S["gg"], 1)

        @block.gpsimd
        def _(pool):
            link = Chain(pool, S["chain_p"])

            def rest(p, j, first=False):
                pool.wait_ge(S["hi"], p + 1)
                if not first:
                    pool.wait_ge(S["panel"], p - 1)
                nc.gpsimd.tensor_tensor(w_lo[j % 2][:, :, :].rearrange("p b n -> p (b n)"), raw[j % 4],
                                        w_hi[j % 4][:, :, :].rearrange("p b n -> p (b n)").bitcast(F32),
                                        ALU.subtract).then_inc(S["lo"], 1)

            def rests(p, n):
                for j in range(n):
                    rest(p + j, j)

            def norm(n):
                pool.wait_ge(S["mean"], n + 1)
                nc.gpsimd.tensor_tensor(rstd[:, 1, :], rstd[:, 0, :], minus_half[:, :], ALU.pow).then_inc(S["rs"], 1)

            nc.gpsimd.memset(ones[:, :], 1.0).then_inc(S["init"], 1)
            nc.gpsimd.memset(minus_half[:, :], -0.5).then_inc(S["init"], 1)
            pool.wait_ge(S["par"], 1)
            TT = nc.gpsimd.tensor_tensor
            x = [par(i) for i in (X1, X2, X3, X4, X5)]
            link(nc.gpsimd.tensor_copy(par(PCO), par(CO)), wait=False)
            link(nc.gpsimd.tensor_copy(par(PSI), par(SI)))
            for k in range(7):
                c, s = par(PCO + k), par(PSI + k)
                link(TT(x[0], c, c, ALU.mult), wait=False)
                link(TT(x[1], s, s, ALU.mult), wait=False)
                link(TT(x[2], c, s, ALU.mult))
                link(TT(par(PCO + k + 1), x[0], x[1], ALU.subtract), wait=False)
                link(TT(par(PSI + k + 1), x[2], x[2], ALU.add))
            t2 = ssm_t2[:, :, :].rearrange("p a t -> p (a t)")
            for f in range(2):
                co, si = e_tab[:, 2 * f], e_tab[:, 2 * f + 1]
                link(nc.gpsimd.memset(co[:, :, 0:1], 1.0), wait=False)
                link(nc.gpsimd.memset(si[:, :, 0:1], 0.0))
                for k in range(4):
                    m = 1 << k
                    pc = par(PCO + 4 * f + k).unsqueeze(2).broadcast_to([P, 32, m])
                    ps_ = par(PSI + 4 * f + k).unsqueeze(2).broadcast_to([P, 32, m])
                    c0, s0, c1, s1 = co[:, :, 0:m], si[:, :, 0:m], co[:, :, m:2 * m], si[:, :, m:2 * m]
                    t = t2[:, 0:32 * m].rearrange("p (g m) -> p g m", g=32)
                    tt = t2[:, 256:256 + 32 * m].rearrange("p (g m) -> p g m", g=32)
                    link(TT(t, s0, ps_, ALU.mult), wait=False)
                    link(TT(c1, c0, pc, ALU.mult), wait=False)
                    link(TT(tt, s0, pc, ALU.mult), wait=False)
                    link(TT(s1, c0, ps_, ALU.mult))
                    link(TT(c1, c1, t, ALU.subtract), wait=False)
                    link(TT(s1, s1, tt, ALU.add))
            pool.wait_ge(S["bload"], 16)
            fr = par(FR).unsqueeze(2).broadcast_to([P, 32, 32])
            fi = par(FI).unsqueeze(2).broadcast_to([P, 32, 32])
            link(TT(b_tmp[:, 0], b_x[:, 1], fi, ALU.mult), wait=False)
            link(TT(b_tmp[:, 1], b_x[:, 0], fi, ALU.mult), wait=False)
            link(TT(b_f[:, 0], b_x[:, 0], fr, ALU.mult), wait=False)
            link(TT(b_f[:, 1], b_x[:, 1], fr, ALU.mult))
            link(TT(b_f[:, 0], b_f[:, 0], b_tmp[:, 0], ALU.subtract))
            link(TT(b_f[:, 1], b_f[:, 1], b_tmp[:, 1], ALU.add), wait=False)
            link.wait()
            nc.gpsimd.memset(cs[:, :, :], 0.0).then_inc(S["bf"], 1)
            norm(0)
            for p in range(16):
                rest(p, p, first=p < 2)

            def tables(s):
                if s >= 2:
                    pool.wait_ge(S["prod"], s - 1)
                if s >= 1:
                    pool.wait_ge(S["cs"], 2 * s)
                sh = [P, 2, 16, 16]
                g = slice(2 * s, 2 * s + 2)
                c1 = e_tab[:, 0, g, :].unsqueeze(2).broadcast_to(sh)
                s1 = e_tab[:, 1, g, :].unsqueeze(2).broadcast_to(sh)
                c16 = e_tab[:, 2, g, :].unsqueeze(3).broadcast_to(sh)
                s16 = e_tab[:, 3, g, :].unsqueeze(3).broadcast_to(sh)
                co = ssm_cs[:, s % 2, 0].rearrange("p g (a b) -> p g a b", a=16)
                si = ssm_cs[:, s % 2, 1].rearrange("p g (a b) -> p g a b", a=16)
                t = ssm_t2[:, :, :].rearrange("p g (a b) -> p g a b", a=16)
                link(TT(co, c16, c1, ALU.mult), wait=False)
                link(TT(t, s16, s1, ALU.mult))
                TT(co, co, t, ALU.subtract).then_inc(S["cs"], 1)
                link(TT(si, s16, c1, ALU.mult), wait=False)
                pool.wait_ge(S["cs"], 2 * s + 1)
                link(TT(t, c16, s1, ALU.mult))
                TT(si, si, t, ALU.add).then_inc(S["cs"], 1)

            pool.wait_ge(S["bt"], 8)
            for s in range(16):
                tables(s)
            with pool.Fori(0, 6) as i:
                rests(PAN["qkv"] + i * 8, 8)
            rests(PAN["glu"], 8)
            with pool.Fori(0, 8) as i:
                rests(PAN["merge"] + i * 12, 12)
            with pool.Fori(0, 4) as i:
                rests(PAN["out"] + i * 8, 8)
            norm(1)
            with pool.Fori(0, 32) as i:
                rests(PAN["ff"] + i * 8, 8)
            norm(2)
            norm(3)
            with pool.Fori(0, 9) as i:
                rests(PAN["in2"] + i * 8, 8)
            rests(PAN["in2"] + 72, 4)
            half = minus_half[:, :].unsqueeze(1).broadcast_to([P, 2, T])
            for i in range(6):
                pool.wait_ge(S["zmean"], i + 1)
                if i >= 2:
                    pool.wait_ge(S["zy"], i - 1)
                nc.gpsimd.tensor_tensor(rs2[i % 2], mean2[i % 2], half, ALU.pow).then_inc(S["zrs"], 1)
            rests(PAN["cmp"], 8)
            pool.wait_ge(S["kmean"], 1)
            nc.gpsimd.tensor_tensor(kcr[:, 1, 0:30], kcr[:, 0, 0:30], minus_half[:, 0:30], ALU.pow).then_inc(
                S["krs"], 1)
            pool.wait_ge(S["ymean"], 1)
            nc.gpsimd.tensor_tensor(rs2[0], mean2[0], half, ALU.pow).then_inc(S["yrs"], 1)
            with pool.Fori(0, 4) as i:
                rests(PAN["out2"] + i * 8, 8)
            norm(4)
            with pool.Fori(0, 4) as i:
                rests(PAN["wq"] + i * 8, 8)
            rests(PAN["keys"], 2)
            nc.gpsimd.memset(zero1[:, :], 0).then_inc(S["init"], 1)
            pool.wait_ge(S["init"], 4)
            pool.wait_ge(S["eix"], 1)
            pool.wait_ge(S["lo"], PANELS)
            IT = nc.gpsimd.tensor_tensor

            def gather(j, table):
                pool.indirect_dma_start(gslot[j], None, table, bass.IndirectOffsetOnAxis(
                    ap=st_b[j][:, 0:1], axis=0)).then_inc(S[f"gat{j}"], 16)

            for half_, table in enumerate((a["down"], a["up"])):
                base = 256 * half_

                def stage(j, i, first):
                    n = i * 4 + (base + j)
                    if not (half_ == 0 and first):
                        pool.wait_ge(S[f"gat{j}"], i * 16 + (16 * 64) * half_)
                    IT(st_a[j][:, :], idx_t[:, 4 * i + j:4 * i + j + 1] if first else
                       idx_t[:, bass.ds(i * 4 + j, 1)], zero1[:, :], ALU.add).then_inc(S["stage"], 1)
                    pool.wait_ge(S["stage"], 2 * n + 1 if first else i * 8 + (2 * (base + j) + 1))
                    if not (half_ == 0 and first):
                        pool.wait_ge(S["used"], i * 4 + (base + j - 3))
                    IT(st_b[j][:, :], st_a[j][:, :], zero1[:, :], ALU.add).then_inc(S["stage"], 1)

                for j in range(4):
                    stage(j, 0, True)
                    if j:
                        gather(j - 1, table)
                with pool.Fori(1, 64) as i:
                    for j in range(4):
                        stage(j, i, False)
                        gather((j + 3) % 4, table)
                pool.wait_ge(S["stage"], 2 * (base + 256))
                pool.wait_ge(S["used"], base + 253)
                gather(3, table)

        @block.vector
        def _(dve):
            link = Chain(dve, S["chain_v"])
            V = nc.vector
            TT, TS, STT = V.tensor_tensor, V.tensor_scalar, V.scalar_tensor_tensor

            def ada_step(g, k, first=False):
                blk = g // 3
                for h in range(HALVES):
                    q = 64 * g + k * HALVES + h
                    dve.wait_ge(aland[h], (16 * g + 1) * 16 + k * 16)
                    c = csil[:, blk, k:k + 1] if isinstance(k, int) else csil[:, blk, bass.ds(k, 1)]
                    if first:
                        ins = TS(a_acc[:, h, :], a_raw[h], c, None, ALU.mult)
                    else:
                        dve.wait_ge(S["ada"], q - 3)
                        ins = STT(a_acc[:, h, :], a_raw[h], c, a_acc[:, h, :], ALU.mult, ALU.add)
                    ins.then_inc(S["ada"], 1)

            def ada_cols(g):
                dve.wait_ge(S["adaps"], g + 1)
                b0 = COL["b_ada"][0] if g < 3 else COL["ada_b_2"][0]
                TT(mod[:, 32 * g:32 * g + 32], ps[:, 7, 0:32], cols[:, b0 + 32 * (g % 3):b0 + 32 * (g % 3) + 32],
                   ALU.add).then_inc(S["adacol"], 1)
                if 0 < g < 5:
                    link(V.memset(a_acc[:, :, :], 0.0))

            def norm(n, g_name, scale, final=False):
                dve.wait_ge(S["ss"], n + 1)
                if scale is None:
                    link(V.tensor_copy(gain[:, :], col(g_name, 0, DC)))
                else:
                    link(STT(gain[:, :], scale, 1.0, col(g_name, 0, DC), ALU.add, ALU.mult))
                TS(rstd[:, 0, :], ps[:, 6, 0:T], 1.0 / D, EPS, ALU.mult, ALU.add).then_inc(S["mean"], 1)
                dve.wait_ge(S["rs"], n + 1)
                for j in range(4):
                    s = slice(4 * j, 4 * j + 4)
                    TT(tmp[:, s, :], x_res[:, s, :], rstd[:, 1, :].unsqueeze(1).broadcast_to([P, 4, T]),
                       ALU.mult).then_inc(S["nt"], 1)
                if not final:
                    operand_lo(tmp)

            ops = [0]

            def operand_lo(src):
                for j in range(4):
                    s = slice(4 * j, 4 * j + 4)
                    dve.wait_ge(S["nh"], ops[0] + 1)
                    TT(opa_lo[:, s, :], src[:, s, :], opa_hi[:, s, :].bitcast(F32), ALU.subtract).then_inc(S["op"], 1)
                    ops[0] += 1

            for b, name in enumerate(("c", "c_2")):
                dve.wait_ge(S["sigc"], b + 1)
                link(TT(csil[:, b, :], csil[:, b, :], col(name, 0, DC), ALU.mult))

            def exp(out, x, n=32):
                y, k, r, e = (par(i)[:, 0:n] for i in (X2, X3, X4, X5))
                link(TS(y, x, -87.0, 88.0, ALU.max, ALU.min))
                link(TS(k, y, 1.4426950408889634, 12582912.0, ALU.mult, ALU.add))
                link(TS(k, k, 12582912.0, None, ALU.subtract))
                link(STT(r, k, -LN2[0], y, ALU.mult, ALU.add))
                link(STT(r, k, -LN2[1], r, ALU.mult, ALU.add))
                link(TS(e, r, 1.0 / 5040, None, ALU.mult))
                for d in (720, 120, 24, 6, 2, 1):
                    link(STT(e, e, 1.0 / d, r, ALU.add, ALU.mult))
                link(TS(e, e, 1.0, None, ALU.add))
                link(TS(y.bitcast(I32), k, 127.0, 8388608.0, ALU.add, ALU.mult))
                link(TT(e, e, y, ALU.mult))
                link(STT(out, x, -87.0, e, ALU.is_gt, ALU.mult))

            exp(par(DT), col("ssm_log_dt", 0, 32))
            link(TT(par(X1), par(DT), col("ssm_a_re", 0, 32), ALU.mult))
            exp(par(MAG), par(X1))
            th, k, r = par(X3), par(X4), par(X1)
            link(TT(th, par(DT), col("ssm_a_im", 0, 32), ALU.mult))
            link(TS(k, th, 0.15915494309189535, 12582912.0, ALU.mult, ALU.add))
            link(TS(k, k, 12582912.0, None, ALU.subtract))
            link(STT(r, k, -TWO_PI[0], th, ALU.mult, ALU.add))
            link(STT(r, k, -TWO_PI[1], r, ALU.mult, ALU.add))
            link(STT(r, k, -TWO_PI[2], r, ALU.mult, ALU.add))
            link(TS(r, r, -3.1415925, 3.1415925, ALU.max, ALU.min))
            link(TS(par(X2), r, 1.5707963267948966, None, ALU.add))
            link(TS(k, par(X2), 3.1415926, -6.283185307179586, ALU.is_gt, ALU.mult))
            TT(par(X2), par(X2), k, ALU.add).then_inc(S["ang"], 1)
            dve.wait_ge(S["sin"], 2)
            pr, ai, den, u, v = par(X1), par(X2), par(X3), par(X4), par(X5)
            are, aim = col("ssm_a_re", 0, 32), col("ssm_a_im", 0, 32)
            link(TT(pr, par(MAG), par(CO), ALU.mult))
            link(TS(pr, pr, 1.0, None, ALU.subtract))
            link(TT(ai, par(MAG), par(SI), ALU.mult))
            link(TT(den, are, are, ALU.mult))
            link(TT(u, aim, aim, ALU.mult))
            link(TT(den, den, u, ALU.add))
            link(V.reciprocal(den, den))
            link(TT(u, pr, are, ALU.mult))
            link(TT(v, ai, aim, ALU.mult))
            link(TT(u, u, v, ALU.add))
            link(TT(par(FR), u, den, ALU.mult))
            link(TT(u, ai, are, ALU.mult))
            link(TT(v, pr, aim, ALU.mult))
            link(TT(u, u, v, ALU.subtract))
            link(TT(par(FI), u, den, ALU.mult))

            lam = par(6)[:, 0:8]
            nl, e8, z8, s8, q8 = (par(7 + i)[:, 0:8] for i in range(5))
            link(TS(nl, col("lru_lam_2", 0, 8), -1.0, None, ALU.mult))
            link(TT(nl, nl, col("lru_lam_2", 0, 8), ALU.min))
            exp(e8, nl, 8)
            link(TS(z8, e8, 2.0, None, ALU.add))
            link(V.reciprocal(z8, z8))
            link(TT(z8, z8, e8, ALU.mult))
            link(TT(q8, z8, z8, ALU.mult))
            link(TS(s8, q8, 1.0 / 19, None, ALU.mult))
            for d in (17, 15, 13, 11, 9, 7, 5, 3):
                link(STT(s8, s8, 1.0 / d, q8, ALU.add, ALU.mult))
            link(TS(s8, s8, 1.0, 8.0, ALU.add, ALU.mult))
            link(TT(s8, s8, z8, ALU.mult))
            link(TS(nl, col("lru_lam_2", 0, 8), -1.0, 0.0, ALU.mult, ALU.max))
            link(STT(sp4[:, :], nl, 4.0, s8, ALU.mult, ALU.add))
            V.memset(stat[:, :, :], 0.0).then_inc(S["par"], 1)
            ada_step(0, 0, first=True)
            with dve.Fori(1, 16) as k:
                ada_step(0, k)
            ada_cols(0)
            dve.wait_ge(S["adacol"], 1)
            norm(0, "norm_mix_g", modcol(1))

            def take(p0, dst, n, beside):
                for j in range(4):
                    dve.wait_ge(S["panel"], p0 + 2 * j + 2)
                    TS(dst(n + j), ps[:, j:j + 1, 0:T], 1.0, None, ALU.mult).then_inc(S["freed"], 1)
                    if j % 2:
                        beside(j // 2)

            for t in range(2):
                take(8 * t, lambda n: acts[:, n:n + 1, :], 4 * t,
                     lambda kk: ada_step(1, 2 * t + kk, first=(t == 0 and kk == 0)))

            def y_add(j):
                dve.wait_ge(S["ymm"], 2 * j + 2)
                STT(acts[:, j, :], acts[:, j, :], col("ssm_d", j), ps[:, j % 2, 0:T], ALU.mult, ALU.add).then_inc(
                    S["yadd"], 1)

            for s in range(16):
                co, si = ssm_cs[:, s % 2, 0], ssm_cs[:, s % 2, 1]
                w1, w2, t1, r1 = (ssm_w[:, s % 2, n] for n in range(4))
                i = 2 * (s % 2)
                v_re, v_im = ps[:, 4 + i:6 + i, 0:T], ps[:, 4 + i:6 + i, T:2 * T]
                dve.wait_ge(S["vmm"], s + 1)
                dve.wait_ge(S["cs"], 2 * s + 2)
                if s == 0:
                    dve.wait_ge(S["bt"], 8)
                if s >= 2:
                    dve.wait_ge(S["ymm"], s - 1)
                link(TT(w1, v_re, co, ALU.mult), wait=False)
                link(TT(t1, v_im, si, ALU.mult), wait=False)
                link(TT(w2, v_im, co, ALU.mult))
                link(TT(w1, w1, t1, ALU.add))
                TT(t1, v_re, si, ALU.mult).then_inc(S["wdone"], 1)
                dve.wait_ge(S["wdone"], s + 1)
                link(TT(w2, w2, t1, ALU.subtract))
                for g in range(2):
                    m = par(MAG)[:, 2 * s + g:2 * s + g + 1].broadcast_to([P, T])
                    link(V.tensor_tensor_scan(r1[:, g, :], m, w1[:, g, :], 0.0, ALU.mult, ALU.add), wait=False)
                    link(V.tensor_tensor_scan(ssm_r2[:, g, :], m, w2[:, g, :], 0.0, ALU.mult, ALU.add))
                link(TT(w1, co, r1, ALU.mult), wait=False)
                link(STT(w2, si, -1.0, ssm_r2[:, :, :], ALU.mult, ALU.mult), wait=False)
                link(STT(t1, co, -1.0, ssm_r2[:, :, :], ALU.mult, ALU.mult))
                STT(r1, si, -1.0, r1, ALU.mult, ALU.mult).then_inc(S["prod"], 1)
                if s % 2 == 1 and s >= 3:
                    y_add(s // 2 - 1)
            y_add(7)
            with dve.Fori(0, 6) as i:
                take(PAN["qkv"] + i * 8, lambda n: acts[:, bass.ds(n, 1), :], i * 4 + 8,
                     lambda kk: ada_step(1, 2 * i + (4 + kk)))
            ada_cols(1)
            dve.wait_ge(S["ghi"], 1)
            TT(opb_lo[:, 8:16, :], acts[:, 0:8, :], opb_hi[:, 8:16, :].bitcast(F32), ALU.subtract).then_inc(
                S["glo"], 1)
            for n in range(8):
                dve.wait_ge(S["freed"], GRP["glu"] + n + 1)
                if n >= 1:
                    dve.wait_ge(S["op"], 4 + n)
                y = mix[:, n % 2, :]
                TT(y, acts[:, n, :], sg[:, n % 2, :], ALU.mult).then_inc(S["gmul"], 1)
                dve.wait_ge(S["gmul"], n + 1)
                link(TS(opb_hi[:, n, :], y, 1.0, None, ALU.mult))
                TT(opb_lo[:, n, :], y, opb_hi[:, n, :].bitcast(F32), ALU.subtract).then_inc(S["op"], 1)
            def attend(units, base, per, mask, gate, take_out):
                for n in range(units + 3):
                    if n < units:
                        nk = P * (n // per % 2 + 1)
                        dve.wait_ge(S["sc"], base + n + 1)
                        if n >= 2:
                            dve.wait_ge(S["tp"], base + n - 1)
                        V.tensor_tensor_reduce(p_buf[:, n % 2, 0:nk], ps[:, 4 + n % 2, 0:nk], mask(n)[:, T - nk:T],
                                               1.0, -3e38, ALU.add, ALU.max, stat[:, 0, n:n + 1]).then_inc(
                            S["sm"], 1)
                        dve.wait_ge(S["sm"], base + n + 1)
                        TS(stat[:, 1, n:n + 1], stat[:, 0, n:n + 1], -SC, None, ALU.mult).then_inc(S["nm"], 1)
                    if 1 <= n <= units:
                        u = n - 1
                        nk = P * (u // per % 2 + 1)
                        dve.wait_ge(S["ex"], base + u + 1)
                        link(V.reciprocal(stat[:, 3, u:u + 1], stat[:, 2, u:u + 1]))
                        TS(p_buf[:, u % 2, 0:nk], p_buf[:, u % 2, 0:nk], stat[:, 3, u:u + 1], gate(u),
                           ALU.mult, *([ALU.mult] if gate(u) is not None else [])).then_inc(S["pn"], 1)
                    if n >= 3:
                        take_out(n - 3)

            dve.wait_ge(S["op"], 12)
            V.memset(mix[32:33, 1, 0:8], NEG).then_inc(S["init"], 1)
            dve.wait_ge(S["line_ps"], 1)
            TS(line, ps[0:8, 6, 0:384], 1.0 / SC, None, ALU.mult).then_inc(S["line"], 1)
            dve.wait_ge(S["bias"], 16 * 8)

            def to_operand(u):
                h, qs = u // 2, slice(P * (u % 2), P * (u % 2) + P)
                dve.wait_ge(S["pv"], u + 1)
                link(TS(opb_hi[:, 8 + h, qs], ps[:, u % 2, 0:P], 1.0, None, ALU.mult))
                TT(opb_lo[:, 8 + h, qs], ps[:, u % 2, 0:P], opb_hi[:, 8 + h, qs].bitcast(F32),
                   ALU.subtract).then_inc(S["ov"], 1)

            attend(UNITS, 0, 1, lambda n: bias[n // 2], lambda n: None, to_operand)
            with dve.Fori(0, 8) as i:
                for par_ in range(2):
                    base = PAN["merge"] + 6 * par_
                    for g in range(2):
                        dve.wait_ge(S["panel"], base + 5 + g + i * 12)
                        dve.wait_ge(S["msig"], 4 * i + 2 * par_ + g + 1)
                        TT(mix[:, g, :], sg[:, 2 * par_ + g, :], ps[:, 4 * par_ + 2 + g, 0:T], ALU.mult).then_inc(
                            S["mterm"], 1)
                    dve.wait_ge(S["mterm"], 4 * i + 2 * par_ + 2)
                    n = 16 + 2 * i + par_
                    TT(acts[:, bass.ds(n, 1), :], mix[:, 0:1, :], mix[:, 1:2, :], ALU.add).then_inc(S["freed"], 1)
                    ada_step(2, 2 * i + par_)
            ada_cols(2)
            ops[0] = 4
            operand_lo(tmp)

            def add_gated(p0, n0, gate, beside=None):
                for j in range(4):
                    dve.wait_ge(S["panel"], p0 + 2 * j + 2)
                    xs = x_res[:, bass.ds(n0 + j, 1), :]
                    STT(xs, ps[:, j, 0:T].unsqueeze(1), mod[:, bass.ds(gate * DC + n0 + j, 1)], xs, ALU.mult,
                        ALU.add).then_inc(S["freed"], 1)
                    if j % 2 and beside:
                        beside(j // 2)

            with dve.Fori(0, 4) as i:
                add_gated(PAN["out"] + i * 8, i * 4, 2)
            dve.wait_ge(S["adacol"], 3)
            norm(1, "norm_mlp_g", modcol(4))
            relu, sq = mix[:, 0, :], mix[:, 1, :]
            fc = 0
            for q in range(4):
                with dve.Fori(0, 4) as i:
                    for j in range(4):
                        n = i * 4 + j
                        c = 3 * (16 * q + j) + i * 12
                        dve.wait_ge(S["panel"], PAN["ff"] + 64 * q + 2 * j + 2 + i * 8)
                        TS(relu, ps[:, j, 0:T], 0.0, None, ALU.max).then_inc(S["freed"], 1)
                        dve.wait_ge(S["freed"], GRP["ff"] + 32 * q + j + 1 + i * 4)
                        TT(sq, relu, relu, ALU.mult).then_inc(S["ffc"], 1)
                        dve.wait_ge(S["ffc"], 2 * (16 * q + j) + 1 + i * 8)
                        dst = opb_hi[:, bass.ds(n, 1), :]
                        TS(dst, sq.unsqueeze(1), 1.0, None, ALU.mult).then_inc(S["ffc"], 1)
                        dve.wait_ge(S["ffc"], 2 * (16 * q + j) + 2 + i * 8)
                        TT(opb_lo[:, bass.ds(n, 1), :], sq.unsqueeze(1), dst.bitcast(F32), ALU.subtract).then_inc(
                            S["hid"], 1)
                        if q < 3 and j % 2:
                            ada_step(3 + q, 2 * i + j // 2)
                with dve.Fori(0, 4) as i:
                    add_gated(PAN["ff"] + 64 * q + 32 + i * 8, i * 4, 5,
                              (lambda kk: ada_step(3 + q, 2 * i + (8 + kk))) if q < 3 else None)
                if q < 3:
                    ada_cols(3 + q)
            norm(2, "norm_final_g", None, final=True)
            norm(3, "norm_mix_g_2", modcol(7))

            def take2(p0, dst, n, groups=4):
                for j in range(groups):
                    dve.wait_ge(S["panel"], p0 + 2 * j + 2)
                    TS(dst(n + j), ps[:, j:j + 1, 0:T], 1.0, None, ALU.mult).then_inc(S["freed"], 1)

            with dve.Fori(0, 8) as i:
                take2(PAN["in2"] + i * 8, lambda n: acts[:, bass.ds(n, 1), :], i * 4)
            take2(PAN["in2"] + 64, lambda n: acc16[:, n:n + 1, :], 0)
            take2(PAN["in2"] + 72, lambda n: acc16[:, n:n + 1, :], 4, groups=1)
            dve.wait_ge(S["freed"], GRP["out2"])
            for k in range(8):
                xr = acts[:, 20 + k, :]
                link(TS(u_buf[:, k, :], xr, col("conv_w_2", 24 + k), col("conv_b_2", k), ALU.mult, ALU.add),
                     wait=False)
            for d in range(1, 4):
                link.wait()
                for k in range(8):
                    link(STT(u_buf[:, k, d:T], acts[:, 20 + k, 0:T - d], col("conv_w_2", 8 * (3 - d) + k),
                             u_buf[:, k, d:T], ALU.mult, ALU.add), wait=False)
            link.wait()
            link(TS(opb_hi[:, 8:16, :], u_buf, 1.0, None, ALU.mult))
            TT(opb_lo[:, 8:16, :], u_buf, opb_hi[:, 8:16, :].bitcast(F32), ALU.subtract).then_inc(S["uop"], 1)
            cosb, sinb = (cst(x).unsqueeze(1).broadcast_to([P, 2, T]) for x in ("rope_cos", "rope_sin"))
            for i in range(9):
                if i < 6:
                    dve.wait_ge(S["zss"], i + 1)
                    TS(flat(mean2[i % 2]), ps[:, 4 + i % 2, :], 1.0 / P, EPS, ALU.mult, ALU.add).then_inc(
                        S["zmean"], 1)
                if 1 <= i <= 6:
                    k = i - 1
                    dve.wait_ge(S["zrs"], k + 1)
                    z = acts[:, PAIRS[k]:PAIRS[k] + 2, :]
                    g = col("q_norm_g_2") if k < 4 else col("k_norm_g_2", k - 3)
                    STT(z, z, g, rs2[k % 2], ALU.mult, ALU.mult).then_inc(S["zy"], 1)
                if i == 7:
                    dve.wait_ge(S["zy"], 6)
                    V.memset(cs[:, :, :], 0.0).then_inc(S["zy"], 1)
                if i >= 2:
                    k = i - 2
                    z = acts[:, PAIRS[k]:PAIRS[k] + 2, :]
                    t = r_buf[:, 4 + 2 * (k % 2):6 + 2 * (k % 2), :]
                    dve.wait_ge(S["zsw"], k + 1)
                    link(TT(t, ps[:, 6 + k % 2, :].rearrange("p (a t) -> p a t", a=2), sinb, ALU.mult), wait=False)
                    link(TT(z, z, cosb, ALU.mult))
                    TT(z, z, t, ALU.add).then_inc(S["zrot"], 1)
            dve.wait_ge(S["zrot"], 7)
            for x, (c0, pe_name) in enumerate(((8, "cmp_pe_k_2"), (14, "cmp_pe_v_2"))):
                for g in range(2):
                    at = acts[:, c0 + g, :]
                    src = bass.AP(at.tensor, at.offset, [at.ap[0], [1, 32], [16, 15]])
                    dst = blk[x].rearrange("p (l m) -> p l m", m=30)[:, :, 15 * g:15 * g + 15]
                    link(TT(dst, src, col(pe_name, 0, 32).unsqueeze(2).broadcast_to([P, 32, 15]), ALU.add),
                         wait=False)
            link.wait()
            for x in range(2):
                link(TS(blk_hi[x], blk[x], 1.0, None, ALU.mult))
                ins = TT(blk_lo[x], blk[x], blk_hi[x].bitcast(F32), ALU.subtract)
                if x == 0:
                    link(ins)
                else:
                    ins.then_inc(S["blkd"], 1)
            dve.wait_ge(S["lsq"], 1)
            dve.wait_ge(S["lsig"], 16)
            link(TS(r_buf, r_buf, 1.0, None, ALU.add))
            link(V.reciprocal(r_buf, r_buf), wait=False)
            link(TT(i_buf, i_buf, u_buf, ALU.mult))
            link(TT(q_buf, q_buf, r_buf, ALU.mult))
            link(STT(q_buf, q_buf, 2.0, i_buf, ALU.mult, ALU.mult), wait=False)
            link(TS(r_buf, r_buf, 2.0, -1.0, ALU.mult, ALU.add))
            for k in range(8):
                link(V.tensor_tensor_scan(u_buf[:, k, :], r_buf[:, k, :], q_buf[:, k, :], 0.0, ALU.mult, ALU.add),
                     wait=False)
            link.wait()
            dve.wait_ge(S["lgel"], 2)
            link(TT(u_buf[:, 0:4, :], u_buf[:, 0:4, :], acts[:, 28:32, :], ALU.mult))
            TT(u_buf[:, 4:8, :], u_buf[:, 4:8, :], acc16[:, 0:4, :], ALU.mult).then_inc(S["rnn"], 1)
            dve.wait_ge(S["panel"], PAN["cmp"] + 4)
            TS(kcn[:, 0:30], ps[:, 0, 0:30], 1.0, None, ALU.mult).then_inc(S["kcc"], 1)
            dve.wait_ge(S["panel"], PAN["cmp"] + 8)
            TS(vcx[:, 0:30], ps[:, 1, 0:30], 1.0, None, ALU.mult).then_inc(S["vcc"], 1)
            dve.wait_ge(S["kss"], 1)
            TS(kcr[:, 0, 0:30], ps[:, 2, 0:30], 1.0 / P, EPS, ALU.mult, ALU.add).then_inc(S["kmean"], 1)
            dve.wait_ge(S["krs"], 1)
            STT(kcn[:, 0:30], kcn[:, 0:30], col("k_norm_g_2", 0), kcr[:, 1, 0:30], ALU.mult, ALU.mult).then_inc(
                S["kcd"], 1)
            dve.wait_ge(S["vctp"], 1)
            TS(vct[0:15], ps[0:15, 3, 0:2 * P].rearrange("p (g d) -> p g d", g=2), 1.0, None,
               ALU.mult).then_inc(S["vctc"], 1)
            dve.wait_ge(S["gtt"], 1)
            TS(gate_t[:, :, :], ps[:, 6, 0:2 * P].rearrange("p (c g) -> p c g", c=2)[:, :, 0:24], 1.0, None,
               ALU.mult).then_inc(S["gtc"], 1)
            dve.wait_ge(S["csc"], 1)
            pcx = pc[:, :, 0:15]
            pc4 = pc.rearrange("p (h c) n -> p h c n", c=2)[:, :, :, 0:15]

            def mask4(name):
                m = cst(name).rearrange("p (c n) -> p c n", c=2)[:, :, 0:15]
                return m.unsqueeze(1).broadcast_to([P, 8, 2, 15])

            sc4 = ps[:, 7, 0:256].rearrange("p (h c n) -> p h c n", h=8, c=2)[:, :, :, 0:15]
            link(TT(pc4, sc4, mask4("cmp_add"), ALU.add))
            link(V.tensor_reduce(cs[:, 0, :], pcx, AX.X, ALU.max))
            TT(pcx, pcx, cs[:, 0, :].unsqueeze(2).broadcast_to([P, 16, 15]), ALU.subtract).then_inc(S["cmx"], 1)
            dve.wait_ge(S["cex"], 1)
            link(TT(pc4, pc4, mask4("cmp_mul"), ALU.mult))
            link(V.tensor_reduce(cs[:, 0, :], pcx, AX.X, ALU.add))
            link(TS(cs[:, 1, :], cs[:, 0, :], 0.0, None, ALU.is_equal))
            link(TT(cs[:, 0, :], cs[:, 0, :], cs[:, 1, :], ALU.add))
            link(V.reciprocal(cs[:, 0, :], cs[:, 0, :]))
            dve.wait_ge(S["gtc"], 1)
            g0 = gate_t[:, :, :].rearrange("p c (h k) -> p h c k", k=3)[:, :, :, 0]
            link(TT(cs[:, 2, :].rearrange("p (h c) -> p h c", c=2), cs[:, 0, :].rearrange("p (h c) -> p h c", c=2),
                    g0, ALU.mult))
            TT(pcx, pcx, cs[:, 2, :].unsqueeze(2).broadcast_to([P, 16, 15]), ALU.mult).then_inc(S["cpn"], 1)

            def take_head(n):
                if n % 2:
                    u = n // 2
                    h, qs = u // 2, slice(P * (u % 2), P * (u % 2) + P)
                    dve.wait_ge(S["pv"], UNITS + n + 1)
                    TS(acts[:, h, qs], ps[:, u % 2, 0:P], 1.0, None, ALU.mult).then_inc(S["ov"], 1)

            def unit_gate(n):
                at = 3 * (n // 4) + 1 + n % 2
                return gate_t[:, n // 2 % 2, at:at + 1]

            attend(N2, UNITS, 2, lambda n: cst("causal"), unit_gate, take_head)
            dve.wait_ge(S["yss"], 2)
            TS(flat(mean2[0]), ps[:, 2, :], 1.0 / 1024, EPS, ALU.mult, ALU.add).then_inc(S["ymean"], 1)
            dve.wait_ge(S["yrs"], 1)
            outs = (acts[:, 0:8, :], u_buf)
            for x in range(2):
                for k in range(8):
                    ins = STT(outs[x][:, k, :], outs[x][:, k, :], col("out_g_2", 8 * x + k), rs2[0][:, x, :],
                              ALU.mult, ALU.mult)
                    if k < 7:
                        link(ins, wait=False)
                    else:
                        link.wait()
                        ins.then_inc(S["yy"], 1)
            for x in range(2):
                dve.wait_ge(S["yhi"], x + 1)
                TT(opb_lo[:, 8 * x:8 * x + 8, :], outs[x], opb_hi[:, 8 * x:8 * x + 8, :].bitcast(F32),
                   ALU.subtract).then_inc(S["yop"], 1)
            with dve.Fori(0, 4) as i:
                add_gated(PAN["out2"] + i * 8, i * 4, 8)
            norm(4, "norm_ffn_g_2", modcol(10))
            with dve.Fori(0, 4) as i:
                for j in range(4):
                    n = i * 4 + j
                    dve.wait_ge(S["panel"], PAN["wq"] + 2 * j + 2 + i * 8)
                    dst = opb_hi[:, bass.ds(n, 1), :]
                    TS(dst, ps[:, j:j + 1, 0:T], 1.0, None, ALU.mult).then_inc(S["hid"], 1)
                    dve.wait_ge(S["hid"], 64 + j + 1 + i * 4)
                    TT(opb_lo[:, bass.ds(n, 1), :], ps[:, j:j + 1, 0:T], dst.bitcast(F32), ALU.subtract).then_inc(
                        S["freed"], 1)
            dve.wait_ge(S["scc"], 8)

            def best16(units, src, values, indices):
                for r in range(2):
                    s8_ = slice(8 * r, 8 * r + 8)
                    for u in range(units):
                        link(V.max(values[:, u, s8_], src[:, u, :]), wait=False)
                    link.wait()
                    for u in range(units):
                        link(V.max_index(indices[:, u, s8_], values[:, u, s8_], src[:, u, :]), wait=False)
                    link.wait()
                    if r == 0:
                        for u in range(units):
                            link(V.match_replace(src[:, u, :], values[:, u, s8_], src[:, u, :], -3e38), wait=False)
                        link.wait()

            best16(32, score, top_v, top_u)
            link(V.tensor_copy(top_f, top_u), wait=False)
            tv = top_v.rearrange("p (u h) k -> p u h k", h=2)
            sh = [P, 16, 16, 16]
            c4 = cand.rearrange("p u (a b) -> p u a b", a=16)
            link(TT(c4, tv[:, :, 0, :].unsqueeze(3).broadcast_to(sh), tv[:, :, 1, :].unsqueeze(2).broadcast_to(sh),
                    ALU.add))
            best16(16, cand, val, pick.bitcast(U32))
            g3 = gsm_t.rearrange("p (u k) -> p u k", u=16)
            TT(g3, val, val[:, :, 0:1].broadcast_to([P, 16, 16]), ALU.subtract).then_inc(S["g1"], 1)
            key = []
            for x, (op, arg) in enumerate(((ALU.logical_shift_right, 4), (ALU.bitwise_and, 15))):
                link(TS(dec[x].bitcast(I32), pick.bitcast(I32), arg, None, op))
                link(V.tensor_copy(dec[2 + x], dec[x].bitcast(I32)))
                hot = flat(acts[:, 16:32, :]).rearrange("p (u k a) -> p u k a", u=16, k=16)
                iota = cst("iota16").unsqueeze(1).unsqueeze(1).broadcast_to(sh)
                link(TT(hot, dec[2 + x].unsqueeze(3).broadcast_to(sh), iota, ALU.is_equal))
                tf = top_f.rearrange("p (u h) k -> p u h k", h=2)[:, :, x, :]
                link(TT(hot, hot, tf.unsqueeze(2).broadcast_to(sh), ALU.mult))
                link(V.tensor_reduce(dec[4 + x], hot, AX.X, ALU.add))
            link(STT(dec[6], dec[4], 128.0, dec[5], ALU.mult, ALU.add))
            V.tensor_copy(idx_t[:, :], dec[6].rearrange("p u k -> p (u k)")).then_inc(S["eix"], 1)
            dve.wait_ge(S["gg"], 1)
            link(V.tensor_reduce(cs[:, 0, :], g3, AX.X, ALU.add))
            link(V.reciprocal(cs[:, 0, :], cs[:, 0, :]))
            link(TT(g3, g3, cs[:, 0, :].unsqueeze(2).broadcast_to([P, 16, 16]), ALU.mult))
            V.memset(dot4[:, :], 0.0).then_inc(S["used"], 1)
            dve.wait_ge(S["used"], 1)
            for c in range(2):
                with dve.Fori(0, 32) as i:
                    for j in range(4):
                        dve.wait_ge(S[f"gat{j}"], i * 16 + 16 * (32 * c + 1))
                        V.tensor_tensor_reduce(gslot[j], gslot[j], hf[c], 1.0, 0.0, ALU.mult, ALU.add,
                                               dot4[:, j:j + 1]).then_inc(S["used"], 1)
                        dve.wait_ge(S["used"], i * 4 + (128 * c + j + 2))
                        TS(dots_t[:, bass.ds(i * 4 + (128 * c + j), 1)], dot4[:, j:j + 1], 1.0, None,
                           ALU.mult).then_inc(S["dcp"], 1)
                        dve.wait_ge(S["dcp"], i * 4 + (128 * c + j + 1))
            link(V.memset(acts[:, 16:32, :], 0.0))
            for c in range(2):
                cc = slice(c * P, c * P + P)
                dve.wait_ge(S["gg"], 2 + c)
                link(TT(dots_t[:, cc], dots_t[:, cc], gsm_t[:, cc], ALU.mult))
            for c in range(2):
                with dve.Fori(0, 32) as i:
                    for j in range(4):
                        dve.wait_ge(S[f"gat{j}"], i * 16 + 16 * (64 + 32 * c + 1))
                        dve.wait_ge(S["used"], i * 4 + (256 + 128 * c + j + 1))
                        STT(p_acc[c], gslot[j], dots_t[:, bass.ds(i * 4 + (128 * c + j), 1)], p_acc[c], ALU.mult,
                            ALU.add).then_inc(S["used"], 1)
            for c in range(2):
                for b in range(4):
                    dve.wait_ge(S["tout"], 4 * c + b + 1)
                    for k in range(4):
                        xs = x_res[:, 4 * b + k, c * P:(c + 1) * P]
                        ins = STT(xs, ps[:, 4 * c + b, k * P:(k + 1) * P], modcol(11, 1, 4 * b + k), xs, ALU.mult,
                                  ALU.add)
                        if k < 3:
                            link(ins, wait=False)
                        else:
                            link.wait()
                            ins.then_inc(S["xout"], 1)


def panels(w):
    k, n = w.shape
    return w.reshape(k // 1024, 8, P, n // P, P).transpose(3, 0, 2, 1, 4).reshape(-1, P, PW)


def column(v):
    return v.reshape(-1, P).T


def layout(i):
    g = {k: np.asarray(v) for k, v in i.items()}
    w_in = g["w_in"][0]
    parts = [panels(w_in[:, :4096]), panels(g["w_glu"][0])]
    ga, gb = panels(w_in[:, 4096:6144]), panels(w_in[:, 6144:])
    ws, wa = panels(g["w_proj_ssm"][0]), panels(g["w_proj_attn"][0])
    merge = np.concatenate([ga.reshape(16, 2, P, PW), gb.reshape(16, 2, P, PW), ws[:, None], wa[:, None]], 1)
    parts += [merge.reshape(-1, P, PW), panels(g["w_out"][0])]
    f1, f2 = g["w_ff1"][0], g["w_ff2"][0]
    for q in range(4):
        parts += [panels(f1[:, q * D:(q + 1) * D]), panels(f2[q * D:(q + 1) * D])]
    w2 = g["w_in_2"][0]
    q, kc, vc, ks, vs, kw, vw, gl, xr, xg = np.split(
        w2, np.cumsum([1024, 256, 256, 256, 256, 256, 256, 24, 1024]), axis=1)
    gl = np.concatenate([gl, np.zeros((D, P - 24), np.float32)], 1)
    parts.append(panels(np.concatenate([q, kc, ks, kw, vc, vs, vw, xr, xg, gl], 1)))
    for name in ("lru_wa_2", "lru_wi_2"):
        parts.append(g[name][0].transpose(1, 0, 2).reshape(1, P, PW))
    for name in ("cmp_w_k_2", "cmp_w_v_2"):
        parts.append(panels(g[name][0]))
    parts += [panels(g["w_out_2"][0]), panels(g["peer_wq_2"][0])]
    keys = g["peer_keys_2"][0].reshape(2, 8, P, P)
    parts.append(keys.transpose(0, 3, 1, 2).reshape(2, P, PW))
    w = np.concatenate(parts)
    assert w.shape[0] == PANELS
    ada = np.stack([g["w_ada"][0], g["ada_w_2"][0]])
    ada = ada.reshape(2, DC, P, 3, HALVES, PW).transpose(0, 3, 1, 4, 2, 5).reshape(-1, P, PW)
    cols = np.zeros((P, COLS), np.float32)

    def put(name, value):
        at, n = COL[name]
        cols[:value.shape[0], at:at + value.shape[1]] = value

    for name in ("c", "c_2", "b_ada", "ada_b_2", "norm_mix_g", "norm_mlp_g", "norm_final_g", "norm_mix_g_2",
                 "norm_ffn_g_2", "ssm_a_re", "ssm_a_im", "ssm_d", "b_glu", "q_norm_g_2", "k_norm_g_2", "conv_b_2",
                 "lru_ba_2", "lru_bi_2", "lru_lam_2"):
        put(name, column(g[name].reshape(-1)))
    put("ssm_log_dt", column(np.repeat(g["ssm_log_dt"].reshape(-1), 64)))
    put("gate_b_2", g["gate_b_2"].reshape(-1, 1))
    put("conv_w_2", column(g["conv_w_2"].reshape(-1)))
    put("out_g_2", np.concatenate([column(g["out_g_attn_2"].reshape(-1)), column(g["out_g_rnn_2"].reshape(-1))], 1))
    put("cmp_pe_k_2", g["cmp_pe_k_2"][0].T)
    put("cmp_pe_v_2", g["cmp_pe_v_2"][0].T)

    def blocks(v):
        out = np.zeros((2, 64, 32, 2, 16), np.float32)
        v = v.reshape(32, 2, 64, 16)
        for e in range(2):
            out[e, :, :, e, :] = v[:, e].transpose(1, 0, 2)
        return out.reshape(P, 32, 32)

    b_x = np.stack([blocks(g["ssm_b_re"][0]), blocks(g["ssm_b_im"][0])], 1)
    c_x = np.stack([blocks(g["ssm_c_re"][0].transpose(0, 2, 1)), blocks(g["ssm_c_im"][0].transpose(0, 2, 1))], 1)
    return {
        "w": w, "ada": ada, "cols": cols, "consts": constants(),
        "xT": g["x"][0].T.reshape(DC, P, T).transpose(1, 0, 2), "b_x": b_x, "c_x": c_x,
        "relb": g["rel_bias"], "down": g["peer_down_2"][0], "up": g["peer_up_2"][0],
    }


def kernel(**inputs):
    import concourse.bacc as bacc
    from concourse.bass_utils import run_bass_kernel_spmd

    nc = bacc.Bacc("TRN2", target_bir_lowering=False, num_devices=1)
    arrays = {f"in_{k}": np.ascontiguousarray(v) for k, v in layout(inputs).items()}
    a = {k[3:]: nc.dram_tensor(k, v.shape, mybir.dt.from_np(v.dtype), kind="ExternalInput").ap()
         for k, v in arrays.items()}
    a["line"] = nc.dram_tensor("bias_line", (8, P * 3 * P), F32, kind="Internal").ap()
    out = nc.dram_tensor("out", (P, DC, T), F32, kind="ExternalOutput").ap()
    a["out"] = out
    build(nc, a)
    r = run_bass_kernel_spmd(nc, [arrays], core_ids=[0])
    o = r.results[0]["out"]
    return o.transpose(2, 1, 0).reshape(1, T, D)
```

```python
from contextlib import ExitStack

import numpy as np
import concourse.bass as bass
from concourse import mybir

F32 = mybir.dt.float32
F32R = mybir.dt.float32r
I32 = mybir.dt.int32
U32 = mybir.dt.uint32
ALU = mybir.AluOpType
ACT = mybir.ActivationFunctionType
AX = mybir.AxisListType

P = 128
T = 256
D = 2048
DC = D // P
EPS = 1e-6
NEG = -1e30

COL = {}


def _columns():
    at = 0
    for name, n in (
        ("c", DC), ("c_2", DC), ("b_ada", 6 * DC), ("ada_b_2", 6 * DC),
        ("norm_mix_g", DC), ("norm_mlp_g", DC), ("norm_final_g", DC), ("norm_mix_g_2", DC), ("norm_ffn_g_2", DC),
        ("ssm_a_re", 32), ("ssm_a_im", 32), ("ssm_log_dt", 32), ("ssm_d", 8), ("b_glu", 8),
        ("q_norm_g_2", 1), ("k_norm_g_2", 3), ("gate_b_2", 1), ("conv_w_2", 32), ("conv_b_2", 8),
        ("lru_ba_2", 8), ("lru_bi_2", 8), ("lru_lam_2", 8), ("out_g_2", DC),
        ("cmp_pe_k_2", 32), ("cmp_pe_v_2", 32),
    ):
        COL[name] = (at, n)
        at += n
    return at


COLS = _columns()

PW = 1024
RAW, HI, LO = 4, 4, 2
PAN = {}


def _panels():
    at = 0
    for name, n in (
        ("u", 16), ("qkv", 48), ("glu", 8), ("merge", 96), ("out", 32), ("ff", 256),
        ("in2", 32), ("lru", 2), ("in2b", 24), ("cmp", 8), ("in2c", 18), ("out2", 32), ("wq", 32), ("keys", 2),
    ):
        PAN[name] = at
        at += n
    return at


PANELS = _panels()


class Chain:

    def __init__(self, engine, semaphore):
        self.engine, self.semaphore, self.n = engine, semaphore, 0

    def __call__(self, instruction, wait=True):
        instruction.then_inc(self.semaphore, 1)
        self.n += 1
        if wait:
            self.engine.wait_ge(self.semaphore, self.n)

    def wait(self):
        self.engine.wait_ge(self.semaphore, self.n)


GRP = {}


def _groups():
    at = 0
    for name, n in (
        ("u", 8), ("qkv", 24), ("glu", 8), ("merge", 16), ("out", 16), ("ff", 128),
        ("in2", 37), ("out2", 16), ("wq", 16),
    ):
        GRP[name] = at
        at += n


_groups()
ADA_GROUPS, HALVES = 6, 4
SC = float(P) ** -0.5
TWO_PI = (6.28125, 0.0019350051879882812, 3.0199159819e-07)
IN2_PLACES = (20, 24, 28, None, (8, 9, 14, 15), 10, 16, 0, 4)
PAIRS = (0, 2, 4, 6, 10, 12)
MOD_PARTS = [(3 + n // 3, (0, 4, 12)[n % 3], (1, 2, 1)[n % 3]) for n in range(9)]
N2 = 32
PICKS = 128
LN2 = (0.693359375, -2.12194440e-4)

CON = {}
CON_N = (("ident", P), ("swap", P), ("rope_cos", T), ("rope_sin", T), ("causal", 3 * P), ("cmp_add", 2 * 16),
         ("cmp_mul", 2 * 16), ("bucket", 384), ("iota16", 16))


def _consts():
    at = 0
    for name, n in CON_N:
        CON[name] = (at, n)
        at += n
    return at


CONSTS = _consts()


SEMS = """
small xload bload land0 land1 land2 land3 aland0 aland1 aland2 aland3 hi lo panel freed init sigc ada
adaps adacol sq ss mean rs nt nh op chain_v chain_p chain_a par ang sin bf bt btc cs cx vmm wdone prod
ymm yadd yg ghi glo gmul msig mterm hid ffc line_ps line line_out bias vt vtc sc sm ex pn tp ptc pv ov
uop gn zsq zss zmean zrs zy zsw zrot blkd lsig lsq lgel gsig rnn kcc ksq kss kmean krs kcd vcc vctp vctc
vtt2 vtc2 gtt gtc csc cmx cex cpn cpt ptct ysq yss ymean yrs yy yhi yop hft hfc scc eix g1 gg stage used
dcp gat0 gat1 gat2 gat3 tout xout store
"""


def constants():
    out = np.zeros((P, CONSTS), np.float32)

    def put(name, value):
        at, n = CON[name]
        out[:value.shape[0], at:at + n] = value

    put("ident", np.eye(P, dtype=np.float32))
    half = P // 2
    swap = np.zeros((P, P), np.float32)
    for i in range(half):
        swap[half + i, i] = -1.0
        swap[i, half + i] = 1.0
    put("swap", swap)
    freqs = (np.float32(10000.0) ** (-np.arange(half, dtype=np.float32) / np.float32(half))).astype(np.float32)
    ang = (np.arange(T, dtype=np.float32)[:, None] * freqs[None]).astype(np.float32)
    put("rope_cos", np.concatenate([np.cos(ang), np.cos(ang)], 1).T.astype(np.float32))
    put("rope_sin", np.concatenate([np.sin(ang), np.sin(ang)], 1).T.astype(np.float32))
    p = np.arange(P)
    m = np.arange(3 * P)
    put("causal", np.where(m[None] - P > p[:, None] + 0, NEG, 0.0).astype(np.float32)[:, :3 * P])
    add, mul = np.zeros((P, 2, 16), np.float32), np.zeros((P, 2, 16), np.float32)
    for qc in range(2):
        for n in range(16):
            ok = (n < 15) & (16 * n + 31 <= qc * P + p)
            add[:, qc, n] = np.where(ok, 0.0, NEG)
            mul[:, qc, n] = ok
    put("cmp_add", add.reshape(P, 32))
    put("cmp_mul", mul.reshape(P, 32))
    rel = 255 - np.arange(384)
    n = np.maximum(rel, 0)
    nf = np.maximum(n, 1).astype(np.float32)
    large = 16 + (np.log(nf / np.float32(16)) / np.float32(np.log(8.0)) * np.float32(16)).astype(np.int32)
    bucket = np.where(n < 16, n, np.minimum(large, 31))
    hot = np.zeros((P, 384), np.float32)
    for b in range(32):
        hot[b] = (bucket == b) & (rel >= 0)
    hot[32] = rel < 0
    put("bucket", hot)
    put("iota16", np.broadcast_to(np.arange(16, dtype=np.float32), (P, 16)))
    return out



def build(nc, a):
    ctx = ExitStack()
    with ctx:
        def sb(name, shape, dt=F32):
            return ctx.enter_context(nc.sbuf_tensor(name, shape, dt))

        x_res = sb("x_res", [P, DC, T])
        cols = sb("cols", [P, COLS])
        con = sb("con", [P, CONSTS])
        ones = sb("ones", [P, P])
        mod = sb("mod", [P, 12 * DC])
        gain = sb("gain", [P, DC])
        rstd = sb("rstd", [P, 2, T])
        csil = sb("csil", [P, 2, DC])
        sg = sb("sg", [P, 4, T])
        mix = sb("mix", [P, 2, T])
        stat = sb("stat", [P, 5, 32])
        sp4 = sb("sp4", [P, 8])
        gate_t = sb("gate_t", [P, 2, 24])
        kcn = sb("kcn", [P, 32])
        kcn2 = sb("kcn2", [P, 32])
        kcr = sb("kcr", [P, 2, 32])
        vcx = sb("vcx", [P, 32])
        cs = sb("cs", [P, 3, 16])
        dot4 = sb("dot4", [P, 4])
        zero1 = sb("zero1", [P, 1], I32)
        st_a = [sb(f"st_a{i}", [P, 1], I32) for i in range(4)]
        st_b = [sb(f"st_b{i}", [P, 1], I32) for i in range(4)]
        raws = sb("raws", [P, RAW, PW])
        raw = [raws[:, i, :] for i in range(RAW)]
        w_hi = [sb(f"w_hi{i}", [P, 8, P], F32R) for i in range(HI)]
        w_lo = [sb(f"w_lo{i}", [P, 8, P], F32R) for i in range(LO)]
        a_raws = sb("a_raws", [P, HALVES, PW])
        a_raw = [a_raws[:, i, :] for i in range(HALVES)]
        a_acc = sb("a_acc", [P, HALVES, PW])
        opa_hi = sb("opa_hi", [P, DC, T], F32R)
        opa_lo = sb("opa_lo", [P, DC, T], F32R)
        acts = sb("acts", [P, 32, T])
        tmp = acts[:, 16:32, :]
        with ExitStack() as early:
            def es(name, shape, dt=F32):
                return early.enter_context(nc.sbuf_tensor(name, shape, dt))
            ssm_w = es("ssm_w", [P, 2, 4, 2, T])
            ssm_cs = es("ssm_cs", [P, 2, 2, 2, T])
            ssm_r2 = es("ssm_r2", [P, 2, T])
            ssm_t2 = es("ssm_t2", [P, 2, T])
            ssm_par = es("ssm_par", [P, 32, 32])
        idx_t = sb("idx_t", [P, 2 * PICKS], I32)
        opb_hi = sb("opb_hi", [P, DC, T], F32R)
        opb_lo = sb("opb_lo", [P, DC, T], F32R)

        def flat(ap):
            return ap.rearrange("p a t -> p (a t)")

        e_tab = flat(acts[:, 8:16, :]).rearrange("p (f g n) -> p f g n", f=4, g=32)
        b_t = flat(acts[:, 16:24, :]).rearrange("p (r j s) -> p r j s", r=2, j=8)
        c_x = flat(acts[:, 24:32, :]).rearrange("p (r g m) -> p r g m", r=2, g=32)
        ssm_flat = ssm_w[:, :, :, :, :].rearrange("p a b c t -> p (a b c t)")
        b_x = ssm_flat[:, 0:2048].rearrange("p (r g m) -> p r g m", r=2, g=32)
        b_f = ssm_flat[:, 2048:4096].rearrange("p (r g m) -> p r g m", r=2, g=32)
        b_tmp = ssm_cs[:, :, :, :, :].rearrange("p a b c t -> p (a b c t)")[:, 0:2048].rearrange(
            "p (r g m) -> p r g m", r=2, g=32)
        v_tok = flat(acts[:, 0:8, :]).rearrange("p (k h d) -> p k h d", k=2, h=8)
        p_buf = acts[:, 24:28, :]
        pt_buf = mix
        score_bank = (4, 5, 2, 3)
        bias = [sg[:, h, :] if h < 4 else acts[:, 24 + h, :] for h in range(8)]
        acc16 = a_acc[:, :, :].rearrange("p h (c t) -> p (h c) t", t=T)
        raw16 = a_raws[:, :, :].rearrange("p h (c t) -> p (h c) t", t=T)
        u_buf, r_buf = raw16[:, 0:8, :], raw16[:, 8:16, :]
        i_buf, q_buf = acts[:, 20:28, :], acc16[:, 5:13, :]
        blk = [flat(acts[:, 4 * i:4 * i + 4, :])[:, 0:960] for i in range(2)]
        blk_hi = [flat(opb_hi[:, 4 * i:4 * i + 4, :])[:, 0:960] for i in range(2)]
        blk_lo = [flat(opb_lo[:, 4 * i:4 * i + 4, :])[:, 0:960] for i in range(2)]
        v_tok2 = flat(acts[:, 20:24, :]).rearrange("p (k v d) -> p k v d", k=2, v=4)
        pct = flat(acc16[:, 5:13, :]).rearrange("p (u q) -> p u q", u=16)
        pc = acc16[:, 13, :].rearrange("p (u n) -> p u n", u=16)
        vct = acc16[:, 14, :].rearrange("p (g d) -> p g d", g=2)
        hf = [flat(acts[:, 8 * c:8 * c + 8, :]) for c in range(2)]
        score = flat(acts[:, 16:32, :]).rearrange("p (u k) -> p u k", u=32)
        p_acc = [flat(acts[:, 16 + 8 * c:24 + 8 * c, :]) for c in range(2)]
        top_v = flat(raw16[:, 0:2, :]).rearrange("p (u k) -> p u k", u=32)
        top_i = flat(raw16[:, 2:4, :]).rearrange("p (u k) -> p u k", u=32)
        top_u = top_i.bitcast(U32)
        top_f = flat(raw16[:, 4:6, :]).rearrange("p (u k) -> p u k", u=32)
        val = raw16[:, 6, :].rearrange("p (u k) -> p u k", u=16)
        pick = raw16[:, 7, :].rearrange("p (u k) -> p u k", u=16)
        dec = [raw16[:, 8 + i, :].rearrange("p (u k) -> p u k", u=16) for i in range(8)]
        cand = flat(acc16).rearrange("p (u k) -> p u k", u=16)
        gslot = [flat(raws[:, 2 * i:2 * i + 2, :]) for i in range(2)] + [
            flat(a_acc[:, 2 * i:2 * i + 2, :]) for i in range(2)]
        dots_t, gsm_t = raw16[:, 0, :], raw16[:, 15, :]
        line = flat(rstd[0:8, :, :])[:, 0:384]
        rel_b = mix[0:33, 1, 0:8]

        ps = ctx.enter_context(nc.psum_tensor("ps", [P, 8, 512], F32))

        S = {n: ctx.enter_context(nc.semaphore("s_" + n)) for n in SEMS.split()}
        land = [S[f"land{i}"] for i in range(4)]
        aland = [S[f"aland{i}"] for i in range(4)]

        def col(name, j=0, n=1):
            at = COL[name][0] + j
            return cols[:, at:at + n]

        def cst(name):
            at, n = CON[name]
            return con[:, at:at + n]

        ident = cst("ident")
        par = lambda i: ssm_par[:, i, :]
        DT, MAG, CO, SI, FR, FI, PCO, PSI = 0, 1, 2, 3, 4, 5, 6, 14
        X1, X2, X3, X4, X5 = 22, 23, 24, 25, 26
        UNITS = 16
        mean2, rs2 = [mix[:, :, :], sg[:, 0:2, :]], [rstd[:, :, :], sg[:, 2:4, :]]

        def modcol(v, n=DC, j=0):
            return mod[:, v * DC + j:v * DC + j + n]

        block = ctx.enter_context(nc.Block())

        @block.sync
        def _(sp):
            sp.dma_start(cols[:, :], a["cols"]).then_inc(S["small"], 16)
            sp.dma_start(con[:, :], a["consts"]).then_inc(S["small"], 16)

            def load_w(p, slot, first=False):
                if not first:
                    sp.wait_ge(S["lo"], p - 3)
                sp.dma_start(raw[slot], a["w"][bass.ds(p, 1)].rearrange("o p n -> (o p) n")).then_inc(
                    land[slot], 16)

            def load_a(q, slot, first=False):
                if not first:
                    sp.wait_ge(S["ada"], q - 3)
                sp.dma_start(a_raw[slot], a["ada"][bass.ds(q, 1)].rearrange("o p n -> (o p) n")).then_inc(
                    aland[slot], 16)

            for h in range(HALVES):
                load_a(h, h, first=True)
            sp.dma_start(x_res[:, :, :], a["xT"]).then_inc(S["xload"], 16)
            sp.dma_start(b_x, a["b_x"]).then_inc(S["bload"], 16)
            with sp.Fori(1, 16) as k:
                for h in range(HALVES):
                    load_a(k * HALVES + h, h)
            for p in range(4):
                load_w(p, p, first=True)
            sp.wait_ge(S["op"], 4)
            sp.dma_start(c_x, a["c_x"]).then_inc(S["cx"], 16)

            def stream(p0, n, aq=None, na=8):
                for j in range(n):
                    load_w(p0 + j, j % 4)
                    if aq is not None and j < na:
                        load_a(aq + j, j % 4)

            for j in range(8):
                load_w(4 + j, j % 4)
                load_a(64 + j, j % 4)
            stream(12, 8, 72)
            with sp.Fori(0, 6) as i:
                stream(PAN["qkv"] + 4 + i * 8, 8, i * 8 + 80)
            stream(PAN["glu"] + 4, 8)
            sp.wait_ge(S["op"], 4 + 8)
            sp.dma_start(mix[0:32, 1, 0:8], a["relb"]).then_inc(S["bload"], 16)
            sp.wait_ge(S["line"], 1)
            sp.dma_start(a["line"].rearrange("h (p m) -> h p m", p=P),
                         line.unsqueeze(1).broadcast_to([8, P, 3 * P])).then_inc(S["line_out"], 16)
            sp.wait_ge(S["line_out"], 16)
            sp.wait_ge(S["vt"], 4)
            for h in range(8):
                src = bass.AP(a["line"].tensor, h * P * 3 * P + P - 1, [[3 * P - 1, P], [1, T]])
                sp.dma_start(bias[h], src).then_inc(S["bias"], 16)
            with sp.Fori(0, 8) as i:
                stream(PAN["merge"] + 4 + i * 12, 12, i * 8 + 128)
            for n, (g, k0, per) in enumerate(MOD_PARTS):
                with sp.Fori(0, 4) as i:
                    stream(PAN["out"] + 4 + 32 * n + i * 8, 8, i * (4 * per) + (64 * g + 4 * k0), 4 * per)
            with sp.Fori(0, (PANELS - PAN["in2"] - 4) // 8) as i:
                stream(PAN["in2"] + 4 + i * 8, 8)
            for p in range(PANELS - 2, PANELS):
                load_w(p, p % 4)
            for c in range(2):
                sp.wait_ge(S["xout"], 4 * (c + 1))
                ts = slice(c * P, c * P + P)
                sp.dma_start(a["out"][:, :, ts], x_res[:, :, ts]).then_inc(S["store"], 16)
            sp.wait_ge(S["store"], 32)
            for s in range(4):
                sp.wait_ge(land[s], 16 * ((PANELS - s + 3) // 4))
                sp.wait_ge(aland[s], 16 * 96)

        @block.tensor
        def _(pe):
            def mm(out, lhs, rhs, start, stop):
                return nc.tensor.matmul(out, lhs, rhs, start=start, stop=stop)

            def panel(p, j, out, rhs, c0, first, last):
                hi, lo = w_hi[j % 4], w_lo[j % 2]
                pe.wait_ge(S["lo"], p + 1)
                for b in range(8):
                    mm(out, hi[:, b, :], rhs[0][:, c0 + b, :], first and b == 0, False)
                    mm(out, hi[:, b, :], rhs[1][:, c0 + b, :], False, False)
                    m = mm(out, lo[:, b, :], rhs[0][:, c0 + b, :], False, last and b == 7)
                m.then_inc(S["panel"], 1)

            opa, opb = (opa_hi, opa_lo), (opb_hi, opb_lo)

            def linear(p0, g0, rhs, groups=4, wait=True, ready=None, off=0):
                for j in range(groups):
                    if wait:
                        pe.wait_ge(S["freed"], g0 + j - 3)
                    out = ps[:, j % 4, 0:T]
                    if ready and j == 0:
                        pe.wait_ge(S[ready[0]], ready[1])
                    panel(p0 + 2 * j, off + 2 * j, out, rhs, 0, True, False)
                    if ready and j == 0:
                        pe.wait_ge(S[ready[0]], ready[2])
                    panel(p0 + 2 * j + 1, off + 2 * j + 1, out, rhs, 8, False, True)

            def part(n, g0, rhs, ready):
                g, k0, per = MOD_PARTS[n]
                p0 = PAN["out"] + 32 * n
                linear(p0, g0, rhs, ready=ready)
                if k0 == 0:
                    ada_sums(g - 1)
                with pe.Fori(1, 4) as i:
                    linear(p0 + i * 8, g0 + i * 4, rhs)

            def ada_sums(g):
                pe.wait_ge(S["ada"], 64 * (g + 1))
                if g:
                    pe.wait_ge(S["adacol"], g)
                for h in range(HALVES):
                    for b in range(8):
                        m = mm(ps[:, 7, 8 * h + b:8 * h + b + 1], a_acc[:, h, b * P:(b + 1) * P], ones[:, 0:1],
                               True, True)
                m.then_inc(S["adaps"], 1)

            def norm(n):
                for j in range(4):
                    pe.wait_ge(S["sq"], 4 * n + j + 1)
                    for k in range(4 * j, 4 * j + 4):
                        m = mm(ps[:, 6, 0:T], ones[:, :], tmp[:, k, :], k == 0, k == DC - 1)
                m.then_inc(S["ss"], 1)

            def scores(n, at, qc, q, k):
                if n >= 4:
                    pe.wait_ge(S["sm"], at - 3)
                mm(ps[:, score_bank[n % 4], 0:P * (qc + 1)], q, k, True, True).then_inc(S["sc"], 1)

            def turn_rows(n, at, qc):
                pe.wait_ge(S["pn"], at + 1)
                if n >= 2:
                    pe.wait_ge(S["ptc"], at - 1)
                for kc in range(qc + 1):
                    m = nc.tensor.transpose(ps[:, 6 + n % 2, kc * P:(kc + 1) * P],
                                            p_buf[:, n % 4, kc * P:(kc + 1) * P], ident)
                m.then_inc(S["tp"], 1)

            pe.wait_ge(S["small"], 32)
            pe.wait_ge(S["init"], 1)
            norm(0)
            ada_sums(0)
            pe.wait_ge(S["op"], 4)
            linear(0, 0, opa, wait=False)
            linear(8, 4, opa)
            pe.wait_ge(S["bf"], 1)
            for j in range(8):
                if j >= 4:
                    pe.wait_ge(S["btc"], j - 3)
                for r in range(2):
                    src = b_f[:, r, 4 * j:4 * j + 4, :].rearrange("p g m -> p (g m)")
                    m = nc.tensor.transpose(ps[:, 4 + j % 4, r * P:(r + 1) * P], src, ident)
                m.then_inc(S["bt"], 1)
            pe.wait_ge(S["freed"], 8)
            pe.wait_ge(S["btc"], 8)
            pe.wait_ge(S["cx"], 16)

            def drive(s):
                if s >= 2:
                    pe.wait_ge(S["wdone"], s - 1)
                j = s // 2
                for i in (2 * (s % 2), 2 * (s % 2) + 1):
                    rows = slice(32 * i, 32 * i + 32)
                    for r in range(2):
                        m = mm(ps[:, 4 + i, r * T:(r + 1) * T], b_t[rows, r, j, :], acts[rows, j, :], True, True)
                m.then_inc(S["vmm"], 1)

            def read_out(s):
                pe.wait_ge(S["prod"], s + 1)
                j = s // 2
                if s % 2 == 0 and j >= 2:
                    pe.wait_ge(S["yadd"], j - 1)
                w = ssm_w[:, s % 2]
                for g in range(2):
                    i = 2 * (s % 2) + g
                    out = ps[32 * i:32 * i + 32, j % 2, 0:T]
                    tile = 4 * j + i
                    for n, (r, part) in enumerate(((0, 0), (0, 1), (1, 2), (1, 3))):
                        m = mm(out, c_x[:, r, tile, :], w[:, part, g, :], n == 0, n == 3)
                m.then_inc(S["ymm"], 1)

            drive(0)
            for s in range(16):
                if s + 1 < 16:
                    drive(s + 1)
                read_out(s)
            with pe.Fori(0, 6) as i:
                linear(PAN["qkv"] + i * 8, GRP["qkv"] + i * 4, opa)
            for n in range(8):
                if n == 0:
                    pe.wait_ge(S["glo"], 1)
                pe.wait_ge(S["freed"], GRP["glu"] + n - 3)
                panel(PAN["glu"] + n, n, ps[:, n % 4, 0:T], opb, 8, True, True)
            ada_sums(1)
            pe.wait_ge(S["bload"], 32)
            pe.wait_ge(S["init"], 2)
            mm(ps[0:8, 6, 0:384], rel_b, con[0:33, CON["bucket"][0]:CON["bucket"][0] + 384], True, True).then_inc(
                S["line_ps"], 1)
            pe.wait_ge(S["freed"], GRP["merge"])
            for b in range(4):
                for kc in range(2):
                    for hh in range(2):
                        at = (2 * kc + hh) * P
                        m = nc.tensor.transpose(ps[:, b, at:at + P], acts[:, 24 + 2 * b + hh, kc * P:(kc + 1) * P],
                                                ident)
                m.then_inc(S["vt"], 1)
            for n in range(-2, UNITS + 3):
                if n == 0:
                    pe.wait_ge(S["vtc"], 4)
                if n + 2 < UNITS:
                    h, qc = (n + 2) // 2, n % 2
                    scores(n + 2, n + 2, qc, acts[:, 8 + h, qc * P:(qc + 1) * P], acts[:, 16 + h, 0:P * (qc + 1)])
                if 2 <= n < UNITS + 2:
                    turn_rows(n - 2, n - 2, n % 2)
                if n >= 3:
                    u = n - 3
                    pe.wait_ge(S["ptc"], u + 1)
                    if u >= 2:
                        pe.wait_ge(S["ov"], u - 1)
                    for kc in range(u % 2 + 1):
                        m = mm(ps[:, u % 2, 0:P], v_tok[:, kc, u // 2, :], pt_buf[:, u % 2, kc * P:(kc + 1) * P],
                               kc == 0, kc == u % 2)
                    m.then_inc(S["pv"], 1)
            pe.wait_ge(S["ov"], UNITS)
            with pe.Fori(0, 8) as i:
                for par_ in range(2):
                    p0 = PAN["merge"] + i * 12 + 6 * par_
                    b0 = 4 * par_
                    pe.wait_ge(S["freed"], GRP["merge"] + 2 * i + par_ - 1)
                    for g in range(2):
                        panel(p0 + 2 * g, 6 * par_ + 2 * g, ps[:, b0 + g, 0:T], opa, 0, True, False)
                        panel(p0 + 2 * g + 1, 6 * par_ + 2 * g + 1, ps[:, b0 + g, 0:T], opa, 8, False, True)
                    for g in range(2):
                        panel(p0 + 4 + g, 6 * par_ + 4 + g, ps[:, b0 + 2 + g, 0:T], opb, 8 * g, True, True)
            pe.wait_ge(S["freed"], GRP["out"])
            part(0, GRP["out"], opa, ("op", 14, 16))
            norm(1)
            for q in range(4):
                part(1 + 2 * q, GRP["ff"] + 32 * q, opa, ("op", 18, 20))
                part(2 + 2 * q, GRP["ff"] + 32 * q + 16, opb, ("hid", 16 * q + 8, 16 * q + 16))
            norm(2)
            ada_sums(5)
            norm(3)
            with pe.Fori(0, 4) as i:
                linear(PAN["in2"] + i * 8, GRP["in2"] + i * 4, opa, ready=("op", 22, 24))
            pe.wait_ge(S["uop"], 1)
            for r in range(2):
                p = PAN["lru"] + r
                pe.wait_ge(S["lo"], p + 1)
                if r == 1:
                    pe.wait_ge(S["lsig"], 8)
                for b in range(8):
                    out = ps[:, 4 + b // 2, (b % 2) * T:(b % 2 + 1) * T]
                    mm(out, w_hi[p % 4][:, b, :], opb_hi[:, 8 + b, :], True, False)
                    mm(out, w_hi[p % 4][:, b, :], opb_lo[:, 8 + b, :], False, False)
                    m = mm(out, w_lo[p % 2][:, b, :], opb_hi[:, 8 + b, :], False, True)
                m.then_inc(S["panel"], 1)
            with pe.Fori(0, 2) as i:
                linear(PAN["in2b"] + i * 8, GRP["in2"] + 16 + i * 4, opa, off=PAN["in2b"] % 4)
            pe.wait_ge(S["lsig"], 16)
            mm(ps[:, 4, :], cst("swap"), flat(acts[:, 8:10, :]), True, True).then_inc(S["zsw"], 1)
            linear(PAN["in2b"] + 16, GRP["in2"] + 24, opa, off=PAN["in2b"] % 4)
            pe.wait_ge(S["blkd"], 1)
            for x in range(2):
                for j in range(4):
                    p = PAN["cmp"] + 4 * x + j
                    pe.wait_ge(S["lo"], p + 1)
                    for b in range(8):
                        at = 30 * (8 * j + b)
                        hi, lo = blk_hi[x][:, at:at + 30], blk_lo[x][:, at:at + 30]
                        first, last = j + b == 0, j == 3 and b == 7
                        mm(ps[:, 6 + x, 0:30], w_hi[p % 4][:, b, :], hi, first, False)
                        mm(ps[:, 6 + x, 0:30], w_hi[p % 4][:, b, :], lo, False, False)
                        m = mm(ps[:, 6 + x, 0:30], w_lo[p % 2][:, b, :], hi, False, last)
                    m.then_inc(S["panel"], 1)
            with pe.Fori(0, 2) as i:
                linear(PAN["in2c"] + i * 8, GRP["in2"] + 28 + i * 4, opa, off=PAN["in2c"] % 4)
            linear(PAN["in2c"] + 16, GRP["in2"] + 36, opa, groups=1, off=PAN["in2c"] % 4)
            pe.wait_ge(S["vcc"], 1)
            pe.wait_ge(S["kcc"], 1)
            for i in range(7):
                if i < 6:
                    pe.wait_ge(S["zsq"], i + 1)
                    if i >= 2:
                        pe.wait_ge(S["zmean"], i - 1)
                    sq2 = flat(r_buf[:, 2 * (i % 2):2 * (i % 2) + 2, :])
                    mm(ps[:, 4 + i % 2, :], ones[:, :], sq2, True, True).then_inc(S["zss"], 1)
                if i >= 1:
                    k = i - 1
                    pe.wait_ge(S["zy"], k + 1)
                    if k >= 2:
                        pe.wait_ge(S["zrot"], k)
                    mm(ps[:, 6 + k % 2, :], cst("swap"), flat(acts[:, PAIRS[k]:PAIRS[k] + 2, :]), True,
                       True).then_inc(S["zsw"], 1)
            pe.wait_ge(S["freed"], GRP["out2"])
            pe.wait_ge(S["zrot"], 7)
            pe.wait_ge(S["ksq"], 1)
            mm(ps[:, 2, 0:30], ones[:, :], kcn2[:, 0:30], True, True).then_inc(S["kss"], 1)
            pe.wait_ge(S["vcc"], 1)
            for g in range(2):
                m = nc.tensor.transpose(ps[0:15, 3, g * P:(g + 1) * P], vcx[:, 15 * g:15 * g + 15], ident)
            m.then_inc(S["vctp"], 1)
            pe.wait_ge(S["lsig"], 16)
            for v in range(4):
                for kc in range(2):
                    at = ((v % 2) * 2 + kc) * P
                    m = nc.tensor.transpose(ps[:, 4 + v // 2, at:at + P], acts[:, 16 + v, kc * P:(kc + 1) * P], ident)
                if v % 2:
                    m.then_inc(S["vtt2"], 1)
            pe.wait_ge(S["gsig"], 1)
            for qc in range(2):
                m = nc.tensor.transpose(ps[:, 6, qc * P:(qc + 1) * P], acc16[:, 4, qc * P:(qc + 1) * P], ident)
            m.then_inc(S["gtt"], 1)
            pe.wait_ge(S["kcd"], 1)
            for u in range(16):
                h, qc = u // 2, u % 2
                g = h // 4
                m = mm(ps[:, 7, 16 * u:16 * u + 15], acts[:, h, qc * P:(qc + 1) * P], kcn[:, 15 * g:15 * g + 15],
                       True, True)
            m.then_inc(S["csc"], 1)
            pe.wait_ge(S["cpn"], 1)
            pe.wait_ge(S["vctc"], 1)
            for u in range(16):
                m = nc.tensor.transpose(ps[0:15, u // 4, (u % 4) * P:(u % 4 + 1) * P], pc[:, u, 0:15], ident)
                if u % 4 == 3:
                    m.then_inc(S["cpt"], 1)
            pe.wait_ge(S["ptct"], 4)
            pe.wait_ge(S["vtc2"], 2)
            pe.wait_ge(S["gtc"], 1)
            for n in range(-2, N2 + 3):
                if n + 2 < N2:
                    m = n + 2
                    h, qc, kind = m // 4, m // 2 % 2, m % 2
                    scores(m, UNITS + m, qc, acts[:, h, qc * P:(qc + 1) * P],
                           acts[:, 10 + 2 * kind + h // 4, 0:P * (qc + 1)])
                if 2 <= n < N2 + 2:
                    turn_rows(n - 2, UNITS + n - 2, (n - 2) // 2 % 2)
                if n >= 3:
                    k = n - 3
                    h, qc, kind, u = k // 4, k // 2 % 2, k % 2, k // 2
                    pe.wait_ge(S["ptc"], UNITS + k + 1)
                    if kind == 0 and u >= 2:
                        pe.wait_ge(S["ov"], UNITS + u - 1)
                    out = ps[:, u % 2, 0:P]
                    for kc in range(qc + 1):
                        m = mm(out, v_tok2[:, kc, 2 * kind + h // 4, :], pt_buf[:, k % 2, kc * P:(kc + 1) * P],
                               kind == 0 and kc == 0, False)
                    if kind == 1:
                        m = mm(out, vct[0:15, h // 4, :], pct[0:15, u, :], False, True)
                    m.then_inc(S["pv"], 1)
            for x in range(2):
                pe.wait_ge(S["ysq"], x + 1)
                src = i_buf if x == 0 else r_buf
                for k in range(8):
                    m = mm(ps[:, 2, x * T:(x + 1) * T], ones[:, :], src[:, k, :], k == 0, k == 7)
                m.then_inc(S["yss"], 1)
            with pe.Fori(0, 4) as i:
                linear(PAN["out2"] + i * 8, GRP["out2"] + i * 4, opb, ready=("yop", 1, 2))
            norm(4)
            with pe.Fori(0, 4) as i:
                linear(PAN["wq"] + i * 8, GRP["wq"] + i * 4, opa, ready=("op", 26, 28))
            pe.wait_ge(S["freed"], GRP["wq"] + 16)
            for c in range(2):
                for b in range(4):
                    for k in range(4):
                        m = nc.tensor.transpose(ps[:, 4 * c + b, k * P:(k + 1) * P],
                                                tmp[:, 4 * b + k, c * P:(c + 1) * P], ident)
                    m.then_inc(S["hft"], 1)
            for x in range(2):
                p = PAN["keys"] + x
                pe.wait_ge(S["lo"], p + 1)
                for c in range(2):
                    for b in range(8):
                        hp = 8 * x + b
                        bank = 4 * c + hp // 4
                        if hp % 4 == 0:
                            pe.wait_ge(S["hfc"], bank + 1)
                        out = ps[:, bank, (hp % 4) * P:(hp % 4 + 1) * P]
                        hi, lo = opb_hi[:, hp, c * P:(c + 1) * P], opb_lo[:, hp, c * P:(c + 1) * P]
                        mm(out, hi, w_hi[p % 4][:, b, :], True, False)
                        mm(out, hi, w_lo[p % 2][:, b, :], False, False)
                        m = mm(out, lo, w_hi[p % 4][:, b, :], False, True)
                m.then_inc(S["panel"], 1)
            pe.wait_ge(S["scc"], 8)
            for c in range(2):
                pe.wait_ge(S["used"], 256 + 128 * (c + 1) + 1)
                for b in range(4):
                    for k in range(4):
                        m = nc.tensor.transpose(ps[:, 4 * c + b, k * P:(k + 1) * P],
                                                p_acc[c][:, (4 * b + k) * P:(4 * b + k + 1) * P], ident)
                    m.then_inc(S["tout"], 1)

        @block.scalar
        def _(act):
            link = Chain(act, S["chain_a"])

            def split(p, n):
                for q in range(p, p + n):
                    act.wait_ge(land[q % 4], 16 * (q // 4 + 1))
                    if q >= 4:
                        act.wait_ge(S["panel"], q - 3)
                    s = q % 4
                    nc.scalar.activation(w_hi[s][:, :, :].rearrange("p b n -> p (b n)"), raw[s],
                                         ACT.Copy).then_inc(S["hi"], 1)

            def split_loop(base, i, n, per):
                for j in range(n):
                    act.wait_ge(land[j % 4], (base // 4 + j // 4 + 1) * 16 + i * (per * 4))
                    act.wait_ge(S["panel"], base + j - 3 + i * per)
                    nc.scalar.activation(w_hi[j % 4][:, :, :].rearrange("p b n -> p (b n)"), raw[j % 4],
                                         ACT.Copy).then_inc(S["hi"], 1)

            def inverse_root(out, x):
                link(nc.scalar.activation(out, x, ACT.Ln))
                return nc.scalar.activation(out, out, ACT.Exp, scale=-0.5)

            def norm(n, ready, shift):
                act.wait_ge(*ready)
                for j in range(4):
                    s = slice(4 * j, 4 * j + 4)
                    nc.scalar.activation(tmp[:, s, :], x_res[:, s, :], ACT.Square).then_inc(S["sq"], 1)
                act.wait_ge(S["mean"], n + 1)
                inverse_root(rstd[:, 1, :], rstd[:, 0, :]).then_inc(S["rs"], 1)
                act.wait_ge(S["gn"], n + 1)
                for j in range(4):
                    act.wait_ge(S["nt"], 4 * n + j + 1)
                    for k in range(4 * j, 4 * j + 4):
                        out = tmp if shift is not None else x_res
                        link(nc.scalar.activation(out[:, k, :], tmp[:, k, :], ACT.Identity,
                                                  bias=shift[:, k:k + 1] if shift is not None else 0.0,
                                                  scale=gain[:, k:k + 1]), wait=False)
                    link.wait()
                    if shift is not None:
                        s = slice(4 * j, 4 * j + 4)
                        nc.scalar.activation(opa_hi[:, s, :], tmp[:, s, :], ACT.Copy).then_inc(S["nh"], 1)

            def attend(units, base, per):
                for n in range(units + 2):
                    if n < units:
                        nk = P * (n // per % 2 + 1)
                        act.wait_ge(S["sm"], base + n + 1)
                        nc.scalar.activation(p_buf[:, n % 4, 0:nk], p_buf[:, n % 4, 0:nk], ACT.Exp,
                                             bias=stat[:, 0, n:n + 1], scale=-1.0,
                                             accum_out=stat[:, 2, n:n + 1]).then_inc(S["ex"], 1)
                    if n >= 2:
                        u = n - 2
                        nk = P * (u // per % 2 + 1)
                        act.wait_ge(S["tp"], base + u + 1)
                        if u >= 2:
                            act.wait_ge(S["pv"], base + u - 1)
                        nc.scalar.activation(pt_buf[:, u % 2, 0:nk], ps[:, 6 + u % 2, 0:nk], ACT.Copy).then_inc(
                            S["ptc"], 1)

            act.wait_ge(S["small"], 32)
            for b, name in enumerate(("c", "c_2")):
                nc.scalar.activation(csil[:, b, :], col(name, 0, DC), ACT.Sigmoid).then_inc(S["sigc"], 1)
            act.wait_ge(S["ang"], 1)
            for k in range(2):
                nc.scalar.activation(par(SI if k == 0 else CO), par(X1 if k == 0 else X2), ACT.Sin).then_inc(
                    S["sin"], 1)
            norm(0, (S["xload"], 16), modcol(0))
            for j in range(2):
                split(8 * j, 8)
            for j in range(8):
                act.wait_ge(S["bt"], j + 1)
                nc.scalar.activation(b_t[:, :, j, :], ps[:, 4 + j % 4, 0:2 * P].rearrange("p (r s) -> p r s", r=2),
                                     ACT.Copy).then_inc(S["btc"], 1)
            for j in range(8):
                act.wait_ge(S["yadd"], j + 1)
                nc.scalar.activation(acts[:, j, :], acts[:, j, :], ACT.Gelu_apprx_tanh).then_inc(S["yg"], 1)
            with act.Fori(0, 6) as i:
                split_loop(PAN["qkv"], i, 8, 8)
            act.wait_ge(S["yg"], 8)
            nc.scalar.activation(opb_hi[:, 8:16, :], acts[:, 0:8, :], ACT.Copy).then_inc(S["ghi"], 1)
            split(PAN["glu"], 8)
            for n in range(8):
                act.wait_ge(S["panel"], PAN["glu"] + n + 1)
                if n >= 2:
                    act.wait_ge(S["gmul"], n - 1)
                nc.scalar.activation(sg[:, n % 2, :], ps[:, n % 4, 0:T], ACT.Sigmoid,
                                     bias=col("b_glu", n)).then_inc(S["freed"], 1)
            for b in range(4):
                act.wait_ge(S["vt"], b + 1)
                nc.scalar.activation(v_tok[:, :, 2 * b:2 * b + 2, :],
                                     ps[:, b, :].rearrange("p (k h d) -> p k h d", k=2, h=2),
                                     ACT.Copy).then_inc(S["vtc"], 1)
            attend(UNITS, 0, 1)
            with act.Fori(0, 8) as i:
                base = PAN["merge"]

                def sigmoids(par_):
                    for g in range(2):
                        act.wait_ge(S["panel"], base + 6 * par_ + 2 * g + 2 + i * 12)
                        if g == 0:
                            act.wait_ge(S["freed"], GRP["merge"] + 2 * i + par_ - 1)
                        nc.scalar.activation(sg[:, 2 * par_ + g, :], ps[:, 4 * par_ + g, 0:T],
                                             ACT.Sigmoid).then_inc(S["msig"], 1)

                for j in range(12):
                    act.wait_ge(land[j % 4], (base // 4 + j // 4 + 1) * 16 + i * 48)
                    act.wait_ge(S["panel"], base + j - 3 + i * 12)
                    nc.scalar.activation(w_hi[j % 4][:, :, :].rearrange("p b n -> p (b n)"), raw[j % 4],
                                         ACT.Copy).then_inc(S["hi"], 1)
                    if j == 7:
                        sigmoids(0)
                sigmoids(1)
            for j in range(4):
                s = slice(4 * j, 4 * j + 4)
                act.wait_ge(S["freed"], GRP["out"])
                nc.scalar.activation(opa_hi[:, s, :], tmp[:, s, :], ACT.Copy).then_inc(S["nh"], 1)
            with act.Fori(0, 4) as i:
                split_loop(PAN["out"], i, 8, 8)
            norm(1, (S["freed"], GRP["ff"]), modcol(3))
            with act.Fori(0, 32) as i:
                split_loop(PAN["ff"], i, 8, 8)
            norm(2, (S["freed"], GRP["in2"]), None)
            norm(3, (S["nt"], 12), modcol(6))
            A = nc.scalar.activation
            with act.Fori(0, 4) as i:
                split_loop(PAN["in2"], i, 8, 8)
            split(PAN["lru"], 4)
            for r, (name, buf) in enumerate((("lru_ba_2", r_buf), ("lru_bi_2", i_buf))):
                act.wait_ge(S["panel"], PAN["lru"] + r + 1)
                for k in range(8):
                    A(buf[:, k, :], ps[:, 4 + k // 2, (k % 2) * T:(k % 2 + 1) * T], ACT.Sigmoid,
                      bias=col(name, k)).then_inc(S["lsig"], 1)
            split(PAN["lru"] + 4, 4)
            act.wait_ge(S["lsig"], 8)
            for k in range(8):
                link(A(r_buf[:, k, :], r_buf[:, k, :], ACT.Tanh, scale=sp4[:, k:k + 1]), wait=False)
            split(PAN["lru"] + 8, 4)
            link.wait()
            A(q_buf, r_buf, ACT.Sqrt).then_inc(S["lsq"], 1)
            split(PAN["lru"] + 12, 4)
            A(acts[:, 28:32, :], acts[:, 28:32, :], ACT.Gelu).then_inc(S["lgel"], 1)
            A(acc16[:, 0:4, :], acc16[:, 0:4, :], ACT.Gelu).then_inc(S["lgel"], 1)
            with act.Fori(0, 4) as i:
                split_loop(PAN["lru"] + 16, i, 8, 8)
            split(PAN["lru"] + 48, PAN["out2"] - PAN["lru"] - 48)
            act.wait_ge(S["freed"], GRP["out2"])
            act.wait_ge(S["rnn"], 1)
            for i in range(7):
                if i < 6:
                    if i >= 2:
                        act.wait_ge(S["zss"], i - 1)
                    k = 2 * (i % 2)
                    A(r_buf[:, k:k + 2, :], acts[:, PAIRS[i]:PAIRS[i] + 2, :], ACT.Square).then_inc(S["zsq"], 1)
                if i >= 1:
                    k = i - 1
                    act.wait_ge(S["zmean"], k + 1)
                    if k >= 2:
                        act.wait_ge(S["zy"], k - 1)
                    inverse_root(rs2[k % 2], mean2[k % 2]).then_inc(S["zrs"], 1)
            A(acc16[:, 4, :], acc16[:, 4, :], ACT.Sigmoid, bias=col("gate_b_2")).then_inc(S["gsig"], 1)
            act.wait_ge(S["kcc"], 1)
            A(kcn2[:, 0:30], kcn[:, 0:30], ACT.Square).then_inc(S["ksq"], 1)
            act.wait_ge(S["kmean"], 1)
            inverse_root(kcr[:, 1, 0:30], kcr[:, 0, 0:30]).then_inc(S["krs"], 1)
            act.wait_ge(S["rnn"], 1)
            for b in range(2):
                act.wait_ge(S["vtt2"], b + 1)
                for v in range(2):
                    ins = A(v_tok2[:, :, 2 * b + v, :], ps[:, 4 + b, 2 * v * P:2 * (v + 1) * P].rearrange(
                        "p (k d) -> p k d", k=2), ACT.Copy)
                ins.then_inc(S["vtc2"], 1)
            act.wait_ge(S["cmx"], 1)
            A(pc[:, :, 0:15], pc[:, :, 0:15], ACT.Exp, scale=SC).then_inc(S["cex"], 1)
            for b in range(4):
                act.wait_ge(S["cpt"], b + 1)
                A(pct[0:15, 4 * b:4 * b + 4, :], ps[0:15, b, :].rearrange("p (u q) -> p u q", u=4),
                  ACT.Copy).then_inc(S["ptct"], 1)
            attend(N2, UNITS, 2)
            act.wait_ge(S["ov"], UNITS + 16)
            A(i_buf, acts[:, 0:8, :], ACT.Square).then_inc(S["ysq"], 1)
            A(r_buf, u_buf, ACT.Square).then_inc(S["ysq"], 1)
            act.wait_ge(S["ymean"], 1)
            inverse_root(rs2[0], mean2[0]).then_inc(S["yrs"], 1)
            for x in range(2):
                act.wait_ge(S["yy"], x + 1)
                A(opb_hi[:, 8 * x:8 * x + 8, :], acts[:, 0:8, :] if x == 0 else u_buf, ACT.Copy).then_inc(S["yhi"], 1)
            with act.Fori(0, 4) as i:
                split_loop(PAN["out2"], i, 8, 8)
            norm(4, (S["freed"], GRP["wq"]), modcol(9))
            with act.Fori(0, 4) as i:
                split_loop(PAN["wq"], i, 8, 8)
            split(PAN["keys"], 2)
            for b in range(8):
                act.wait_ge(S["hft"], b + 1)
                c = b // 4
                A(hf[c][:, (b % 4) * 512:(b % 4 + 1) * 512], ps[:, b, :], ACT.Copy).then_inc(S["hfc"], 1)
            act.wait_ge(S["panel"], PANELS)
            for b in range(8):
                A(score[:, 4 * b:4 * b + 4, :], ps[:, b, :].rearrange("p (u k) -> p u k", u=4),
                  ACT.Copy).then_inc(S["scc"], 1)
            act.wait_ge(S["g1"], 1)
            A(gsm_t, gsm_t, ACT.Exp).then_inc(S["gg"], 1)
            for c in range(2):
                act.wait_ge(S["dcp"], PICKS * (c + 1))
                A(dots_t[:, c * P:(c + 1) * P], dots_t[:, c * P:(c + 1) * P], ACT.Gelu).then_inc(S["gg"], 1)

        @block.gpsimd
        def _(pool):
            link = Chain(pool, S["chain_p"])

            def rest(p, j, first=False):
                pool.wait_ge(S["hi"], p + 1)
                if not first:
                    pool.wait_ge(S["panel"], p - 1)
                nc.gpsimd.tensor_tensor(w_lo[j % 2][:, :, :].rearrange("p b n -> p (b n)"), raw[j % 4],
                                        w_hi[j % 4][:, :, :].rearrange("p b n -> p (b n)").bitcast(F32),
                                        ALU.subtract).then_inc(S["lo"], 1)

            def rests(p, n):
                for j in range(n):
                    rest(p + j, j)

            nc.gpsimd.memset(ones[:, :], 1.0).then_inc(S["init"], 1)
            pool.wait_ge(S["par"], 1)
            TT = nc.gpsimd.tensor_tensor
            x = [par(i) for i in (X1, X2, X3, X4, X5)]
            link(nc.gpsimd.tensor_copy(par(PCO), par(CO)), wait=False)
            link(nc.gpsimd.tensor_copy(par(PSI), par(SI)))
            for k in range(7):
                c, s = par(PCO + k), par(PSI + k)
                link(TT(x[0], c, c, ALU.mult), wait=False)
                link(TT(x[1], s, s, ALU.mult), wait=False)
                link(TT(x[2], c, s, ALU.mult))
                link(TT(par(PCO + k + 1), x[0], x[1], ALU.subtract), wait=False)
                link(TT(par(PSI + k + 1), x[2], x[2], ALU.add))
            t2 = ssm_t2[:, :, :].rearrange("p a t -> p (a t)")
            for f in range(2):
                co, si = e_tab[:, 2 * f], e_tab[:, 2 * f + 1]
                link(nc.gpsimd.memset(co[:, :, 0:1], 1.0), wait=False)
                link(nc.gpsimd.memset(si[:, :, 0:1], 0.0))
                for k in range(4):
                    m = 1 << k
                    pc = par(PCO + 4 * f + k).unsqueeze(2).broadcast_to([P, 32, m])
                    ps_ = par(PSI + 4 * f + k).unsqueeze(2).broadcast_to([P, 32, m])
                    c0, s0, c1, s1 = co[:, :, 0:m], si[:, :, 0:m], co[:, :, m:2 * m], si[:, :, m:2 * m]
                    t = t2[:, 0:32 * m].rearrange("p (g m) -> p g m", g=32)
                    tt = t2[:, 256:256 + 32 * m].rearrange("p (g m) -> p g m", g=32)
                    link(TT(t, s0, ps_, ALU.mult), wait=False)
                    link(TT(c1, c0, pc, ALU.mult), wait=False)
                    link(TT(tt, s0, pc, ALU.mult), wait=False)
                    link(TT(s1, c0, ps_, ALU.mult))
                    link(TT(c1, c1, t, ALU.subtract), wait=False)
                    link(TT(s1, s1, tt, ALU.add))
            pool.wait_ge(S["bload"], 16)
            fr = par(FR).unsqueeze(2).broadcast_to([P, 32, 32])
            fi = par(FI).unsqueeze(2).broadcast_to([P, 32, 32])
            link(TT(b_tmp[:, 0], b_x[:, 1], fi, ALU.mult), wait=False)
            link(TT(b_tmp[:, 1], b_x[:, 0], fi, ALU.mult), wait=False)
            link(TT(b_f[:, 0], b_x[:, 0], fr, ALU.mult), wait=False)
            link(TT(b_f[:, 1], b_x[:, 1], fr, ALU.mult))
            link(TT(b_f[:, 0], b_f[:, 0], b_tmp[:, 0], ALU.subtract))
            link(TT(b_f[:, 1], b_f[:, 1], b_tmp[:, 1], ALU.add), wait=False)
            link.wait()
            nc.gpsimd.memset(cs[:, :, :], 0.0).then_inc(S["bf"], 1)
            for p in range(16):
                rest(p, p, first=p < 2)

            def tables(s):
                if s >= 2:
                    pool.wait_ge(S["prod"], s - 1)
                if s >= 1:
                    pool.wait_ge(S["cs"], 2 * s)
                sh = [P, 2, 16, 16]
                g = slice(2 * s, 2 * s + 2)
                c1 = e_tab[:, 0, g, :].unsqueeze(2).broadcast_to(sh)
                s1 = e_tab[:, 1, g, :].unsqueeze(2).broadcast_to(sh)
                c16 = e_tab[:, 2, g, :].unsqueeze(3).broadcast_to(sh)
                s16 = e_tab[:, 3, g, :].unsqueeze(3).broadcast_to(sh)
                co = ssm_cs[:, s % 2, 0].rearrange("p g (a b) -> p g a b", a=16)
                si = ssm_cs[:, s % 2, 1].rearrange("p g (a b) -> p g a b", a=16)
                t = ssm_t2[:, :, :].rearrange("p g (a b) -> p g a b", a=16)
                link(TT(co, c16, c1, ALU.mult), wait=False)
                link(TT(t, s16, s1, ALU.mult))
                TT(co, co, t, ALU.subtract).then_inc(S["cs"], 1)
                link(TT(si, s16, c1, ALU.mult), wait=False)
                pool.wait_ge(S["cs"], 2 * s + 1)
                link(TT(t, c16, s1, ALU.mult))
                TT(si, si, t, ALU.add).then_inc(S["cs"], 1)

            pool.wait_ge(S["bt"], 8)
            for s in range(16):
                tables(s)
            with pool.Fori(0, 6) as i:
                rests(PAN["qkv"] + i * 8, 8)
            rests(PAN["glu"], 8)
            with pool.Fori(0, 8) as i:
                rests(PAN["merge"] + i * 12, 12)
            with pool.Fori(0, 4) as i:
                rests(PAN["out"] + i * 8, 8)
            with pool.Fori(0, 32) as i:
                rests(PAN["ff"] + i * 8, 8)
            with pool.Fori(0, 10) as i:
                rests(PAN["in2"] + i * 8, 8)
            rests(PAN["in2"] + 80, 4)
            with pool.Fori(0, 4) as i:
                rests(PAN["out2"] + i * 8, 8)
            with pool.Fori(0, 4) as i:
                rests(PAN["wq"] + i * 8, 8)
            rests(PAN["keys"], 2)
            nc.gpsimd.memset(zero1[:, :], 0).then_inc(S["init"], 1)
            pool.wait_ge(S["init"], 3)
            pool.wait_ge(S["eix"], 1)
            pool.wait_ge(S["lo"], PANELS)
            IT = nc.gpsimd.tensor_tensor

            def gather(j, table):
                pool.indirect_dma_start(gslot[j], None, table, bass.IndirectOffsetOnAxis(
                    ap=st_b[j][:, 0:1], axis=0)).then_inc(S[f"gat{j}"], 16)

            for half_, table in enumerate((a["down"], a["up"])):
                base = 256 * half_

                def stage(j, i, first):
                    n = i * 4 + (base + j)
                    if not (half_ == 0 and first):
                        pool.wait_ge(S[f"gat{j}"], i * 16 + (16 * 64) * half_)
                    IT(st_a[j][:, :], idx_t[:, 4 * i + j:4 * i + j + 1] if first else
                       idx_t[:, bass.ds(i * 4 + j, 1)], zero1[:, :], ALU.add).then_inc(S["stage"], 1)
                    pool.wait_ge(S["stage"], 2 * n + 1 if first else i * 8 + (2 * (base + j) + 1))
                    if not (half_ == 0 and first):
                        pool.wait_ge(S["used"], i * 4 + (base + j - 3))
                    IT(st_b[j][:, :], st_a[j][:, :], zero1[:, :], ALU.add).then_inc(S["stage"], 1)

                for j in range(4):
                    stage(j, 0, True)
                    if j:
                        gather(j - 1, table)
                with pool.Fori(1, 64) as i:
                    for j in range(4):
                        stage(j, i, False)
                        gather((j + 3) % 4, table)
                pool.wait_ge(S["stage"], 2 * (base + 256))
                pool.wait_ge(S["used"], base + 253)
                gather(3, table)

        @block.vector
        def _(dve):
            link = Chain(dve, S["chain_v"])
            V = nc.vector
            TT, TS, STT = V.tensor_tensor, V.tensor_scalar, V.scalar_tensor_tensor

            def ada_step(g, k, first=False):
                blk = g // 3
                for h in range(HALVES):
                    q = 64 * g + k * HALVES + h
                    dve.wait_ge(aland[h], (16 * g + 1) * 16 + k * 16)
                    c = csil[:, blk, k:k + 1] if isinstance(k, int) else csil[:, blk, bass.ds(k, 1)]
                    if first:
                        ins = TS(a_acc[:, h, :], a_raw[h], c, None, ALU.mult)
                    else:
                        dve.wait_ge(S["ada"], q - 3)
                        ins = STT(a_acc[:, h, :], a_raw[h], c, a_acc[:, h, :], ALU.mult, ALU.add)
                    ins.then_inc(S["ada"], 1)

            def ada_cols(g):
                dve.wait_ge(S["adaps"], g + 1)
                b0 = COL["b_ada"][0] if g < 3 else COL["ada_b_2"][0]
                TT(mod[:, 32 * g:32 * g + 32], ps[:, 7, 0:32], cols[:, b0 + 32 * (g % 3):b0 + 32 * (g % 3) + 32],
                   ALU.add).then_inc(S["adacol"], 1)
                if g == 1:
                    link(V.memset(a_acc[:, :, :], 0.0))

            def norm_rows(n, beside=None):
                dve.wait_ge(S["ss"], n + 1)
                TS(rstd[:, 0, :], ps[:, 6, 0:T], 1.0 / D, EPS, ALU.mult, ALU.add).then_inc(S["mean"], 1)
                dve.wait_ge(S["rs"], n + 1)
                refine(rstd[:, 1, :], rstd[:, 0, :])
                for j in range(4):
                    if beside:
                        beside(j)
                    s = slice(4 * j, 4 * j + 4)
                    TT(tmp[:, s, :], x_res[:, s, :], rstd[:, 1, :].unsqueeze(1).broadcast_to([P, 4, T]),
                       ALU.mult).then_inc(S["nt"], 1)

            def norm_gain(g_name, scale):
                if scale is None:
                    V.tensor_copy(gain[:, :], col(g_name, 0, DC)).then_inc(S["gn"], 1)
                else:
                    STT(gain[:, :], scale, 1.0, col(g_name, 0, DC), ALU.add, ALU.mult).then_inc(S["gn"], 1)

            def norm(n, g_name, scale, final=False):
                dve.wait_ge(S["ss"], n + 1)
                norm_gain(g_name, scale)
                norm_rows(n)
                if not final:
                    operand_lo(tmp)

            def refine(r, mean):
                link(TT(mean, mean, r, ALU.mult))
                link(TT(mean, mean, r, ALU.mult))
                link(TS(mean, mean, -0.5, 1.5, ALU.mult, ALU.add))
                link(TT(r, r, mean, ALU.mult))

            ops = [0]

            def operand_lo(src):
                for j in range(4):
                    s = slice(4 * j, 4 * j + 4)
                    dve.wait_ge(S["nh"], ops[0] + 1)
                    TT(opa_lo[:, s, :], src[:, s, :], opa_hi[:, s, :].bitcast(F32), ALU.subtract).then_inc(S["op"], 1)
                    ops[0] += 1

            for b, name in enumerate(("c", "c_2")):
                dve.wait_ge(S["sigc"], b + 1)
                link(TT(csil[:, b, :], csil[:, b, :], col(name, 0, DC), ALU.mult))

            def exp(out, x, n=32):
                y, k, r, e = (par(i)[:, 0:n] for i in (X2, X3, X4, X5))
                link(TS(y, x, -87.0, 88.0, ALU.max, ALU.min))
                link(TS(k, y, 1.4426950408889634, 12582912.0, ALU.mult, ALU.add))
                link(TS(k, k, 12582912.0, None, ALU.subtract))
                link(STT(r, k, -LN2[0], y, ALU.mult, ALU.add))
                link(STT(r, k, -LN2[1], r, ALU.mult, ALU.add))
                link(TS(e, r, 1.0 / 5040, None, ALU.mult))
                for d in (720, 120, 24, 6, 2, 1):
                    link(STT(e, e, 1.0 / d, r, ALU.add, ALU.mult))
                link(TS(e, e, 1.0, None, ALU.add))
                link(TS(y.bitcast(I32), k, 127.0, 8388608.0, ALU.add, ALU.mult))
                link(TT(e, e, y, ALU.mult))
                link(STT(out, x, -87.0, e, ALU.is_gt, ALU.mult))

            exp(par(DT), col("ssm_log_dt", 0, 32))
            link(TT(par(X1), par(DT), col("ssm_a_re", 0, 32), ALU.mult))
            exp(par(MAG), par(X1))
            th, k, r = par(X3), par(X4), par(X1)
            link(TT(th, par(DT), col("ssm_a_im", 0, 32), ALU.mult))
            link(TS(k, th, 0.15915494309189535, 12582912.0, ALU.mult, ALU.add))
            link(TS(k, k, 12582912.0, None, ALU.subtract))
            link(STT(r, k, -TWO_PI[0], th, ALU.mult, ALU.add))
            link(STT(r, k, -TWO_PI[1], r, ALU.mult, ALU.add))
            link(STT(r, k, -TWO_PI[2], r, ALU.mult, ALU.add))
            link(TS(r, r, -3.1415925, 3.1415925, ALU.max, ALU.min))
            link(TS(par(X2), r, 1.5707963267948966, None, ALU.add))
            link(TS(k, par(X2), 3.1415926, -6.283185307179586, ALU.is_gt, ALU.mult))
            TT(par(X2), par(X2), k, ALU.add).then_inc(S["ang"], 1)
            dve.wait_ge(S["sin"], 2)
            pr, ai, den, u, v = par(X1), par(X2), par(X3), par(X4), par(X5)
            are, aim = col("ssm_a_re", 0, 32), col("ssm_a_im", 0, 32)
            link(TT(pr, par(MAG), par(CO), ALU.mult))
            link(TS(pr, pr, 1.0, None, ALU.subtract))
            link(TT(ai, par(MAG), par(SI), ALU.mult))
            link(TT(den, are, are, ALU.mult))
            link(TT(u, aim, aim, ALU.mult))
            link(TT(den, den, u, ALU.add))
            link(V.reciprocal(den, den))
            link(TT(u, pr, are, ALU.mult))
            link(TT(v, ai, aim, ALU.mult))
            link(TT(u, u, v, ALU.add))
            link(TT(par(FR), u, den, ALU.mult))
            link(TT(u, ai, are, ALU.mult))
            link(TT(v, pr, aim, ALU.mult))
            link(TT(u, u, v, ALU.subtract))
            link(TT(par(FI), u, den, ALU.mult))

            lam = par(6)[:, 0:8]
            nl, e8, z8, s8, q8 = (par(7 + i)[:, 0:8] for i in range(5))
            link(TS(nl, col("lru_lam_2", 0, 8), -1.0, None, ALU.mult))
            link(TT(nl, nl, col("lru_lam_2", 0, 8), ALU.min))
            exp(e8, nl, 8)
            link(TS(z8, e8, 2.0, None, ALU.add))
            link(V.reciprocal(z8, z8))
            link(TT(z8, z8, e8, ALU.mult))
            link(TT(q8, z8, z8, ALU.mult))
            link(TS(s8, q8, 1.0 / 19, None, ALU.mult))
            for d in (17, 15, 13, 11, 9, 7, 5, 3):
                link(STT(s8, s8, 1.0 / d, q8, ALU.add, ALU.mult))
            link(TS(s8, s8, 1.0, 8.0, ALU.add, ALU.mult))
            link(TT(s8, s8, z8, ALU.mult))
            link(TS(nl, col("lru_lam_2", 0, 8), -1.0, 0.0, ALU.mult, ALU.max))
            link(STT(sp4[:, :], nl, 4.0, s8, ALU.mult, ALU.add))
            V.memset(stat[:, :, :], 0.0).then_inc(S["par"], 1)
            ada_step(0, 0, first=True)
            ada_step(0, 1)
            norm_rows(0, beside=lambda j: ada_step(0, 2 + j))
            with dve.Fori(6, 16) as k:
                ada_step(0, k)
            ada_cols(0)
            dve.wait_ge(S["adacol"], 1)
            norm_gain("norm_mix_g", modcol(1))
            operand_lo(tmp)

            def take(p0, dst, n, beside):
                for j in range(4):
                    dve.wait_ge(S["panel"], p0 + 2 * j + 2)
                    TS(dst(n + j), ps[:, j:j + 1, 0:T], 1.0, None, ALU.mult).then_inc(S["freed"], 1)
                    if j % 2:
                        beside(j // 2)

            for t in range(2):
                take(8 * t, lambda n: acts[:, n:n + 1, :], 4 * t,
                     lambda kk: ada_step(1, 2 * t + kk, first=(t == 0 and kk == 0)))

            def y_add(j):
                dve.wait_ge(S["ymm"], 2 * j + 2)
                STT(acts[:, j, :], acts[:, j, :], col("ssm_d", j), ps[:, j % 2, 0:T], ALU.mult, ALU.add).then_inc(
                    S["yadd"], 1)

            for s in range(16):
                co, si = ssm_cs[:, s % 2, 0], ssm_cs[:, s % 2, 1]
                w1, w2, t1, r1 = (ssm_w[:, s % 2, n] for n in range(4))
                i = 2 * (s % 2)
                v_re, v_im = ps[:, 4 + i:6 + i, 0:T], ps[:, 4 + i:6 + i, T:2 * T]
                dve.wait_ge(S["vmm"], s + 1)
                dve.wait_ge(S["cs"], 2 * s + 2)
                if s == 0:
                    dve.wait_ge(S["bt"], 8)
                if s >= 2:
                    dve.wait_ge(S["ymm"], s - 1)
                link(TT(w1, v_re, co, ALU.mult), wait=False)
                link(TT(t1, v_im, si, ALU.mult), wait=False)
                link(TT(w2, v_im, co, ALU.mult))
                link(TT(w1, w1, t1, ALU.add))
                TT(t1, v_re, si, ALU.mult).then_inc(S["wdone"], 1)
                dve.wait_ge(S["wdone"], s + 1)
                link(TT(w2, w2, t1, ALU.subtract))
                for g in range(2):
                    m = par(MAG)[:, 2 * s + g:2 * s + g + 1].broadcast_to([P, T])
                    link(V.tensor_tensor_scan(r1[:, g, :], m, w1[:, g, :], 0.0, ALU.mult, ALU.add), wait=False)
                    link(V.tensor_tensor_scan(ssm_r2[:, g, :], m, w2[:, g, :], 0.0, ALU.mult, ALU.add))
                link(TT(w1, co, r1, ALU.mult), wait=False)
                link(STT(w2, si, -1.0, ssm_r2[:, :, :], ALU.mult, ALU.mult), wait=False)
                link(STT(t1, co, -1.0, ssm_r2[:, :, :], ALU.mult, ALU.mult))
                STT(r1, si, -1.0, r1, ALU.mult, ALU.mult).then_inc(S["prod"], 1)
                if s % 2 == 1 and s >= 3:
                    y_add(s // 2 - 1)
            y_add(7)
            with dve.Fori(0, 6) as i:
                take(PAN["qkv"] + i * 8, lambda n: acts[:, bass.ds(n, 1), :], i * 4 + 8,
                     lambda kk: ada_step(1, 2 * i + (4 + kk)))
            dve.wait_ge(S["ghi"], 1)
            TT(opb_lo[:, 8:16, :], acts[:, 0:8, :], opb_hi[:, 8:16, :].bitcast(F32), ALU.subtract).then_inc(
                S["glo"], 1)
            for n in range(8):
                dve.wait_ge(S["freed"], GRP["glu"] + n + 1)
                if n >= 1:
                    dve.wait_ge(S["op"], 4 + n)
                y = mix[:, n % 2, :]
                TT(y, acts[:, n, :], sg[:, n % 2, :], ALU.mult).then_inc(S["gmul"], 1)
                dve.wait_ge(S["gmul"], n + 1)
                link(TS(opb_hi[:, n, :], y, 1.0, None, ALU.mult))
                TT(opb_lo[:, n, :], y, opb_hi[:, n, :].bitcast(F32), ALU.subtract).then_inc(S["op"], 1)
            ada_cols(1)

            def attend(units, base, per, mask, gate, take_out):
                for n in range(units + 4):
                    if n < units:
                        nk = P * (n // per % 2 + 1)
                        dve.wait_ge(S["sc"], base + n + 1)
                        if n >= 4:
                            dve.wait_ge(S["tp"], base + n - 3)
                        V.tensor_tensor_reduce(p_buf[:, n % 4, 0:nk], ps[:, score_bank[n % 4], 0:nk],
                                               mask(n)[:, T - nk:T], -SC, 3e38, ALU.add, ALU.min,
                                               stat[:, 0, n:n + 1]).then_inc(S["sm"], 1)
                    if 2 <= n < units + 2:
                        u = n - 2
                        nk = P * (u // per % 2 + 1)
                        dve.wait_ge(S["ex"], base + u + 1)
                        link(V.reciprocal(stat[:, 3, u:u + 1], stat[:, 2, u:u + 1]))
                        TS(p_buf[:, u % 4, 0:nk], p_buf[:, u % 4, 0:nk], stat[:, 3, u:u + 1], gate(u),
                           ALU.mult, *([ALU.mult] if gate(u) is not None else [])).then_inc(S["pn"], 1)
                    if n >= 4:
                        take_out(n - 4)

            dve.wait_ge(S["op"], 12)
            V.memset(mix[32:33, 1, 0:8], NEG).then_inc(S["init"], 1)
            dve.wait_ge(S["line_ps"], 1)
            TS(line, ps[0:8, 6, 0:384], 1.0 / SC, None, ALU.mult).then_inc(S["line"], 1)
            dve.wait_ge(S["bias"], 16 * 8)

            def to_operand(u):
                h, qs = u // 2, slice(P * (u % 2), P * (u % 2) + P)
                dve.wait_ge(S["pv"], u + 1)
                link(TS(opb_hi[:, 8 + h, qs], ps[:, u % 2, 0:P], 1.0, None, ALU.mult))
                TT(opb_lo[:, 8 + h, qs], ps[:, u % 2, 0:P], opb_hi[:, 8 + h, qs].bitcast(F32),
                   ALU.subtract).then_inc(S["ov"], 1)

            attend(UNITS, 0, 1, lambda n: bias[n // 2], lambda n: None, to_operand)
            with dve.Fori(0, 8) as i:
                for par_ in range(2):
                    base = PAN["merge"] + 6 * par_
                    for g in range(2):
                        dve.wait_ge(S["panel"], base + 5 + g + i * 12)
                        dve.wait_ge(S["msig"], 4 * i + 2 * par_ + g + 1)
                        TT(mix[:, g, :], sg[:, 2 * par_ + g, :], ps[:, 4 * par_ + 2 + g, 0:T], ALU.mult).then_inc(
                            S["mterm"], 1)
                    dve.wait_ge(S["mterm"], 4 * i + 2 * par_ + 2)
                    n = 16 + 2 * i + par_
                    TT(acts[:, bass.ds(n, 1), :], mix[:, 0:1, :], mix[:, 1:2, :], ALU.add).then_inc(S["freed"], 1)
                    ada_step(2, 2 * i + par_)
            ops[0] = 4
            operand_lo(tmp)

            def add_gated(p0, n0, gate, beside=None):
                for j in range(4):
                    dve.wait_ge(S["panel"], p0 + 2 * j + 2)
                    xs = x_res[:, bass.ds(n0 + j, 1), :]
                    STT(xs, ps[:, j, 0:T].unsqueeze(1), mod[:, bass.ds(gate * DC + n0 + j, 1)], xs, ALU.mult,
                        ALU.add).then_inc(S["freed"], 1)
                    if j % 2 and beside:
                        beside(j // 2)

            def part(n, turn):
                g, k0, per = MOD_PARTS[n]

                def beside(i, half):
                    if per == 2:
                        ada_step(g, 2 * i + (k0 + half))
                    elif half == 0:
                        ada_step(g, i + k0)

                start = 0
                if k0 == 0:
                    turn(0, None)
                    ada_cols(g - 1)
                    ada_step(g, 0, first=True)
                    start = 1
                with dve.Fori(start, 4) as i:
                    turn(i, lambda half: beside(i, half))

            part(0, lambda i, beside: add_gated(PAN["out"] + i * 8, i * 4, 2, beside))
            norm(1, "norm_mlp_g", modcol(4))
            relu, sq = mix[:, 0, :], mix[:, 1, :]

            def hidden(q, i, beside):
                for j in range(4):
                    n = i * 4 + j
                    dve.wait_ge(S["panel"], PAN["ff"] + 64 * q + 2 * j + 2 + i * 8)
                    TS(relu, ps[:, j, 0:T], 0.0, None, ALU.max).then_inc(S["freed"], 1)
                    dve.wait_ge(S["freed"], GRP["ff"] + 32 * q + j + 1 + i * 4)
                    TT(sq, relu, relu, ALU.mult).then_inc(S["ffc"], 1)
                    dve.wait_ge(S["ffc"], 2 * (16 * q + j) + 1 + i * 8)
                    dst = opb_hi[:, bass.ds(n, 1), :]
                    TS(dst, sq.unsqueeze(1), 1.0, None, ALU.mult).then_inc(S["ffc"], 1)
                    dve.wait_ge(S["ffc"], 2 * (16 * q + j) + 2 + i * 8)
                    TT(opb_lo[:, bass.ds(n, 1), :], sq.unsqueeze(1), dst.bitcast(F32), ALU.subtract).then_inc(
                        S["hid"], 1)
                    if j % 2 and beside:
                        beside(j // 2)

            for q in range(4):
                part(1 + 2 * q, lambda i, beside: hidden(q, i, beside))
                part(2 + 2 * q, lambda i, beside: add_gated(PAN["ff"] + 64 * q + 32 + i * 8, i * 4, 5, beside))
            norm(2, "norm_final_g", None, final=True)
            ada_cols(5)
            norm(3, "norm_mix_g_2", modcol(7))

            def take_turn(t):
                p0 = PAN["in2"] + 8 * t + (2 if t >= 4 else 0) + (8 if t >= 7 else 0)
                place = IN2_PLACES[t] if t < 9 else None
                for j in range(4 if t < 9 else 1):
                    dve.wait_ge(S["panel"], p0 + 2 * j + 2)
                    if place is None:
                        dst = acc16[:, j + (4 if t == 9 else 0), :]
                    else:
                        dst = acts[:, place[j] if isinstance(place, tuple) else place + j, :]
                    TS(dst, ps[:, j, 0:T], 1.0, None, ALU.mult).then_inc(S["freed"], 1)
                dve.wait_ge(S["freed"], GRP["in2"] + min(4 * t + 4, 37))

            def conv(half):
                ks = range(4 * half, 4 * half + 4)
                for k in ks:
                    link(TS(u_buf[:, k, :], acts[:, 20 + k, :], col("conv_w_2", 24 + k), col("conv_b_2", k), ALU.mult,
                            ALU.add), wait=False)
                for d in range(1, 4):
                    link.wait()
                    for k in ks:
                        link(STT(u_buf[:, k, d:T], acts[:, 20 + k, 0:T - d], col("conv_w_2", 8 * (3 - d) + k),
                                 u_buf[:, k, d:T], ALU.mult, ALU.add), wait=False)
                link.wait()
                s_, d_ = slice(4 * half, 4 * half + 4), slice(8 + 4 * half, 12 + 4 * half)
                link(TS(opb_hi[:, d_, :], u_buf[:, s_, :], 1.0, None, ALU.mult))
                ins = TT(opb_lo[:, d_, :], u_buf[:, s_, :], opb_hi[:, d_, :].bitcast(F32), ALU.subtract)
                if half:
                    link.wait()
                    ins.then_inc(S["uop"], 1)
                else:
                    link(ins)

            cosb, sinb = (cst(x).unsqueeze(1).broadcast_to([P, 2, T]) for x in ("rope_cos", "rope_sin"))

            def rotate(c, bank, n, t):
                z = acts[:, c:c + 2, :]
                dve.wait_ge(S["zsw"], n + 1)
                link(TT(t, ps[:, bank, :].rearrange("p (a t) -> p a t", a=2), sinb, ALU.mult), wait=False)
                link(TT(z, z, cosb, ALU.mult))
                TT(z, z, t, ALU.add).then_inc(S["zrot"], 1)

            for t in range(2):
                take_turn(t)
                conv(t)
            for t in range(2, 6):
                take_turn(t)
            rotate(8, 4, 0, mix[:, :, :])
            dve.wait_ge(S["zrot"], 1)
            for x, (c0, pe_name) in enumerate(((8, "cmp_pe_k_2"), (14, "cmp_pe_v_2"))):
                for g in range(2):
                    at = acts[:, c0 + g, :]
                    src = bass.AP(at.tensor, at.offset, [at.ap[0], [1, 32], [16, 15]])
                    dst = blk[x].rearrange("p (l m) -> p l m", m=30)[:, :, 15 * g:15 * g + 15]
                    link(TT(dst, src, col(pe_name, 0, 32).unsqueeze(2).broadcast_to([P, 32, 15]), ALU.add),
                         wait=False)
            link.wait()
            for x in range(2):
                link(TS(blk_hi[x], blk[x], 1.0, None, ALU.mult))
                ins = TT(blk_lo[x], blk[x], blk_hi[x].bitcast(F32), ALU.subtract)
                if x == 0:
                    link(ins)
                else:
                    ins.then_inc(S["blkd"], 1)
            dve.wait_ge(S["blkd"], 1)
            dve.wait_ge(S["lsq"], 1)
            dve.wait_ge(S["lsig"], 16)
            link(TS(r_buf, r_buf, 1.0, None, ALU.add))
            link(TT(i_buf, i_buf, u_buf, ALU.mult))
            take_turn(6)
            link(V.reciprocal(r_buf, r_buf))
            link(TT(q_buf, q_buf, r_buf, ALU.mult))
            link(STT(q_buf, q_buf, 2.0, i_buf, ALU.mult, ALU.mult), wait=False)
            link(TS(r_buf, r_buf, 2.0, -1.0, ALU.mult, ALU.add))
            for k in range(8):
                link(V.tensor_tensor_scan(u_buf[:, k, :], r_buf[:, k, :], q_buf[:, k, :], 0.0, ALU.mult, ALU.add),
                     wait=False)
            link.wait()
            dve.wait_ge(S["lgel"], 2)
            link(TT(u_buf[:, 0:4, :], u_buf[:, 0:4, :], acts[:, 28:32, :], ALU.mult))
            TT(u_buf[:, 4:8, :], u_buf[:, 4:8, :], acc16[:, 0:4, :], ALU.mult).then_inc(S["rnn"], 1)
            take_turn(7)
            dve.wait_ge(S["panel"], PAN["cmp"] + 4)
            TS(kcn[:, 0:30], ps[:, 6, 0:30], 1.0, None, ALU.mult).then_inc(S["kcc"], 1)
            dve.wait_ge(S["panel"], PAN["cmp"] + 8)
            TS(vcx[:, 0:30], ps[:, 7, 0:30], 1.0, None, ALU.mult).then_inc(S["vcc"], 1)
            take_turn(8)
            take_turn(9)
            for i in range(8):
                if i < 6:
                    dve.wait_ge(S["zss"], i + 1)
                    TS(flat(mean2[i % 2]), ps[:, 4 + i % 2, :], 1.0 / P, EPS, ALU.mult, ALU.add).then_inc(
                        S["zmean"], 1)
                if 1 <= i <= 6:
                    k = i - 1
                    dve.wait_ge(S["zrs"], k + 1)
                    refine(rs2[k % 2], mean2[k % 2])
                    z = acts[:, PAIRS[k]:PAIRS[k] + 2, :]
                    g = col("q_norm_g_2") if k < 4 else col("k_norm_g_2", k - 3)
                    STT(z, z, g, rs2[k % 2], ALU.mult, ALU.mult).then_inc(S["zy"], 1)
                if i >= 2:
                    k = i - 2
                    rotate(PAIRS[k], 6 + k % 2, k + 1, r_buf[:, 4 + 2 * (k % 2):6 + 2 * (k % 2), :])
            dve.wait_ge(S["kss"], 1)
            TS(kcr[:, 0, 0:30], ps[:, 2, 0:30], 1.0 / P, EPS, ALU.mult, ALU.add).then_inc(S["kmean"], 1)
            dve.wait_ge(S["krs"], 1)
            refine(kcr[:, 1, 0:30], kcr[:, 0, 0:30])
            STT(kcn[:, 0:30], kcn[:, 0:30], col("k_norm_g_2", 0), kcr[:, 1, 0:30], ALU.mult, ALU.mult).then_inc(
                S["kcd"], 1)
            dve.wait_ge(S["vctp"], 1)
            TS(vct[0:15], ps[0:15, 3, 0:2 * P].rearrange("p (g d) -> p g d", g=2), 1.0, None,
               ALU.mult).then_inc(S["vctc"], 1)
            dve.wait_ge(S["gtt"], 1)
            TS(gate_t[:, :, :], ps[:, 6, 0:2 * P].rearrange("p (c g) -> p c g", c=2)[:, :, 0:24], 1.0, None,
               ALU.mult).then_inc(S["gtc"], 1)
            dve.wait_ge(S["csc"], 1)
            pcx = pc[:, :, 0:15]
            pc4 = pc.rearrange("p (h c) n -> p h c n", c=2)[:, :, :, 0:15]

            def mask4(name):
                m = cst(name).rearrange("p (c n) -> p c n", c=2)[:, :, 0:15]
                return m.unsqueeze(1).broadcast_to([P, 8, 2, 15])

            sc4 = ps[:, 7, 0:256].rearrange("p (h c n) -> p h c n", h=8, c=2)[:, :, :, 0:15]
            link(TT(pc4, sc4, mask4("cmp_add"), ALU.add))
            link(V.tensor_reduce(cs[:, 0, :], pcx, AX.X, ALU.max))
            TT(pcx, pcx, cs[:, 0, :].unsqueeze(2).broadcast_to([P, 16, 15]), ALU.subtract).then_inc(S["cmx"], 1)
            dve.wait_ge(S["cex"], 1)
            link(TT(pc4, pc4, mask4("cmp_mul"), ALU.mult))
            link(V.tensor_reduce(cs[:, 0, :], pcx, AX.X, ALU.add))
            link(TS(cs[:, 1, :], cs[:, 0, :], 0.0, None, ALU.is_equal))
            link(TT(cs[:, 0, :], cs[:, 0, :], cs[:, 1, :], ALU.add))
            link(V.reciprocal(cs[:, 0, :], cs[:, 0, :]))
            dve.wait_ge(S["gtc"], 1)
            g0 = gate_t[:, :, :].rearrange("p c (h k) -> p h c k", k=3)[:, :, :, 0]
            link(TT(cs[:, 2, :].rearrange("p (h c) -> p h c", c=2), cs[:, 0, :].rearrange("p (h c) -> p h c", c=2),
                    g0, ALU.mult))
            TT(pcx, pcx, cs[:, 2, :].unsqueeze(2).broadcast_to([P, 16, 15]), ALU.mult).then_inc(S["cpn"], 1)

            def take_head(n):
                if n % 2:
                    u = n // 2
                    h, qs = u // 2, slice(P * (u % 2), P * (u % 2) + P)
                    dve.wait_ge(S["pv"], UNITS + n + 1)
                    TS(acts[:, h, qs], ps[:, u % 2, 0:P], 1.0, None, ALU.mult).then_inc(S["ov"], 1)

            def unit_gate(n):
                at = 3 * (n // 4) + 1 + n % 2
                return gate_t[:, n // 2 % 2, at:at + 1]

            attend(N2, UNITS, 2, lambda n: cst("causal"), unit_gate, take_head)
            dve.wait_ge(S["yss"], 2)
            TS(flat(mean2[0]), ps[:, 2, :], 1.0 / 1024, EPS, ALU.mult, ALU.add).then_inc(S["ymean"], 1)
            dve.wait_ge(S["yrs"], 1)
            refine(rs2[0], mean2[0])
            outs = (acts[:, 0:8, :], u_buf)
            for x in range(2):
                for k in range(8):
                    ins = STT(outs[x][:, k, :], outs[x][:, k, :], col("out_g_2", 8 * x + k), rs2[0][:, x, :],
                              ALU.mult, ALU.mult)
                    if k < 7:
                        link(ins, wait=False)
                    else:
                        link.wait()
                        ins.then_inc(S["yy"], 1)
            for x in range(2):
                dve.wait_ge(S["yhi"], x + 1)
                TT(opb_lo[:, 8 * x:8 * x + 8, :], outs[x], opb_hi[:, 8 * x:8 * x + 8, :].bitcast(F32),
                   ALU.subtract).then_inc(S["yop"], 1)
            with dve.Fori(0, 4) as i:
                add_gated(PAN["out2"] + i * 8, i * 4, 8)
            norm(4, "norm_ffn_g_2", modcol(10))
            with dve.Fori(0, 4) as i:
                for j in range(4):
                    n = i * 4 + j
                    dve.wait_ge(S["panel"], PAN["wq"] + 2 * j + 2 + i * 8)
                    dst = opb_hi[:, bass.ds(n, 1), :]
                    TS(dst, ps[:, j:j + 1, 0:T], 1.0, None, ALU.mult).then_inc(S["hid"], 1)
                    dve.wait_ge(S["hid"], 64 + j + 1 + i * 4)
                    TT(opb_lo[:, bass.ds(n, 1), :], ps[:, j:j + 1, 0:T], dst.bitcast(F32), ALU.subtract).then_inc(
                        S["freed"], 1)
            dve.wait_ge(S["scc"], 8)

            def best16(units, src, values, indices):
                for r in range(2):
                    s8_ = slice(8 * r, 8 * r + 8)
                    for u in range(units):
                        link(V.max(values[:, u, s8_], src[:, u, :]), wait=False)
                    link.wait()
                    for u in range(units):
                        link(V.max_index(indices[:, u, s8_], values[:, u, s8_], src[:, u, :]), wait=False)
                    link.wait()
                    if r == 0:
                        for u in range(units):
                            link(V.match_replace(src[:, u, :], values[:, u, s8_], src[:, u, :], -3e38), wait=False)
                        link.wait()

            best16(32, score, top_v, top_u)
            link(V.tensor_copy(top_f, top_u), wait=False)
            tv = top_v.rearrange("p (u h) k -> p u h k", h=2)
            sh = [P, 16, 16, 16]
            c4 = cand.rearrange("p u (a b) -> p u a b", a=16)
            link(TT(c4, tv[:, :, 0, :].unsqueeze(3).broadcast_to(sh), tv[:, :, 1, :].unsqueeze(2).broadcast_to(sh),
                    ALU.add))
            best16(16, cand, val, pick.bitcast(U32))
            g3 = gsm_t.rearrange("p (u k) -> p u k", u=16)
            TT(g3, val, val[:, :, 0:1].broadcast_to([P, 16, 16]), ALU.subtract).then_inc(S["g1"], 1)
            key = []
            for x, (op, arg) in enumerate(((ALU.logical_shift_right, 4), (ALU.bitwise_and, 15))):
                link(TS(dec[x].bitcast(I32), pick.bitcast(I32), arg, None, op))
                link(V.tensor_copy(dec[2 + x], dec[x].bitcast(I32)))
                hot = flat(acts[:, 16:32, :]).rearrange("p (u k a) -> p u k a", u=16, k=16)
                iota = cst("iota16").unsqueeze(1).unsqueeze(1).broadcast_to(sh)
                link(TT(hot, dec[2 + x].unsqueeze(3).broadcast_to(sh), iota, ALU.is_equal))
                tf = top_f.rearrange("p (u h) k -> p u h k", h=2)[:, :, x, :]
                link(TT(hot, hot, tf.unsqueeze(2).broadcast_to(sh), ALU.mult))
                link(V.tensor_reduce(dec[4 + x], hot, AX.X, ALU.add))
            link(STT(dec[6], dec[4], 128.0, dec[5], ALU.mult, ALU.add))
            V.tensor_copy(idx_t[:, :], dec[6].rearrange("p u k -> p (u k)")).then_inc(S["eix"], 1)
            dve.wait_ge(S["gg"], 1)
            link(V.tensor_reduce(cs[:, 0, :], g3, AX.X, ALU.add))
            link(V.reciprocal(cs[:, 0, :], cs[:, 0, :]))
            link(TT(g3, g3, cs[:, 0, :].unsqueeze(2).broadcast_to([P, 16, 16]), ALU.mult))
            V.memset(dot4[:, :], 0.0).then_inc(S["used"], 1)
            dve.wait_ge(S["used"], 1)
            for c in range(2):
                with dve.Fori(0, 32) as i:
                    for j in range(4):
                        dve.wait_ge(S[f"gat{j}"], i * 16 + 16 * (32 * c + 1))
                        V.tensor_tensor_reduce(gslot[j], gslot[j], hf[c], 1.0, 0.0, ALU.mult, ALU.add,
                                               dot4[:, j:j + 1]).then_inc(S["used"], 1)
                        dve.wait_ge(S["used"], i * 4 + (128 * c + j + 2))
                        TS(dots_t[:, bass.ds(i * 4 + (128 * c + j), 1)], dot4[:, j:j + 1], 1.0, None,
                           ALU.mult).then_inc(S["dcp"], 1)
                        dve.wait_ge(S["dcp"], i * 4 + (128 * c + j + 1))
            link(V.memset(acts[:, 16:32, :], 0.0))
            for c in range(2):
                cc = slice(c * P, c * P + P)
                dve.wait_ge(S["gg"], 2 + c)
                link(TT(dots_t[:, cc], dots_t[:, cc], gsm_t[:, cc], ALU.mult))
            for c in range(2):
                with dve.Fori(0, 32) as i:
                    for j in range(4):
                        dve.wait_ge(S[f"gat{j}"], i * 16 + 16 * (64 + 32 * c + 1))
                        dve.wait_ge(S["used"], i * 4 + (256 + 128 * c + j + 1))
                        STT(p_acc[c], gslot[j], dots_t[:, bass.ds(i * 4 + (128 * c + j), 1)], p_acc[c], ALU.mult,
                            ALU.add).then_inc(S["used"], 1)
            for c in range(2):
                for b in range(4):
                    dve.wait_ge(S["tout"], 4 * c + b + 1)
                    for k in range(4):
                        xs = x_res[:, 4 * b + k, c * P:(c + 1) * P]
                        ins = STT(xs, ps[:, 4 * c + b, k * P:(k + 1) * P], modcol(11, 1, 4 * b + k), xs, ALU.mult,
                                  ALU.add)
                        if k < 3:
                            link(ins, wait=False)
                        else:
                            link.wait()
                            ins.then_inc(S["xout"], 1)


def panels(w):
    k, n = w.shape
    return w.reshape(k // 1024, 8, P, n // P, P).transpose(3, 0, 2, 1, 4).reshape(-1, P, PW)


def column(v):
    return v.reshape(-1, P).T


def layout(i):
    g = {k: np.asarray(v) for k, v in i.items()}
    w_in = g["w_in"][0]
    parts = [panels(w_in[:, :4096]), panels(g["w_glu"][0])]
    ga, gb = panels(w_in[:, 4096:6144]), panels(w_in[:, 6144:])
    ws, wa = panels(g["w_proj_ssm"][0]), panels(g["w_proj_attn"][0])
    merge = np.concatenate([ga.reshape(16, 2, P, PW), gb.reshape(16, 2, P, PW), ws[:, None], wa[:, None]], 1)
    parts += [merge.reshape(-1, P, PW), panels(g["w_out"][0])]
    f1, f2 = g["w_ff1"][0], g["w_ff2"][0]
    for q in range(4):
        parts += [panels(f1[:, q * D:(q + 1) * D]), panels(f2[q * D:(q + 1) * D])]
    w2 = g["w_in_2"][0]
    q, kc, vc, ks, vs, kw, vw, gl, xr, xg = np.split(
        w2, np.cumsum([1024, 256, 256, 256, 256, 256, 256, 24, 1024]), axis=1)
    gl = np.concatenate([gl, np.zeros((D, P - 24), np.float32)], 1)
    parts.append(panels(np.concatenate([xr, xg], 1)))
    for name in ("lru_wa_2", "lru_wi_2"):
        parts.append(g[name][0].transpose(1, 0, 2).reshape(1, P, PW))
    parts.append(panels(np.concatenate([kc, vc, ks, kw, vs, vw], 1)))
    for name in ("cmp_w_k_2", "cmp_w_v_2"):
        parts.append(panels(g[name][0]))
    parts.append(panels(np.concatenate([q, gl], 1)))
    parts += [panels(g["w_out_2"][0]), panels(g["peer_wq_2"][0])]
    keys = g["peer_keys_2"][0].reshape(2, 8, P, P)
    parts.append(keys.transpose(0, 3, 1, 2).reshape(2, P, PW))
    w = np.concatenate(parts)
    assert w.shape[0] == PANELS
    ada = np.stack([g["w_ada"][0], g["ada_w_2"][0]])
    ada = ada.reshape(2, DC, P, 3, HALVES, PW).transpose(0, 3, 1, 4, 2, 5).reshape(-1, P, PW)
    cols = np.zeros((P, COLS), np.float32)

    def put(name, value):
        at, n = COL[name]
        cols[:value.shape[0], at:at + value.shape[1]] = value

    for name in ("c", "c_2", "b_ada", "ada_b_2", "norm_mix_g", "norm_mlp_g", "norm_final_g", "norm_mix_g_2",
                 "norm_ffn_g_2", "ssm_a_re", "ssm_a_im", "ssm_d", "b_glu", "q_norm_g_2", "k_norm_g_2", "conv_b_2",
                 "lru_ba_2", "lru_bi_2", "lru_lam_2"):
        put(name, column(g[name].reshape(-1)))
    put("ssm_log_dt", column(np.repeat(g["ssm_log_dt"].reshape(-1), 64)))
    put("gate_b_2", g["gate_b_2"].reshape(-1, 1))
    put("conv_w_2", column(g["conv_w_2"].reshape(-1)))
    put("out_g_2", np.concatenate([column(g["out_g_attn_2"].reshape(-1)), column(g["out_g_rnn_2"].reshape(-1))], 1))
    put("cmp_pe_k_2", g["cmp_pe_k_2"][0].T)
    put("cmp_pe_v_2", g["cmp_pe_v_2"][0].T)

    def blocks(v):
        out = np.zeros((2, 64, 32, 2, 16), np.float32)
        v = v.reshape(32, 2, 64, 16)
        for e in range(2):
            out[e, :, :, e, :] = v[:, e].transpose(1, 0, 2)
        return out.reshape(P, 32, 32)

    b_x = np.stack([blocks(g["ssm_b_re"][0]), blocks(g["ssm_b_im"][0])], 1)
    c_x = np.stack([blocks(g["ssm_c_re"][0].transpose(0, 2, 1)), blocks(g["ssm_c_im"][0].transpose(0, 2, 1))], 1)
    return {
        "w": w, "ada": ada, "cols": cols, "consts": constants(),
        "xT": g["x"][0].T.reshape(DC, P, T).transpose(1, 0, 2), "b_x": b_x, "c_x": c_x,
        "relb": g["rel_bias"], "down": g["peer_down_2"][0], "up": g["peer_up_2"][0],
    }


def kernel(**inputs):
    import concourse.bacc as bacc
    from concourse.bass_utils import run_bass_kernel_spmd

    nc = bacc.Bacc("TRN2", target_bir_lowering=False, num_devices=1)
    arrays = {f"in_{k}": np.ascontiguousarray(v) for k, v in layout(inputs).items()}
    a = {k[3:]: nc.dram_tensor(k, v.shape, mybir.dt.from_np(v.dtype), kind="ExternalInput").ap()
         for k, v in arrays.items()}
    a["line"] = nc.dram_tensor("bias_line", (8, P * 3 * P), F32, kind="Internal").ap()
    out = nc.dram_tensor("out", (P, DC, T), F32, kind="ExternalOutput").ap()
    a["out"] = out
    build(nc, a)
    r = run_bass_kernel_spmd(nc, [arrays], core_ids=[0])
    o = r.results[0]["out"]
    return o.transpose(2, 1, 0).reshape(1, T, D)
```
